# Optimizing a Trainium2 kernel written in Bass

```python
import math
import jax, jax.numpy as jnp
from jax import lax
import numpy as np

D_MODEL = 1024
BATCH = 1
SEQ = 512
DEPTH = 2

HEAD_DIM = 64
HGRN_WIDTH = D_MODEL // 4
HGRN_HEADS = HGRN_WIDTH // HEAD_DIM
HGRN_CHUNK = 64
FOURIER_WIDTH = D_MODEL // 4
FOURIER_GROUPS = FOURIER_WIDTH // HEAD_DIM
ATTN_WIDTH = D_MODEL // 2
ATTN_HEADS = ATTN_WIDTH // HEAD_DIM
MIX_WIDTH = HGRN_WIDTH + FOURIER_WIDTH + ATTN_WIDTH
DILATED_PATTERNS = ((128, 1), (512, 4), (2048, 16))
ROPE_THETA = 10000.0
D_FF = 4 * D_MODEL
RMS_EPS = 1e-6
NEG_BIG = -1e30
IN_SPLITS = (HGRN_WIDTH, HGRN_WIDTH, HGRN_WIDTH, HGRN_WIDTH, HGRN_WIDTH, FOURIER_WIDTH, ATTN_WIDTH, ATTN_WIDTH, ATTN_WIDTH)
IN_WIDTH = sum(IN_SPLITS)
SPLIT_POINTS = [sum(IN_SPLITS[:i + 1]) for i in range(len(IN_SPLITS) - 1)]


def rms_norm(x, w):
    xf = x.astype(jnp.float32)
    y = xf * lax.rsqrt(jnp.mean(xf * xf, axis=-1, keepdims=True) + RMS_EPS)
    return (y * w.astype(jnp.float32)).astype(x.dtype)

def hgrn2_chunk_scan(q, k, v, log_f):
    B, H, S, dk = q.shape
    dv = v.shape[-1]
    C = HGRN_CHUNK
    n = S // C

    def chunked(t):
        return jnp.moveaxis(t.reshape(B, H, n, C, t.shape[-1]), 2, 0)

    tri = jnp.tril(jnp.ones((C, C), dtype=bool))[:, :, None]

    def step(state, inp):
        qc, kc, vc, gc = inp
        b = jnp.cumsum(gc, axis=-2)
        inter = jnp.einsum('bhtk,bhkv->bhtv', qc * jnp.exp(b), state)
        diff = b[..., :, None, :] - b[..., None, :, :]
        pair = jnp.where(tri, jnp.exp(jnp.where(tri, diff, 0.0)), 0.0)
        scores = jnp.einsum('bhtk,bhsk,bhtsk->bhts', qc, kc, pair)
        intra = jnp.einsum('bhts,bhsv->bhtv', scores, vc)
        b_last = b[..., -1:, :]
        new_state = (jnp.exp(b_last[..., 0, :])[..., None] * state
                     + jnp.einsum('bhsk,bhsv->bhkv', kc * jnp.exp(b_last - b), vc))
        return new_state, inter + intra

    init = jnp.zeros((B, H, dk, dv), dtype=jnp.float32)
    _, out = lax.scan(step, init, (chunked(q), chunked(k), chunked(v), chunked(log_f)))
    return jnp.moveaxis(out, 0, 2).reshape(B, H, S, dv)

def hgrn2_mixer(q_in, i_in, zf, zb, g_in, lb):
    B, S, W = q_in.shape
    H, dh = HGRN_HEADS, HEAD_DIM
    f32 = jnp.float32
    z = jnp.stack([zf, zb[:, ::-1]], axis=1).astype(f32)
    lbb = lb.astype(f32)[None, :, None, :]
    f = lbb + (1.0 - lbb) * jax.nn.sigmoid(z)
    log_f = jnp.log(f)
    k = 1.0 - f
    q = jax.nn.silu(q_in.astype(f32))
    v = i_in.astype(f32)
    q2 = jnp.stack([q, q[:, ::-1]], axis=1)
    v2 = jnp.stack([v, v[:, ::-1]], axis=1)

    def heads(t):
        return t.reshape(B, 2, S, H, dh).transpose(0, 1, 3, 2, 4).reshape(B, 2 * H, S, dh)

    o = hgrn2_chunk_scan(heads(q2), heads(k), heads(v2), heads(log_f)).reshape(B, 2, H, S, dh)
    o = o[:, 0] + o[:, 1][:, :, ::-1]
    o = o * lax.rsqrt(jnp.mean(o * o, axis=-1, keepdims=True) + RMS_EPS)
    o = o.transpose(0, 2, 1, 3).reshape(B, S, W)
    return o * jax.nn.silu(g_in.astype(f32))

def fourier_mixer(u):
    B, S, W = u.shape
    ug = u.astype(jnp.float32).reshape(B, S, FOURIER_GROUPS, W // FOURIER_GROUPS)
    y = jnp.fft.fft2(ug, axes=(1, 3), norm='ortho').real
    return y.reshape(B, S, W)

def rotary(t, positions):
    hd = t.shape[-1]
    inv_freq = ROPE_THETA ** (-jnp.arange(0, hd, 2, dtype=jnp.float32) / hd)
    ang = positions.astype(jnp.float32)[:, None, :, None] * inv_freq
    cos, sin = jnp.cos(ang), jnp.sin(ang)
    t1, t2 = t[..., :hd // 2], t[..., hd // 2:]
    return jnp.concatenate([t1 * cos - t2 * sin, t2 * cos + t1 * sin], axis=-1)

def dilated_window_attention(q, k, v, window, dilation):
    B, H, S, hd = q.shape
    d = dilation
    R = window // (2 * dilation)
    BLK = R
    L = S // d
    nb = -(-L // BLK)
    Lp = nb * BLK

    def sub(t):
        return t.reshape(B, H, L, d, hd).transpose(0, 1, 3, 2, 4)

    qs = jnp.pad(sub(q), ((0, 0), (0, 0), (0, 0), (0, Lp - L), (0, 0))).reshape(B, H, d, nb, BLK, hd)

    def key_blocks(t):
        tp = jnp.pad(sub(t), ((0, 0), (0, 0), (0, 0), (BLK, Lp - L + BLK), (0, 0))).reshape(B, H, d, nb + 2, BLK, hd)
        return jnp.concatenate([tp[:, :, :, :-2], tp[:, :, :, 1:-1], tp[:, :, :, 2:]], axis=-2)

    k3 = key_blocks(k)
    v3 = key_blocks(v)
    qj = jnp.arange(nb)[:, None, None] * BLK + jnp.arange(BLK)[None, :, None]
    kj = (jnp.arange(nb)[:, None, None] - 1) * BLK + jnp.arange(3 * BLK)[None, None, :]
    valid = (kj >= 0) & (kj < L) & (jnp.abs(qj - kj) <= R)
    s = jnp.einsum('bhrnqc,bhrnkc->bhrnqk', qs, k3)
    s = jnp.where(valid, s, NEG_BIG)
    lse = jax.nn.logsumexp(s, axis=-1)
    p = jnp.exp(s - lse[..., None])
    o = jnp.einsum('bhrnqk,bhrnkc->bhrnqc', p, v3)
    o = o.reshape(B, H, d, Lp, hd)[:, :, :, :L].transpose(0, 1, 3, 2, 4).reshape(B, H, S, hd)
    lse = lse.reshape(B, H, d, Lp)[..., :L].transpose(0, 1, 3, 2).reshape(B, H, S)
    return o, lse

def dilated_attention_mixer(cq, ck, cv, positions):
    B, S, W = cq.shape
    f32 = jnp.float32

    def heads(t):
        return t.astype(f32).reshape(B, S, ATTN_HEADS, HEAD_DIM).transpose(0, 2, 1, 3)

    q = rotary(heads(cq), positions) * (HEAD_DIM ** -0.5)
    k = rotary(heads(ck), positions)
    v = heads(cv)
    outs = []
    lses = []
    for window, dilation in DILATED_PATTERNS:
        o_p, lse_p = dilated_window_attention(q, k, v, window, dilation)
        outs.append(o_p)
        lses.append(lse_p)
    weights = jax.nn.softmax(jnp.stack(lses, axis=0), axis=0)
    o = jnp.sum(weights[..., None] * jnp.stack(outs, axis=0), axis=0)
    return o.transpose(0, 2, 1, 3).reshape(B, S, W)

def first_inputs(seed: int = 0) -> dict:
    key = jax.random.key(seed)
    ks = jax.random.split(key, 10)
    f32 = jnp.float32
    x = jax.random.normal(ks[0], (BATCH, SEQ, D_MODEL), f32)
    positions = jnp.broadcast_to(jnp.arange(SEQ, dtype=jnp.int32)[None, :], (BATCH, SEQ))
    attn_norm_w = 1.0 + 0.02 * jax.random.normal(ks[1], (DEPTH, D_MODEL), f32)
    w_in = jax.random.normal(ks[2], (DEPTH, D_MODEL, IN_WIDTH), f32) * D_MODEL ** -0.5
    hgrn_lower_bounds = 0.5 * jax.random.normal(ks[3], (DEPTH, 2, HGRN_WIDTH), f32)
    w_out = jax.random.normal(ks[4], (DEPTH, MIX_WIDTH, D_MODEL), f32) * MIX_WIDTH ** -0.5
    mlp_norm_w = 1.0 + 0.02 * jax.random.normal(ks[5], (DEPTH, D_MODEL), f32)
    w_up = jax.random.normal(ks[6], (DEPTH, D_MODEL, D_FF), f32) * D_MODEL ** -0.5
    w_down = jax.random.normal(ks[7], (DEPTH, D_FF, D_MODEL), f32) * D_FF ** -0.5
    final_norm_w = 1.0 + 0.02 * jax.random.normal(ks[8], (D_MODEL,), f32)
    return {"x": x, "positions": positions, "attn_norm_w": attn_norm_w, "w_in": w_in,
            "hgrn_lower_bounds": hgrn_lower_bounds, "w_out": w_out, "mlp_norm_w": mlp_norm_w,
            "w_up": w_up, "w_down": w_down, "final_norm_w": final_norm_w}

def first_block(x, positions, attn_norm_w, w_in, hgrn_lower_bounds, w_out, mlp_norm_w, w_up, w_down, final_norm_w):
    p_lb = jax.nn.softmax(hgrn_lower_bounds.astype(jnp.float32), axis=0)
    lb_all = jnp.cumsum(p_lb, axis=0) - p_lb[0:1]
    for layer in range(DEPTH):
        h = rms_norm(x, attn_norm_w[layer])
        proj = h @ w_in[layer]
        a_q, a_i, a_zf, a_zb, a_g, b_u, c_q, c_k, c_v = jnp.split(proj, SPLIT_POINTS, axis=-1)
        o_a = hgrn2_mixer(a_q, a_i, a_zf, a_zb, a_g, lb_all[layer]).astype(x.dtype)
        o_b = fourier_mixer(b_u).astype(x.dtype)
        o_c = dilated_attention_mixer(c_q, c_k, c_v, positions).astype(x.dtype)
        mixed = jnp.concatenate([o_a, o_b, o_c], axis=-1)
        x = x + mixed @ w_out[layer]
        h = rms_norm(x, mlp_norm_w[layer])
        x = x + jnp.square(jax.nn.relu(h @ w_up[layer])) @ w_down[layer]
    return rms_norm(x, final_norm_w)


DEPTH_2 = 1

RW_HEADS = 8
RW_HEAD_DIM = 64
RW_DIM = RW_HEADS * RW_HEAD_DIM
W_LORA = 64
A_LORA = 64
G_LORA = 128
GN_EPS = 64e-5
MLA_HEADS = 8
QK_NOPE = 64
QK_ROPE = 32
V_HEAD = 64
Q_LORA = 384
KV_LORA = 256
Q_BLOCK = 128
N_GROUPS = 4
EXPERTS_PER_GROUP = 8
N_EXPERTS = N_GROUPS * EXPERTS_PER_GROUP
TOP_K = 2
D_EXPERT = 256
EXPERT_BLOCK = 256
NORM_EPS = 1e-6

RW_COLS = 3 * RW_DIM + W_LORA + A_LORA + G_LORA
MLA_COLS = Q_LORA + KV_LORA + QK_ROPE
GATE_COLS = 2 * D_MODEL
IN_COLS = RW_COLS + MLA_COLS + GATE_COLS


def rmsnorm(x, g):
    xf = x.astype(jnp.float32)
    y = xf * lax.rsqrt(jnp.mean(xf * xf, axis=-1, keepdims=True) + NORM_EPS)
    return (y * g.astype(jnp.float32)).astype(x.dtype)

def rope(t, cos, sin):
    t1, t2 = jnp.split(t, 2, axis=-1)
    return jnp.concatenate([t1 * cos - t2 * sin, t2 * cos + t1 * sin], axis=-1)

def rwkv7_mix(z_in, mu, w0, w_up, a0, a_up, g_up, k_k, k_a, r_k, gn_w, gn_b):
    B, S, _ = z_in.shape
    dt = z_in.dtype
    prev = jnp.pad(z_in, ((0, 0), (1, 0), (0, 0)))[:, :-1]
    z = z_in + (prev - z_in) * mu
    r, k, v, wd, ad, gd = jnp.split(
        z, [RW_DIM, 2 * RW_DIM, 3 * RW_DIM, 3 * RW_DIM + W_LORA, 3 * RW_DIM + W_LORA + A_LORA], axis=-1)
    w_log = -jax.nn.softplus(-(w0 + jnp.tanh(wd) @ w_up).astype(jnp.float32)) - 0.5
    decay = jnp.exp(-jnp.exp(w_log))
    a = jax.nn.sigmoid(a0 + ad @ a_up)
    g = jax.nn.sigmoid(gd) @ g_up

    def heads(t):
        return t.reshape(B, S, RW_HEADS, RW_HEAD_DIM).astype(jnp.float32)

    kk = heads(k * k_k)
    kk = kk / jnp.maximum(jnp.sqrt(jnp.sum(kk * kk, axis=-1, keepdims=True)), 1e-12)
    k = k * (1.0 + (a - 1.0) * k_a)
    r_h, k_h, v_h, a_h, w_h = heads(r), heads(k), heads(v), heads(a), heads(decay)

    def step(state, inp):
        r_t, w_t, k_t, v_t, kk_t, a_t = inp
        sa = jnp.einsum('bhvk,bhk->bhv', state, -kk_t)
        state = (state * w_t[:, :, None, :]
                 + sa[..., None] * (kk_t * a_t)[:, :, None, :]
                 + v_t[..., None] * k_t[:, :, None, :])
        return state, jnp.einsum('bhvk,bhk->bhv', state, r_t)

    xs = tuple(jnp.moveaxis(t, 1, 0) for t in (r_h, w_h, k_h, v_h, kk, a_h))
    s0 = jnp.zeros((B, RW_HEADS, RW_HEAD_DIM, RW_HEAD_DIM), jnp.float32)
    _, ys = lax.scan(step, s0, xs)
    y = jnp.moveaxis(ys, 0, 1)
    mean = jnp.mean(y, axis=-1, keepdims=True)
    var = jnp.mean(jnp.square(y - mean), axis=-1, keepdims=True)
    y = ((y - mean) * lax.rsqrt(var + GN_EPS)).reshape(B, S, RW_DIM)
    y = y * gn_w.astype(jnp.float32) + gn_b.astype(jnp.float32)
    bonus = jnp.sum(r_h * k_h * r_k.astype(jnp.float32), axis=-1, keepdims=True) * v_h
    y = y + bonus.reshape(B, S, RW_DIM)
    return (y * g.astype(jnp.float32)).astype(dt)

def mla_mix(q_d, kv_d, kr_raw, cos, sin, g_qa, w_q_up, g_kva, w_kv_up):
    B, S, _ = q_d.shape
    q = (rmsnorm(q_d, g_qa) @ w_q_up).reshape(B, S, MLA_HEADS, QK_NOPE + QK_ROPE)
    q_nope, q_rope = q[..., :QK_NOPE], q[..., QK_NOPE:]
    kv = (rmsnorm(kv_d, g_kva) @ w_kv_up).reshape(B, S, MLA_HEADS, QK_NOPE + V_HEAD)
    k_nope, v = kv[..., :QK_NOPE], kv[..., QK_NOPE:]
    q_rope = rope(q_rope, cos[:, :, None, :], sin[:, :, None, :])
    k_rope = rope(kr_raw, cos, sin)
    scale = 1.0 / math.sqrt(QK_NOPE + QK_ROPE)
    outs = []
    for start in range(0, S, Q_BLOCK):
        end = min(start + Q_BLOCK, S)
        s = (jnp.einsum('bqhd,bkhd->bhqk', q_nope[:, start:end], k_nope[:, :end])
             + jnp.einsum('bqhr,bkr->bhqk', q_rope[:, start:end], k_rope[:, :end]))
        s = s.astype(jnp.float32) * scale
        causal = jnp.arange(end)[None, :] <= jnp.arange(start, end)[:, None]
        p = jax.nn.softmax(jnp.where(causal, s, -jnp.inf), axis=-1).astype(v.dtype)
        outs.append(jnp.einsum('bhqk,bkhd->bqhd', p, v[:, :end]))
    return jnp.concatenate(outs, axis=1).reshape(B, S, MLA_HEADS * V_HEAD)

def hier_moe(h, w_group, b_group, w_router, b_router, w_gu, w_down):
    B, S, D = h.shape
    N = B * S
    hf = h.reshape(N, D)
    p_group = jax.nn.softmax((hf @ w_group).astype(jnp.float32) + b_group.astype(jnp.float32), axis=-1)
    g_sel = jnp.argmax(p_group, axis=-1)
    gate_g = jnp.take_along_axis(p_group, g_sel[:, None], axis=-1)
    fine = ((hf @ w_router).astype(jnp.float32) + b_router.astype(jnp.float32)
            ).reshape(N, N_GROUPS, EXPERTS_PER_GROUP)
    fine_sel = jnp.take_along_axis(fine, g_sel[:, None, None], axis=1)[:, 0]
    top_v, top_i = lax.top_k(fine_sel, TOP_K)
    gate = jax.nn.softmax(top_v, axis=-1) * gate_g
    expert = g_sel[:, None] * EXPERTS_PER_GROUP + top_i

    A = N * TOP_K
    e_flat = expert.reshape(A)
    t_flat = jnp.arange(A) // TOP_K
    w_flat = gate.reshape(A)
    order = jnp.argsort(e_flat)
    e_s, t_s, w_s = e_flat[order], t_flat[order], w_flat[order]
    counts = jnp.bincount(e_flat, length=N_EXPERTS)
    starts = jnp.cumsum(counts) - counts
    padded = (counts + EXPERT_BLOCK - 1) // EXPERT_BLOCK * EXPERT_BLOCK
    pad_end = jnp.cumsum(padded)
    pad_start = pad_end - padded
    dest = pad_start[e_s] + (jnp.arange(A) - starts[e_s])
    n_blocks = -(-A // EXPERT_BLOCK) + N_EXPERTS
    P = n_blocks * EXPERT_BLOCK
    tok_buf = jnp.full((P,), N, jnp.int32).at[dest].set(t_s.astype(jnp.int32))
    w_buf = jnp.zeros((P,), jnp.float32).at[dest].set(w_s)
    blk_expert = jnp.minimum(
        jnp.searchsorted(pad_end, jnp.arange(n_blocks) * EXPERT_BLOCK, side='right'), N_EXPERTS - 1)
    x_pad = jnp.concatenate([hf, jnp.zeros((1, D), hf.dtype)], axis=0)
    xb = x_pad[tok_buf].reshape(n_blocks, EXPERT_BLOCK, D)

    def expert_block(args):
        xblk, e = args
        gt, up = jnp.split(xblk @ w_gu[e], 2, axis=-1)
        return (jax.nn.silu(gt) * up) @ w_down[e]

    yb = lax.map(expert_block, (xb, blk_expert)).reshape(P, D)
    out = jnp.zeros((N + 1, D), h.dtype).at[tok_buf].add(yb * w_buf[:, None].astype(h.dtype))
    return out[:N].reshape(B, S, D)

def second_inputs(seed: int = 0) -> dict:
    key = jax.random.key(seed)
    ks = jax.random.split(key, 32)
    f32 = jnp.float32

    def nrm(k, shape, scale):
        return jax.random.normal(k, shape, f32) * scale

    L, D = DEPTH_2, D_MODEL
    x = jax.random.normal(ks[0], (BATCH, SEQ, D), f32)
    offsets = jax.random.randint(ks[1], (BATCH, 1), 0, 1024, dtype=jnp.int32)
    positions = offsets + jnp.arange(SEQ, dtype=jnp.int32)[None, :]
    return {
        "x": x,
        "positions": positions,
        "mix_norm_g": 1.0 + nrm(ks[2], (L, D), 0.02),
        "w_in": nrm(ks[3], (L, D, IN_COLS), D ** -0.5),
        "rw_mu": jax.random.uniform(ks[4], (L, RW_COLS), f32),
        "rw_w0": jax.random.uniform(ks[5], (L, RW_DIM), f32, -6.0, -1.0),
        "rw_w_up": nrm(ks[6], (L, W_LORA, RW_DIM), 0.1 * W_LORA ** -0.5),
        "rw_a0": nrm(ks[7], (L, RW_DIM), 0.1),
        "rw_a_up": nrm(ks[8], (L, A_LORA, RW_DIM), 0.5 * A_LORA ** -0.5),
        "rw_g_up": nrm(ks[9], (L, G_LORA, RW_DIM), G_LORA ** -0.5),
        "rw_k_k": 0.85 + nrm(ks[10], (L, RW_DIM), 0.02),
        "rw_k_a": 1.0 + nrm(ks[11], (L, RW_DIM), 0.02),
        "rw_r_k": nrm(ks[12], (L, RW_HEADS, RW_HEAD_DIM), 0.1),
        "rw_gn_w": 1.0 + nrm(ks[13], (L, RW_DIM), 0.02),
        "rw_gn_b": nrm(ks[14], (L, RW_DIM), 0.02),
        "mla_g_qa": 1.0 + nrm(ks[15], (L, Q_LORA), 0.02),
        "mla_w_q_up": nrm(ks[16], (L, Q_LORA, MLA_HEADS * (QK_NOPE + QK_ROPE)), Q_LORA ** -0.5),
        "mla_g_kva": 1.0 + nrm(ks[17], (L, KV_LORA), 0.02),
        "mla_w_kv_up": nrm(ks[18], (L, KV_LORA, MLA_HEADS * (QK_NOPE + V_HEAD)), KV_LORA ** -0.5),
        "w_branch_rw": nrm(ks[19], (L, RW_DIM, D), RW_DIM ** -0.5),
        "w_branch_mla": nrm(ks[20], (L, MLA_HEADS * V_HEAD, D), (MLA_HEADS * V_HEAD) ** -0.5),
        "w_out": nrm(ks[21], (L, D, D), D ** -0.5),
        "ffn_norm_g": 1.0 + nrm(ks[22], (L, D), 0.02),
        "moe_w_group": nrm(ks[23], (L, D, N_GROUPS), D ** -0.5),
        "moe_b_group": nrm(ks[24], (L, N_GROUPS), 0.01),
        "moe_w_router": nrm(ks[25], (L, D, N_EXPERTS), D ** -0.5),
        "moe_b_router": nrm(ks[26], (L, N_EXPERTS), 0.01),
        "moe_w_gu": nrm(ks[27], (L, N_EXPERTS, D, 2 * D_EXPERT), D ** -0.5),
        "moe_w_down": nrm(ks[28], (L, N_EXPERTS, D_EXPERT, D), D_EXPERT ** -0.5),
        "final_norm_g": 1.0 + nrm(ks[29], (D,), 0.02),
    }

def second_block(x, positions, mix_norm_g, w_in, rw_mu, rw_w0, rw_w_up, rw_a0, rw_a_up, rw_g_up,
              rw_k_k, rw_k_a, rw_r_k, rw_gn_w, rw_gn_b, mla_g_qa, mla_w_q_up, mla_g_kva, mla_w_kv_up,
              w_branch_rw, w_branch_mla, w_out, ffn_norm_g, moe_w_group, moe_b_group, moe_w_router,
              moe_b_router, moe_w_gu, moe_w_down, final_norm_g):
    inv_freq = ROPE_THETA ** (-jnp.arange(0, QK_ROPE, 2, dtype=jnp.float32) / QK_ROPE)
    ang = positions.astype(jnp.float32)[..., None] * inv_freq
    cos, sin = jnp.cos(ang).astype(x.dtype), jnp.sin(ang).astype(x.dtype)

    for l in range(DEPTH_2):
        h = rmsnorm(x, mix_norm_g[l])
        cols = h @ w_in[l]
        c_rw = cols[..., :RW_COLS]
        c_q = cols[..., RW_COLS:RW_COLS + Q_LORA]
        c_kv = cols[..., RW_COLS + Q_LORA:RW_COLS + Q_LORA + KV_LORA]
        c_kr = cols[..., RW_COLS + Q_LORA + KV_LORA:RW_COLS + MLA_COLS]
        gate_rw = jax.nn.sigmoid(cols[..., RW_COLS + MLA_COLS:RW_COLS + MLA_COLS + D_MODEL])
        gate_mla = jax.nn.sigmoid(cols[..., RW_COLS + MLA_COLS + D_MODEL:])

        y_rw = rwkv7_mix(c_rw, rw_mu[l], rw_w0[l], rw_w_up[l], rw_a0[l], rw_a_up[l], rw_g_up[l],
                         rw_k_k[l], rw_k_a[l], rw_r_k[l], rw_gn_w[l], rw_gn_b[l])
        y_mla = mla_mix(c_q, c_kv, c_kr, cos, sin, mla_g_qa[l], mla_w_q_up[l], mla_g_kva[l], mla_w_kv_up[l])
        merged = gate_rw * (y_rw @ w_branch_rw[l]) + gate_mla * (y_mla @ w_branch_mla[l])
        x = x + merged @ w_out[l]

        h2 = rmsnorm(x, ffn_norm_g[l])
        x = x + hier_moe(h2, moe_w_group[l], moe_b_group[l], moe_w_router[l], moe_b_router[l],
                         moe_w_gu[l], moe_w_down[l])

    return rmsnorm(x, final_norm_g)


def setup_inputs(seed=0):
    out = dict(first_inputs(seed))
    for name, value in second_inputs(seed + 1).items():
        if name != "x":
            out[name + "_2"] = value
    return out


def reference(
    x, positions, attn_norm_w, w_in, hgrn_lower_bounds, w_out, mlp_norm_w, w_up, w_down,
    final_norm_w, positions_2, mix_norm_g_2, w_in_2, rw_mu_2, rw_w0_2, rw_w_up_2, rw_a0_2,
    rw_a_up_2, rw_g_up_2, rw_k_k_2, rw_k_a_2, rw_r_k_2, rw_gn_w_2, rw_gn_b_2, mla_g_qa_2,
    mla_w_q_up_2, mla_g_kva_2, mla_w_kv_up_2, w_branch_rw_2, w_branch_mla_2, w_out_2,
    ffn_norm_g_2, moe_w_group_2, moe_b_group_2, moe_w_router_2, moe_b_router_2, moe_w_gu_2,
    moe_w_down_2, final_norm_g_2,
):
    x = first_block(
        x, positions, attn_norm_w, w_in, hgrn_lower_bounds, w_out, mlp_norm_w, w_up, w_down,
        final_norm_w,
    )
    return second_block(
        x, positions_2, mix_norm_g_2, w_in_2, rw_mu_2, rw_w0_2, rw_w_up_2, rw_a0_2, rw_a_up_2,
        rw_g_up_2, rw_k_k_2, rw_k_a_2, rw_r_k_2, rw_gn_w_2, rw_gn_b_2, mla_g_qa_2, mla_w_q_up_2,
        mla_g_kva_2, mla_w_kv_up_2, w_branch_rw_2, w_branch_mla_2, w_out_2, ffn_norm_g_2,
        moe_w_group_2, moe_b_group_2, moe_w_router_2, moe_b_router_2, moe_w_gu_2, moe_w_down_2,
        final_norm_g_2,
    )


_drawn_inputs = setup_inputs


def setup_inputs(seed=0):
    import zlib

    import numpy as np

    out = dict(_drawn_inputs(seed))
    spreads = {}
    factors = {'rw_w_up_2': 18.456,
     'rw_a0_2': 2.843,
     'rw_gn_w_2': 21.872,
     'rw_gn_b_2': 25.311,
     'mla_g_qa_2': 8.0,
     'mla_g_kva_2': 5.657,
     'moe_b_group_2': 19.603,
     'moe_b_router_2': 28.003,
     'final_norm_g_2': 7.765,
     'rw_k_k_2': 3.56,
     'rw_k_a_2': 4.042,
     'ffn_norm_g_2': 6.005}
    for name, (base, spread) in spreads.items():
        noise = np.random.default_rng([zlib.crc32(name.encode()), seed]).standard_normal(out[name].shape)
        drawn = base * np.exp(spread * noise) if base else spread * noise
        out[name] = __import__('jax').numpy.asarray(drawn.astype(out[name].dtype))
    for name, factor in factors.items():
        out[name] = (out[name] * factor).astype(out[name].dtype)
    return out
```

```python
from contextlib import ExitStack

import numpy as np
import concourse.bass as bass
from concourse import mybir

F32 = mybir.dt.float32
I32 = mybir.dt.int32
U8 = mybir.dt.uint8
U32 = mybir.dt.uint32
ALU = mybir.AluOpType
ACT = mybir.ActivationFunctionType
AX_X = mybir.AxisListType.X

S = 512
D = 1024
SLOT = 2048
NSLOT = 7
ARENA = 25344
BIG = 1.0e30

CO = {}
_n = 0
for _name, _w in (("ident", 128), ("ones", 128), ("ones64", 128), ("rot64", 128), ("rot32", 128),
                  ("cd", 128), ("sd", 128), ("tmask", 896), ("causal", 512), ("strict", 128),
                  ("incl", 128), ("invf64", 1), ("invf32", 1), ("iota", 32)):
    CO[_name] = (_n, _w)
    _n += _w
NC32 = _n

VO = {}
_n = 0
for _name, _w in (("an0", 8), ("an1", 8), ("mn0", 8), ("mn1", 8), ("fn1", 8), ("lb", 8),
                  ("mixg", 8), ("mu", 14), ("w0", 4), ("a0", 4), ("kk", 4), ("ka", 4), ("rk", 4),
                  ("gnw", 4), ("gnb", 4), ("gqa", 3), ("gkva", 2), ("ffg", 8), ("fing", 8)):
    VO[_name] = (_n, _w)
    _n += _w
NV = _n


class Tok:

    def __init__(self, sem, value=None):
        self.sem, self.value, self.used = sem, value, False


class Prog:

    def __init__(self, sems):
        self.sems = sems
        self.q = {e: [] for e in sems}
        self.q["sp"] = []
        self.fence = {}
        self.dma_count = {}

    def last(self, e):
        return self.q[e][-1][2]

    def op(self, e, fn, after=()):
        need = [t for t in flat(after) if t is not None]
        if e in ("act", "dve", "pool") and self.q[e] and self.q[e][-1][2].sem in self.sems:
            need.append(self.last(e))
        need += self.fence.pop(e, [])
        t = Tok(e)
        self.q[e].append((fn, need, t))
        return t

    def dma(self, e, out, in_, sem, after=()):
        self.dma_count[sem] = self.dma_count.get(sem, 0) + 16
        t = Tok(sem, self.dma_count[sem])
        self.q[e].append((lambda eng: eng.dma_start(out, in_), [x for x in flat(after) if x is not None], t))
        return t

    def barrier(self):
        ends = [self.last(e) for e in ("pe", "act", "dve", "pool") if self.q[e]]
        for e in ("pe", "act", "dve", "pool"):
            self.fence[e] = list(ends)
        return ends

    def settle(self):
        for e in self.q:
            for _, need, _ in self.q[e]:
                for t in need:
                    t.used = True
        for e in self.sems:
            n = 0
            for _, _, t in self.q[e]:
                if t.sem == e:
                    n += t.used
                    t.value = n

    def run(self, e, eng, sem_of):
        seen = {}
        for fn, need, t in self.q[e]:
            most = {}
            for x in need:
                most[x.sem] = max(most.get(x.sem, 0), x.value)
            for s, v in most.items():
                if seen.get(s, 0) < v:
                    eng.wait_ge(sem_of(s), v)
                    seen[s] = v
            ins = fn(eng)
            if t.sem != e:
                ins.then_inc(sem_of(t.sem), 16)
            elif t.used:
                ins.then_inc(sem_of(t.sem), 1)


def flat(x):
    if x is None or isinstance(x, Tok):
        return [x]
    out = []
    for y in x:
        out += flat(y)
    return out


class Room:

    def __init__(self, ap, sem=None):
        self.ap, self.sem, self.free = ap, sem, []


def bcast(ap, axis, n):
    a = ap.unsqueeze(axis)
    shape = list(a.shape)
    shape[axis] = n
    return a.broadcast_to(shape)


def build(nc, I, out, stop=None, dumps=None):
    ctx = ExitStack()
    with ctx:
        def sb(name, n, dt=F32):
            return ctx.enter_context(nc.sbuf_tensor(name, [128, n], dt))

        semh = {}

        def sem_of(s):
            if s not in semh:
                raise KeyError(s)
            return semh[s]

        for s in ["pe", "act", "dve", "pool", "const", "out"] + [f"ring{i}" for i in range(NSLOT)]:
            semh[s] = ctx.enter_context(nc.semaphore("s_" + s))
        P = Prog(["pe", "act", "dve", "pool"])

        C = sb("C", NC32)
        V = sb("V", NV)
        M8 = sb("M8", 14 * 512, U8)
        X = sb("X", 8 * S)
        H = sb("H", 8 * S)
        ring = sb("ring", NSLOT * SLOT)
        A = sb("A", ARENA)
        small = sb("small", 384)
        psum = ctx.enter_context(nc.psum_tensor("psum", [128, 8, 512], F32))

        def c(name):
            o, w = CO[name]
            return C[:, o:o + w]

        def v(name, i=0, n=1):
            o, w = VO[name]
            return V[:, o + i:o + i + n]

        slots = [Room(ring[:, i * SLOT:(i + 1) * SLOT], f"ring{i}") for i in range(NSLOT)]
        banks = [Room(psum[:, i, :]) for i in range(8)]
        turn = {"slot": 0, "bank": 0}
        held = set()

        def load(src):
            s = slots[turn["slot"] % NSLOT]
            turn["slot"] += 1
            t = P.dma("sp", s.ap[:, 0:src.shape[-1]], src, s.sem, s.free)
            return s, t

        def bank(hold=False):
            while True:
                i = turn["bank"] % 8
                turn["bank"] += 1
                if i not in held:
                    break
            if hold:
                held.add(i)
            return banks[i]

        def release(b):
            held.discard(banks.index(b))

        def mm(o, l, r, start=True, stop=True, after=()):
            return P.op("pe", lambda e: e.matmul(o, l, r, start=start, stop=stop), after)

        def tr(o, i, after=()):
            return P.op("pe", lambda e: e.matmul(o, i, c("ident")[0:i.shape[0], 0:i.shape[0]], is_transpose=True,
                                                 start=True, stop=True), after)

        def act(o, i, f, scale=1.0, bias=None, accum=None, after=()):
            kw = {}
            if bias is not None:
                kw["bias"] = bias
            if accum is not None:
                kw["accum_out"] = accum
            return P.op("act", lambda e: e.activation(o, i, f, scale=scale, **kw), after)

        def tt(e, o, a, b, op, after=()):
            return P.op(e, lambda g: g.tensor_tensor(o, a, b, op), after)

        def ts(e, o, a, s1, s2, op0, op1=None, after=()):
            if op1 is None:
                return P.op(e, lambda g: g.tensor_scalar(o, a, s1, None, op0), after)
            return P.op(e, lambda g: g.tensor_scalar(o, a, s1, s2, op0, op1), after)

        def stt(o, a, s, b, op0, op1, after=()):
            return P.op("dve", lambda g: g.scalar_tensor_tensor(o, a, s, b, op0, op1), after)

        def cp(e, o, a, after=()):
            if e == "act":
                return act(o, a, ACT.Copy, after=after)
            return P.op(e, lambda g: g.tensor_copy(o, a), after)

        def setv(e, o, x, after=()):
            return P.op(e, lambda g: g.memset(o, x), after)

        class Arena:
            def __init__(self, lo, hi):
                self.at, self.hi = lo, hi

            def take(self, n):
                assert self.at + n <= self.hi, (self.at, n, self.hi)
                a = A[:, self.at:self.at + n]
                self.at += n
                return a

        def t3(ap, n):
            return ap.rearrange("p (a b) -> p a b", a=n)

        Xt, Ht = t3(X[:, :], 8), t3(H[:, :], 8)

        t_const = [P.dma("act", C[:, :], I["c32"], "const"), P.dma("act", V[:, :], I["vecs"], "const"),
                   P.dma("act", A[:, 0:1792], I["m32"], "const")]
        for kt in range(8):
            t_const.append(P.dma("act", Xt[:, kt, :], I["x"][kt], "const"))
        t_const = t_const[-1]
        consts_at = t_const
        for e in ("pe", "act", "dve", "pool"):
            P.fence[e] = [t_const]
        eps = small[:, 0:1]
        halfpi = small[:, 1:2]
        gneps = small[:, 2:3]
        one_row = small[:, 3:4]
        cp("dve", M8[:, :].rearrange("p (l c t) -> p l c t", l=14, c=4),
           bcast(A[:, 0:1792].rearrange("p (l t) -> p l t", l=14), 2, 4))
        setv("pool", eps, 1e-6)
        setv("pool", gneps, 64e-5)
        setv("pool", one_row, 1.0)
        P.barrier()

        def rms(dst, src, nt, width, wname, scratch, rs, after=()):
            b = bank()
            t = None
            for i in range(nt):
                q = scratch[:, (i % 2) * S:(i % 2 + 1) * S]
                ta = act(q, src[:, i, :], ACT.Square, after=(after, t_mm[i - 2] if i >= 2 else None))
                if i == 0:
                    t_mm = []
                t_mm.append(mm(b.ap, c("ones"), q, i == 0, i == nt - 1, after=(ta, b.free if i == 0 else ())))
            ta = act(rs, b.ap, ACT.Sqrt, scale=1.0 / width, bias=eps, after=t_mm[-1])
            b.free = [ta]
            t = P.op("dve", lambda g: g.reciprocal(rs, rs), ta)
            for i in range(nt):
                t = stt(dst[:, i, :], src[:, i, :], v(wname, i), rs, ALU.mult, ALU.mult, after=after)
            return t

        def lin(chunks, act_of, nc_, kts, evac, after=()):
            per = nc_ // 128
            bs = [bank() for _ in range(per)]
            for j, src in enumerate(chunks):
                s, tl = load(src)
                for m in range(per):
                    for kt in range(kts):
                        t = mm(bs[m].ap, s.ap[:, kt * nc_ + m * 128:kt * nc_ + (m + 1) * 128], act_of(j * kts + kt),
                               j == 0 and kt == 0, j == len(chunks) - 1 and kt == kts - 1,
                               after=(tl, after, bs[m].free if j == 0 and kt == 0 else ()))
                s.free = [t]
                if j < len(chunks) - 1:
                    continue
                for m in range(per):
                    bs[m].free = [evac(m, bs[m].ap, t)]

        def lin_tok(s, tl, off, width, kts, nc_, act_of, dst, eng, after=()):
            for tk in range(4):
                b = bank()
                for kt in range(kts):
                    t = mm(b.ap[:, 0:width], act_of(kt)[:, tk * 128:(tk + 1) * 128],
                           s.ap[:, kt * nc_ + off:kt * nc_ + off + width], kt == 0, kt == kts - 1,
                           after=(tl, after, b.free if kt == 0 else ()))
                b.free = [cp(eng, dst[:, tk, :], b.ap[:, 0:width], after=t)]
            return t, b.free

        def tables(pos, invf, cosT, sinT, ar):
            pi = ar.take(S)
            ang, n, r = ar.take(S), ar.take(S), ar.take(S)
            tp = P.dma("act", pi.bitcast(I32), pos.partition_broadcast(128), "const", after=P.barrier())
            cp("dve", ang, pi.bitcast(I32), after=tp)
            ts("dve", ang, ang, invf, None, ALU.mult)
            MAG = 12582912.0
            for dst, q in ((sinT, 0.0), (cosT, 0.25)):
                ts("dve", n, ang, float(1 / (2 * np.pi)), float(q), ALU.mult, ALU.add)
                ts("dve", n, n, MAG, None, ALU.add)
                ts("dve", n, n, MAG, None, ALU.subtract)
                C1 = 6.28125
                C2 = float(np.float32(2 * np.pi - C1))
                C2 = float(np.float32(np.round(C2 * 2 ** 20) / 2 ** 20))
                C3 = float(2 * np.pi - C1 - C2)
                stt(r, n, -C1, ang, ALU.mult, ALU.add)
                stt(r, n, -C2, r, ALU.mult, ALU.add)
                stt(r, n, -C3, r, ALU.mult, ALU.add)
                if q:
                    ts("dve", r, r, float(np.pi / 2), None, ALU.add)
                t = ts("dve", r, r, 3.1415925, -3.1415925, ALU.min, ALU.max)
                t2 = act(dst, r, ACT.Sin, after=t)
                P.fence["dve"] = [t2]
            return t2

        class Attn:
            def __init__(self, ar):
                self.S = [ar.take(S) for _ in range(3)]
                self.PT = [ar.take(4 * S) for _ in range(2)]
                self.m = small[:, 16:48]
                self.r = small[:, 48:80]
                self.i = small[:, 80:112]
                self.tPT = [[], []]
                self.tS = [[], [], []]
                self.n = 0
                self.hd = 0
                self.b_out = None

            def head(self, scores, mask_of, klen, vtok, hp, dst_evac, after=()):
                PT = t3(self.PT[self.hd % 2], 4)
                free_PT = self.tPT[self.hd % 2]
                t_pt = []
                for qt in range(4):
                    i = self.n
                    self.n += 1
                    kl = klen(qt)
                    Sb = self.S[i % 3][:, 0:kl]
                    b = bank()
                    t = scores(b.ap[:, 0:kl], qt, kl, (after, b.free))
                    m, r, ri = (x[:, i % 32:i % 32 + 1] for x in (self.m, self.r, self.i))
                    t = mask_of(b.ap, Sb, m, qt, kl, (t, self.tS[i % 3]))
                    b.free = [t]
                    t = act(Sb, Sb, ACT.Exp, scale=-1.0, bias=m, accum=r, after=t)
                    t = P.op("dve", lambda g, ri=ri, r=r: g.reciprocal(ri, r), t)
                    t = ts("pool", Sb, Sb, ri, None, ALU.mult, after=t)
                    b = bank()
                    for k in range(kl // 128):
                        t2 = tr(b.ap[:, k * 128:(k + 1) * 128], Sb[:, k * 128:(k + 1) * 128], after=(t, b.free))
                    self.tS[i % 3] = [t2]
                    t_pt.append(cp("act" if qt % 2 else "dve", PT[:, 0:kl // 128, qt * 128:(qt + 1) * 128],
                                   t3(b.ap[:, 0:kl], kl // 128), after=(t2, free_PT)))
                    b.free = [t_pt[-1]]
                if hp == 0:
                    self.b_out = bank(hold=True)
                bo = self.b_out
                o = bo.ap[64 * hp:64 * hp + 64, :]
                for k in range(4):
                    q0 = min(q for q in range(4) if klen(q) > k * 128)
                    t = mm(o[:, q0 * 128:S], vtok(k), PT[:, k, q0 * 128:S], k == 0, k == 3,
                           after=(t_pt, bo.free if k == 0 and hp == 0 else ()))
                self.tPT[self.hd % 2] = [t]
                self.hd += 1
                if hp == 1:
                    bo.free = [dst_evac(bo.ap, t)]
                    release(bo)

        tabs = Arena(0, 1024)
        cos64, sin64 = tabs.take(S), tabs.take(S)
        tables(I["pos1"], c("invf64"), cos64, sin64, Arena(1024, 3072))
        P.barrier()

        lbv = t3(v("lb", 0, 8), 2)
        lm, le0, le1, ls = (small[:, 112 + 4 * i:116 + 4 * i] for i in range(4))
        lbs = [small[:, 128:132], small[:, 132:136]]
        oml = [small[:, 136:140], small[:, 140:144]]
        tt("dve", lm, lbv[:, 0, :], lbv[:, 1, :], ALU.max)
        tt("dve", le0, lbv[:, 0, :], lm, ALU.subtract)
        t = tt("dve", le1, lbv[:, 1, :], lm, ALU.subtract)
        act(le0, le0, ACT.Exp, after=t)
        t = act(le1, le1, ACT.Exp)
        tt("dve", ls, le0, le1, ALU.add, after=t)
        P.op("dve", lambda g: g.reciprocal(ls, ls))
        tt("dve", le0, le0, ls, ALU.mult)
        tt("dve", le1, le1, ls, ALU.mult)
        tt("dve", lbs[0], le0, le0, ALU.subtract)
        tt("dve", lbs[1], le0, le1, ALU.add)
        tt("dve", lbs[1], lbs[1], le0, ALU.subtract)
        for i in range(2):
            ts("dve", oml[i], lbs[i], -1.0, 1.0, ALU.mult, ALU.add)
        P.barrier()

        for layer in range(2):
            ar = Arena(1024, ARENA)
            scratch, rs = ar.take(2 * S), ar.take(S)
            t_h = rms(Ht, Xt, 8, D, f"an{layer}", scratch, rs)
            if stop == f"norm{layer}":
                break
            aq, ai, k2 = ar.take(2 * S), ar.take(4 * 256), ar.take(4 * S)
            ag, L, oc = ar.take(2 * S), ar.take(4 * S), None
            u, cq, ck, cv = ar.take(4 * 256), ar.take(4 * S), ar.take(4 * S), ar.take(4 * S)
            aq3, k3, L3, ag3 = t3(aq, 2), t3(k2, 4), t3(L, 4), t3(ag, 2)
            ai3, u3, cq3, ck3, cv3 = t3(ai, 4), t3(u, 4), t3(cq, 4), t3(ck, 4), t3(cv, 4)
            W = I["w_in"][layer]
            h_of = lambda kt: Ht[:, kt, :]
            tmp_at = ar.at
            sg = [ar.take(S) for _ in range(2)]
            sgt = [[], []]

            def ev_silu(dst):
                def f(m, ps, t):
                    ta = act(sg[m], ps, ACT.Sigmoid, after=(t, sgt[m]))
                    t = tt("dve", dst[:, m, :], ps, sg[m], ALU.mult, after=ta)
                    sgt[m] = [t]
                    return t
                return f

            def ev_gate(dr):
                def f(m, ps, t):
                    j = dr * 2 + m
                    ta = act(sg[m], ps, ACT.Sigmoid, after=(t, sgt[m]))
                    ts("dve", sg[m], sg[m], oml[layer][:, j:j + 1], lbs[layer][:, j:j + 1], ALU.mult, ALU.add,
                       after=ta)
                    ts("dve", k3[:, j, :], sg[m], -1.0, 1.0, ALU.mult, ALU.add)
                    t = ts("dve", L3[:, j, :], sg[m], 2.0 ** -63, None, ALU.max)
                    sgt[m] = [t]
                    return ta
                return f

            for dr in range(2):
                lin([W[2 + dr, 0]], h_of, 256, 8, ev_gate(dr), after=t_h)
            lin([W[0, 0]], h_of, 256, 8, ev_silu(aq3))
            lin([W[4, 0]], h_of, 256, 8, ev_silu(ag3))
            s, tl = load(W[1, 0])
            t, t_ai = lin_tok(s, tl, 0, 256, 8, 256, h_of, ai3, "act")
            s.free = [t]
            s, tl = load(W[5, 0])
            t, t_u = lin_tok(s, tl, 0, 256, 8, 256, h_of, u3, "act")
            s.free = [t]

            def ev_copy(dst, base):
                return lambda m, ps, t: cp("act", dst[:, base + m, :], ps, after=t)

            for j in range(2):
                lin([W[6 + j, 0]], h_of, 256, 8, ev_copy(cq3, 2 * j))
            for j in range(2):
                lin([W[8 + j, 0]], h_of, 256, 8, ev_copy(ck3, 2 * j))
            for j in range(2):
                s, tl = load(W[10 + j, 0])
                t, t_cv = lin_tok(s, tl, 0, 256, 8, 256, h_of, cv3[:, :, 256 * j:256 * j + 256], "act")
                s.free = [t]
            P.barrier()
            act(L, L, ACT.Ln)
            bre, bim = [bank() for _ in range(2)], [bank() for _ in range(2)]
            us = [ar.take(S) for _ in range(4)]
            for part, bs in ((0, bre), (1, bim)):
                s, tl = load(I["dft"][part])
                for dt_ in range(2):
                    for k in range(4):
                        t = mm(bs[dt_].ap, u3[:, k, dt_ * 128:(dt_ + 1) * 128], s.ap[:, k * S:(k + 1) * S],
                               k == 0, k == 3, after=(tl, bs[dt_].free))
                    bs[dt_].free = [cp("act", us[part * 2 + dt_], bs[dt_].ap, after=t)]
                s.free = [t]
            for dt_ in range(2):
                b = bank()
                mm(b.ap, c("cd"), us[dt_], True, False, after=(bre[dt_].free, b.free))
                t = mm(b.ap, c("sd"), us[2 + dt_], False, True, after=bim[dt_].free)
                b.free = [cp("act", Ht[:, 2 + dt_, :], b.ap, after=t)]
            P.barrier()
            if stop == f"proj{layer}":
                break

            ar.at = tmp_at
            B = ar.take(4 * 516)
            B3 = B.rearrange("p (g j) -> p g j", j=129)
            E, Kl, Ql = ar.take(2 * S), ar.take(2 * S), ar.take(S)
            Kt, Sc = ar.take(2 * S), ar.take(4 * S)
            St, dec = ar.take(4 * 2 * 64), small[:, 160:168]
            setv("pool", B3[:, :, 0:1], 0.0)
            ones_b = c("ones")
            t_b = P.last("pool")
            for g in range(16):
                j, ch = g // 4, g % 4
                t_b = P.op("dve", lambda e, g=g, j=j, ch=ch, B3=B3, L3=L3: e.tensor_tensor_scan(
                    B3[:, g, 1:129], ones_b, L3[:, j, ch * 128:(ch + 1) * 128], 0.0, ALU.mult, ALU.add), after=t_b)
            q8 = aq.rearrange("p (g t) -> p g t", t=128)
            E8, Kl8 = (x.rearrange("p (g t) -> p g t", t=128) for x in (E, Kl))
            ob = [bank(hold=True) for _ in range(2)]
            t_o = None
            for dr in range(2):
                k8 = k2[:, dr * 2 * S:(dr + 1) * 2 * S].rearrange("p (g t) -> p g t", t=128)
                Bd = B3[:, dr * 8:dr * 8 + 8, :]
                sh = 1 - dr
                ml = lambda l: M8[:, (dr * 7 + l) * 512:(dr * 7 + l + 1) * 512]

                def halves(ap, l, second, lo=0):
                    w = 2 ** l
                    return ap[:, :, lo:lo + 128].rearrange("p g (n two w) -> p g n two w", two=2, w=w)[
                        :, :, :, 1 if second else 0, :]

                for l in range(-1, 7):
                    if l >= 0:
                        w = 2 ** l
                        mid = Bd[:, :, w:w + 128 - 2 * w + 1:2 * w] if l < 6 else Bd[:, :, 64:65]
                        mid = bcast(mid, 3, w)
                        e1, e2 = halves(E8, l, False), halves(E8, l, True)
                        b1, b2 = halves(Bd, l, False, sh), halves(Bd, l, True, sh)
                        tt("dve", e1, mid, b1, ALU.subtract, after=P.last("pool"))
                        t = tt("dve", e2, b2, mid, ALU.subtract)
                        t_e = act(E, E, ACT.Exp, after=t)
                        t_k = tt("pool", Kl, E, k2[:, dr * 2 * S:(dr + 1) * 2 * S], ALU.mult, after=(t_e, t_o))
                        half = dr == 0
                        q_l = Ql.rearrange("p (g n w) -> p g n w", g=8, w=w)
                        t_q = tt("dve", q_l, halves(q8, l, half), halves(E8, l, half), ALU.mult, after=(t_e, t_o))
                        n = 64
                    else:
                        t_k = t_q = t_b
                        n = 128
                    for h in range(4):
                        hp, lo = h // 2, 64 * (h % 2)
                        b = bank()
                        for ch in range(4):
                            kk = (Kl8 if l >= 0 else k8)[lo:lo + 64, hp * 4 + ch, :]
                            qq = (Ql[lo:lo + 64, (hp * 4 + ch) * 64:(hp * 4 + ch + 1) * 64] if l >= 0
                                  else q8[lo:lo + 64, hp * 4 + ch, :])
                            t = mm(b.ap[:, ch * n:(ch + 1) * n], kk, qq, after=(t_k, t_q, b.free))
                        if l < 0:
                            t = tt("dve", t3(Sc[:, h * S:(h + 1) * S], 4), t3(b.ap, 4),
                                   bcast(c("ident"), 1, 4), ALU.mult, after=(t, t_o))
                        else:
                            w = 2 ** l
                            f = lambda ap: ap.rearrange("p (n two w) -> p n two w", two=2, w=w)[
                                :, :, 1 if half else 0, :]
                            o_, m_ = f(Sc[:, h * S:(h + 1) * S]), f(ml(l))
                            d_ = b.ap[:, 0:256].rearrange("p (n w) -> p n w", w=w)
                            t = P.op("dve", lambda g, o_=o_, m_=m_, d_=d_: g.copy_predicated(o_, m_, d_), t)
                        b.free = [t]
                    t_o = P.last("pe")
                t_sc = P.last("dve")
                tot = bcast(Bd[:, :, 128:129].squeeze(2), 2, 128)
                fl = (Bd[:, :, 1:129], Bd[:, :, 0:128])
                if dr == 0:
                    t = tt("dve", E8, tot, fl[0], ALU.subtract)
                    t_e = act(E, E, ACT.Exp, after=t)
                else:
                    t_e = act(E8, fl[1], ACT.Exp, after=P.last("dve"))
                t_k = tt("pool", Kl, E, k2[:, dr * 2 * S:(dr + 1) * 2 * S], ALU.mult, after=(t_e, t_o))
                t_dec = act(dec, Bd[:, :, 128:129].squeeze(2), ACT.Exp)
                if dr == 0:
                    t_e = act(E8, fl[0], ACT.Exp, after=t_k)
                else:
                    t = tt("dve", E8, tot, fl[1], ALU.subtract, after=t_k)
                    t_e = act(E, E, ACT.Exp, after=t)
                t_q = tt("dve", E, E, aq, ALU.mult, after=t_e)
                for hp in range(2):
                    b = bank()
                    for ch in range(4):
                        t = tr(b.ap[:, ch * 128:(ch + 1) * 128], Kl8[:, hp * 4 + ch, :], after=(t_k, b.free))
                    b.free = [cp("act", Kt.rearrange("p (c a f) -> p a c f", c=4, a=2)[:, hp], t3(b.ap, 4), after=t)]
                t_kt = P.last("act")
                St4 = St.rearrange("p (c a f) -> p c a f", c=4, a=2)
                order = [0, 1, 2, 3] if dr == 0 else [3, 2, 1, 0]
                b = bank()
                for ch in order[:3]:
                    for h in range(4):
                        hp, lo = h // 2, 64 * (h % 2)
                        t = mm(b.ap[lo:lo + 64, (ch * 2 + hp) * 64:(ch * 2 + hp + 1) * 64],
                               Kt[:, (ch * 2 + hp) * 128 + lo:(ch * 2 + hp) * 128 + lo + 64],
                               ai3[:, ch, h * 64:(h + 1) * 64], after=(t_kt, b.free))
                bs = b.ap.rearrange("p (c a f) -> p c a f", c=4, a=2)
                t = cp("dve", St4[:, order[1]], bs[:, order[0]], after=(t, t_dec))
                for i in (1, 2):
                    for hp in range(2):
                        t = stt(St4[:, order[i + 1], hp, :], St4[:, order[i], hp, :],
                                dec[:, hp * 4 + order[i]:hp * 4 + order[i] + 1], bs[:, order[i], hp, :],
                                ALU.mult, ALU.add)
                b.free = [t]
                t_st = t
                oac = [ar_o[hp] for hp in range(2)] if dr else None
                for hp in range(2):
                    for hh in range(2):
                        h, lo = hp * 2 + hh, 64 * hh
                        for ch in range(4):
                            cs = slice(ch * 128, (ch + 1) * 128)
                            inter = ch != order[0]
                            o_ = ob[hp].ap[lo:lo + 64, cs]
                            t = mm(o_, ai3[:, ch, h * 64:(h + 1) * 64],
                                   Sc[:, h * S + ch * 128:h * S + (ch + 1) * 128], True, not inter,
                                   after=(t_sc, t_st, t_q, ob[hp].free))
                            if inter:
                                t = mm(o_, St4[lo:lo + 64, ch, hp, :], E8[lo:lo + 64, hp * 4 + ch, :], False, True)
                t_o = t
                if dr == 0:
                    ar_o = [Ht[:, hp, :] for hp in range(2)]
                    for hp in range(2):
                        ob[hp].free = [cp("act", ar_o[hp], ob[hp].ap, after=t)]
                else:
                    for hp in range(2):
                        t = tt("dve", ar_o[hp], ar_o[hp], ob[hp].ap, ALU.add, after=t_o)
                        ob[hp].free = [t]
                        release(ob[hp])
                P.barrier()
            for hp in range(2):
                sq, r_ = E[:, 0:S], E[:, S:2 * S]
                t = act(sq, ar_o[hp], ACT.Square, after=P.last("dve"))
                b = bank()
                t = mm(b.ap, c("ones64"), sq, after=(t, b.free))
                t = act(r_, b.ap, ACT.Sqrt, scale=1.0 / 64, bias=eps, after=t)
                b.free = [t]
                P.op("dve", lambda g, r_=r_: g.reciprocal(r_, r_), t)
                tt("dve", r_, r_, ar_o[hp], ALU.mult)
                t = tt("dve", Ht[:, hp, :], r_, ag3[:, hp, :], ALU.mult)
                P.fence["act"] = [t]
            P.barrier()
            if stop == f"hgrn{layer}":
                break

            ar.at = tmp_at
            rt = [ar.take(S) for _ in range(2)]
            rtt = [[], []]
            n = 0
            for src in (cq3, ck3):
                for m in range(4):
                    b = bank()
                    t = mm(b.ap, c("rot64"), src[:, m, :], after=b.free)
                    t = tt("dve", rt[n % 2], b.ap, sin64, ALU.mult, after=(t, rtt[n % 2]))
                    b.free = [t]
                    t2 = tt("pool", src[:, m, :], src[:, m, :], cos64, ALU.mult, after=P.last("pe"))
                    t = tt("dve", src[:, m, :], src[:, m, :], rt[n % 2], ALU.add, after=t2)
                    n += 1
            t_rot = P.last("dve")
            at = Attn(ar)
            for h in range(8):
                hp, lo = h // 2, 64 * (h % 2)

                def scores(o, qt, kl, after, hp=hp, lo=lo):
                    return mm(o, cq3[lo:lo + 64, hp, qt * 128:(qt + 1) * 128], ck3[lo:lo + 64, hp, :],
                              after=(after, t_rot))

                def mask(ps, Sb, m, qt, kl, after):
                    tm = c("tmask")[:, (3 - qt) * 128:(3 - qt) * 128 + S]
                    return P.op("dve", lambda g: g.tensor_tensor_reduce(
                        Sb, ps[:, 0:kl], tm, -0.125, 3.0e38, ALU.add, ALU.min, m), after)

                at.head(scores, mask, lambda qt: S, lambda k, h=h: cv3[:, k, h * 64:(h + 1) * 64], h % 2,
                        lambda ps, t, hp=hp: cp("act", Ht[:, 4 + hp, :], ps, after=t))
            P.barrier()
            if stop == f"mix{layer}":
                break

            def ev_res(mt):
                return lambda m, ps, t: tt("dve", Xt[:, 2 * mt + m, :], Xt[:, 2 * mt + m, :], ps, ALU.add, after=t)

            for j in range(4):
                lin([I["w_out"][layer][j, 0]], h_of, 256, 8, ev_res(j))
            P.barrier()
            if stop == f"res{layer}":
                break

            ar = Arena(1024, ARENA)
            scratch, rs = ar.take(2 * S), ar.take(S)
            hid = t3(ar.take(32 * S), 32)
            rl = [ar.take(S) for _ in range(2)]
            rlt = [[], []]
            t_h = rms(Ht, Xt, 8, D, f"mn{layer}", scratch, rs)

            def ev_hid(j):
                def f(m, ps, t):
                    ta = act(rl[m], ps, ACT.Relu, after=(t, rlt[m]))
                    t = tt("dve", hid[:, 2 * j + m, :], rl[m], rl[m], ALU.mult, after=ta)
                    rlt[m] = [t]
                    return ta
                return f

            for j in range(16):
                lin([I["w_up"][layer][j, 0]], h_of, 256, 8, ev_hid(j), after=t_h)
            t_hid = P.last("dve")
            for j in range(4):
                lin([I["w_down"][layer][j, k] for k in range(4)], lambda kt: hid[:, kt, :], 256, 8, ev_res(j),
                    after=t_hid)
            P.barrier()
            if stop == f"ffn{layer}":
                break
        else:
            ar = Arena(1024, ARENA)
            rms(Xt, Xt, 8, D, "fn1", ar.take(2 * S), ar.take(S))
            P.barrier()
            if stop != "b1":
                second = True
                tabs = Arena(0, 1024)
                cos32, sin32 = tabs.take(S), tabs.take(S)
                tables(I["pos2"], c("invf32"), cos32, sin32, Arena(1024, 3072))
                P.barrier()
                ar = Arena(1024, ARENA)
                yrw, ymla = t3(ar.take(4 * S), 4), None
                rw_at = ar.at
                scratch, rs = ar.take(2 * S), ar.take(S)
                t_h = rms(Ht, Xt, 8, D, "mixg", scratch, rs)
                P.barrier()
                ar.at = rw_at
                h_of = lambda kt: Ht[:, kt, :]
                W2 = I["w_in2"]

                sgd = ar.take(S)
                Z = t3(ar.take(12 * S), 12)
                zr, zk, zv = Z[:, 0:4], Z[:, 4:8], Z[:, 8:12]
                aa, kkv = t3(ar.take(4 * S), 4), t3(ar.take(4 * S), 4)
                keep_at = ar.at
                cb = [ar.take(S + 1) for _ in range(2)]
                df = [ar.take(S) for _ in range(2)]
                zwa = ar.take(S)
                for m in range(2):
                    setv("pool", cb[m][:, 0:1], 0.0)
                t_z0 = P.last("pool")
                cbt = [[], []]

                def ev_shift(j):
                    def f(m, ps, t):
                        i = 2 * j + m
                        dst = Z[:, i, :] if i < 12 else (zwa if i == 12 else sgd)
                        ta = cp("act", cb[m][:, 1:S + 1], ps, after=(t, cbt[m]))
                        tt("dve", df[m], cb[m][:, 0:S], cb[m][:, 1:S + 1], ALU.subtract, after=(ta, t_z0))
                        t = stt(dst, df[m], v("mu", i), cb[m][:, 1:S + 1], ALU.mult, ALU.add)
                        cbt[m] = [t]
                        return ta
                    return f

                for j in range(7):
                    lin([W2[j, 0]], h_of, 256, 8, ev_shift(j))
                t_z = P.last("dve")
                act(zwa[0:64, :], zwa[0:64, :], ACT.Tanh, after=t_z)
                t_wa = act(sgd, sgd, ACT.Sigmoid)
                Bw = ar.take(4 * 516)
                E1, E2 = ar.take(4 * 516), ar.take(4 * 516)
                sgw = [df[0], df[1]]
                B3, E13, E23 = (x.rearrange("p (g j) -> p g j", j=129) for x in (Bw, E1, E2))
                setv("pool", B3[:, :, 0:1], 0.0)
                t_b0 = P.last("pool")
                s, tl = load(I["wa_up"])
                sct = [[], []]
                for j in range(4):
                    b = bank()
                    t = mm(b.ap, s.ap[0:64, j * 128:(j + 1) * 128], zwa[0:64, :], after=(tl, t_wa, b.free))
                    ta = act(sgw[j % 2], b.ap, ACT.Sigmoid, bias=v("w0", j), after=(t, sct[j % 2]))
                    b.free = [ta]
                    for ch in range(4):
                        t = P.op("dve", lambda e, j=j, ch=ch: e.tensor_tensor_scan(
                            B3[:, j * 4 + ch, 1:129], c("ones"), sgw[j % 2][:, ch * 128:(ch + 1) * 128], 0.0,
                            ALU.mult, ALU.add), after=(ta, t_b0))
                    sct[j % 2] = [t]
                for j in range(4):
                    b = bank()
                    t = mm(b.ap, s.ap[64:128, j * 128:(j + 1) * 128], zwa[64:128, :], after=b.free)
                    b.free = [act(aa[:, j, :], b.ap, ACT.Sigmoid, bias=v("a0", j), after=t)]
                s.free = [t]
                t_aa = P.last("act")
                for j in range(4):
                    ts("dve", kkv[:, j, :], zk[:, j, :], v("kk", j), None, ALU.mult)
                    t = tt("dve", df[0], kkv[:, j, :], kkv[:, j, :], ALU.mult, after=t_aa)
                    b = bank()
                    t = mm(b.ap, c("ones64"), df[0], after=(t, b.free))
                    t = act(df[1], b.ap, ACT.Sqrt, after=t)
                    b.free = [t]
                    ts("dve", df[1], df[1], 1e-12, None, ALU.max, after=t)
                    P.op("dve", lambda g: g.reciprocal(df[1], df[1]))
                    tt("dve", kkv[:, j, :], kkv[:, j, :], df[1], ALU.mult)
                    ts("dve", df[0], aa[:, j, :], -1.0, v("ka", j), ALU.add, ALU.mult)
                    stt(zk[:, j, :], df[0], 1.0, zk[:, j, :], ALU.add, ALU.mult)
                    stt(aa[:, j, :], kkv[:, j, :], -1.0, aa[:, j, :], ALU.mult, ALU.mult)
                LD = float(-np.exp(-0.5))
                midc = small[:, 160:176]
                cp("dve", midc, B3[:, :, 64:65].squeeze(2))
                t = tt("dve", B3, B3, bcast(midc, 2, 129), ALU.subtract)
                act(E1, Bw, ACT.Exp, scale=LD, after=t)
                t_e = act(E2, Bw, ACT.Exp, scale=-LD)
                sp = lambda x: x.rearrange("p a (c t) -> p (a c) t", c=4)
                tt("dve", sp(zr), sp(zr), E13[:, :, 1:129], ALU.mult, after=t_e)
                tt("dve", sp(kkv), sp(kkv), E13[:, :, 0:128], ALU.mult)
                tt("dve", sp(zk), sp(zk), E23[:, :, 1:129], ALU.mult)
                tt("dve", sp(aa), sp(aa), E23[:, :, 1:129], ALU.mult)
                e_in, e_out, e_all = small[:, 176:192], small[:, 192:208], small[:, 208:224]
                cp("dve", e_in, E23[:, :, 0:1].squeeze(2))
                cp("dve", e_out, E13[:, :, 128:129].squeeze(2))
                tt("dve", e_all, e_in, e_out, ALU.mult)
                P.barrier()

                ar.at = keep_at
                tok = [ar.take(S) for _ in range(3)]
                G = []
                for g in range(2):
                    G.append({n: ar.take(S) for n in ("AT", "X", "XT", "T1", "ak", "rb", "rk")})
                rhs, sa = ar.take(S), ar.take(S)
                St, S0 = ar.take(256), ar.take(256)
                St3, S03 = t3(St, 4), t3(S0, 4)
                tmp = rhs[:, 0:256]
                setv("pool", St, 0.0)
                t_s = P.last("pool")
                eq = lambda x, ch: x.rearrange("p (a c) -> p a c", c=4)[:, :, ch]
                done = []
                for ch in range(4):
                    cs = slice(ch * 128, (ch + 1) * 128)
                    for i, src in enumerate((aa, zk, zv)):
                        b = bank()
                        for j in range(4):
                            t = tr(b.ap[:, j * 128:(j + 1) * 128], src[:, j, cs], after=(b.free, done))
                        b.free = [cp("act", tok[i], b.ap, after=(t, done))]
                    t_tok = P.last("act")

                    def pairs(g, l, r, after):
                        b = bank()
                        for i in range(4):
                            j, lo = i, 64 * g
                            t = mm(b.ap[:, i * 128:(i + 1) * 128], l[lo:lo + 64, j, cs], r[lo:lo + 64, j, cs],
                                   after=(after, b.free))
                        return b, t

                    def masked(o, b, t, name, after):
                        b.free = [tt("dve", t3(o, 4), t3(b.ap, 4), bcast(c(name), 1, 4), ALU.mult, after=(t, after))]

                    def pred(o, l, ps, t):
                        return P.op("dve", lambda e: e.copy_predicated(o, M8[:, l * 512:(l + 1) * 512], ps), t)

                    for g in range(2):
                        g_ = G[g]
                        b, t = pairs(g, aa, kkv, done)
                        masked(g_["AT"], b, t, "strict", done)
                        cp("dve", t3(g_["XT"], 4), bcast(c("ident"), 1, 4))
                        pred(g_["XT"], 0, b.ap, None)
                        b.free = [P.last("dve")]
                        b, t = pairs(g, kkv, aa, done)
                        cp("dve", t3(g_["X"], 4), bcast(c("ident"), 1, 4))
                        b.free = [pred(g_["X"], 7, b.ap, t)]
                        for name, l, r, mk in (("ak", zk, kkv, "strict"), ("rb", aa, zr, "incl"), ("rk", zk, zr, "incl")):
                            b, t = pairs(g, l, r, done)
                            masked(g_[name], b, t, mk, done)
                    tx = [P.last("dve")] * 2
                    for l in range(1, 7):
                        t1 = [None, None]
                        for g in range(2):
                            g_ = G[g]
                            b = bank()
                            for i in range(4):
                                k = slice(i * 128, (i + 1) * 128)
                                t = mm(b.ap[:, k], g_["AT"][:, k], g_["X"][:, k], after=(tx[g], b.free))
                            b.free = [cp("act", g_["T1"], b.ap, after=t)]
                            t1[g] = b.free
                        for g in range(2):
                            g_ = G[g]
                            b2 = bank()
                            for i in range(4):
                                k = slice(i * 128, (i + 1) * 128)
                                t2 = mm(b2.ap[:, k], g_["T1"][:, k], g_["XT"][:, k], after=(t1[g], b2.free))
                            if l < 6:
                                b = bank()
                                for i in range(4):
                                    k = slice(i * 128, (i + 1) * 128)
                                    t = mm(b.ap[:, k], g_["XT"][:, k], g_["T1"][:, k], after=(t1[g], b.free))
                                b.free = [pred(g_["X"], 7 + l, b.ap, t)]
                            b2.free = [pred(g_["XT"], l, b2.ap, (t2, t if l < 6 else None))]
                            tx[g] = b2.free
                    t_s0 = tt("dve", S03, St3, bcast(eq(e_in, ch), 2, 64), ALU.mult, after=(t_s, done))
                    t_r = []
                    for g in range(2):
                        b = bank()
                        lo = 64 * g
                        for j in range(4):
                            h, k = 2 * j + g, slice(j * 128, j * 128 + 128)
                            o = b.ap[:, j * 64:(j + 1) * 64]
                            mm(o, G[g]["ak"][:, k], tok[2][:, h * 64:(h + 1) * 64], True, False,
                               after=(t_tok, t_s0, b.free))
                            t = mm(o, kkv[lo:lo + 64, j, cs], S03[lo:lo + 64, j, :], False, True)
                        b.free = [cp("act", rhs.rearrange("p (j g f) -> p g j f", j=4, g=2)[:, g],
                                     t3(b.ap[:, 0:256], 4), after=t)]
                        t_r.append(b.free)
                    t = t_r
                    b = bank()
                    for h in range(8):
                        g_, k = G[h % 2], slice(h // 2 * 128, h // 2 * 128 + 128)
                        t2 = mm(b.ap[:, h * 64:(h + 1) * 64], g_["XT"][:, k], rhs[:, h * 64:(h + 1) * 64],
                                after=(t, tx, b.free))
                    b.free = [cp("act", sa, b.ap, after=t2)]
                    t_sa = b.free
                    b, by = bank(), bank()
                    for h in range(8):
                        g_, k, j, lo = G[h % 2], slice(h // 2 * 128, h // 2 * 128 + 128), h // 2, 64 * (h % 2)
                        hs = slice(h * 64, (h + 1) * 64)
                        o = b.ap[lo:lo + 64, j * 64:(j + 1) * 64]
                        mm(o, tok[0][:, hs], sa[:, hs], True, False, after=(t_sa, b.free))
                        t = mm(o, tok[1][:, hs], tok[2][:, hs], False, True)
                    for h in range(8):
                        g_, k, j, lo = G[h % 2], slice(h // 2 * 128, h // 2 * 128 + 128), h // 2, 64 * (h % 2)
                        hs = slice(h * 64, (h + 1) * 64)
                        o = by.ap[lo:lo + 64, j * 128:(j + 1) * 128]
                        mm(o, tok[2][:, hs], g_["rk"][:, k], True, False, after=by.free)
                        mm(o, sa[:, hs], g_["rb"][:, k], False, False)
                        t_y = mm(o, S03[lo:lo + 64, j, :], zr[lo:lo + 64, j, cs], False, True)
                    tt("dve", t3(tmp, 4), t3(b.ap[:, 0:256], 4), bcast(eq(e_out, ch), 2, 64), ALU.mult, after=t)
                    b.free = [P.last("dve")]
                    tt("dve", St3, St3, bcast(eq(e_all, ch), 2, 64), ALU.mult)
                    t_s = tt("dve", St, St, tmp, ALU.add)
                    by.free = [cp("act", yrw[:, :, cs], t3(by.ap, 4), after=t_y)]
                    done = [t_y, t_s, by.free]
                P.barrier()
                ar.at = keep_at
                w = [ar.take(S) for _ in range(8)]
                s, tl = load(I["g_up"])
                for j in range(4):
                    y_, (d_, q_, r_, p_) = yrw[:, j, :], w[4 * (j % 2):4 * (j % 2) + 4]
                    P.fence["dve"] = P.fence["act"] = P.fence["pool"] = P.barrier() if j > 1 else []
                    b = bank()
                    t = mm(b.ap, c("ones64"), y_, after=b.free)
                    t = stt(d_, b.ap, -1.0 / 64, y_, ALU.mult, ALU.add, after=t)
                    b.free = [t]
                    t = act(q_, d_, ACT.Square, after=t)
                    b = bank()
                    t = mm(b.ap, c("ones64"), q_, after=(t, b.free))
                    t = act(r_, b.ap, ACT.Sqrt, scale=1.0 / 64, bias=gneps, after=t)
                    b.free = [t]
                    P.op("dve", lambda g, r_=r_: g.reciprocal(r_, r_), t)
                    tt("dve", d_, d_, r_, ALU.mult)
                    ts("dve", d_, d_, v("gnw", j), v("gnb", j), ALU.mult, ALU.add)
                    t = stt(p_, zr[:, j, :], v("rk", j), zk[:, j, :], ALU.mult, ALU.mult)
                    b = bank()
                    t = mm(b.ap, c("ones64"), p_, after=(t, b.free))
                    t = tt("dve", p_, b.ap, zv[:, j, :], ALU.mult, after=t)
                    b.free = [t]
                    tt("dve", d_, d_, p_, ALU.add)
                    b = bank()
                    t = mm(b.ap, s.ap[:, j * 128:(j + 1) * 128], sgd, after=(tl, b.free))
                    t = tt("dve", y_, d_, b.ap, ALU.mult, after=t)
                    b.free = [t]
                s.free = [P.last("pe")]
                P.barrier()
            if stop == "rwkv":
                pass
            elif stop != "b1":
                ar.at = rw_at
                ymla = t3(ar.take(4 * S), 4)
                mrg_at = ar.at
                qd, kvd, kr = t3(ar.take(3 * S), 3), t3(ar.take(2 * S), 2), ar.take(S)
                scratch, rs = ar.take(2 * S), ar.take(S)
                lat = [qd[:, 0, :], qd[:, 1, :], qd[:, 2, :], kvd[:, 0, :], kvd[:, 1, :], kr]
                for j in range(3):
                    lin([W2[7 + j, 0]], h_of, 256, 8,
                        lambda m, ps, t, j=j: cp("act", lat[2 * j + m], ps, after=t))
                t_l = P.last("act")
                t_q = rms(qd, qd, 3, 384, "gqa", scratch, rs, after=t_l)
                P.barrier()
                t_kv = rms(kvd, kvd, 2, 256, "gkva", scratch, rs)
                P.barrier()
                qn, qr, kn, vt = t3(ar.take(4 * S), 4), t3(ar.take(2 * S), 2), t3(ar.take(4 * S), 4), t3(ar.take(4 * S), 4)
                lin_q = lambda kt: qd[:, kt, :]
                lin([I["qn_up"]], lin_q, 512, 3, lambda m, ps, t: cp("act", qn[:, m, :], ps, after=t))
                lin([I["qr_up"]], lin_q, 256, 3, lambda m, ps, t: cp("dve", qr[:, m, :], ps, after=t))
                s, tl = load(I["kv_up"])
                for m in range(4):
                    b = bank()
                    for kt in range(2):
                        t = mm(b.ap, s.ap[:, kt * 1024 + m * 128:kt * 1024 + (m + 1) * 128], kvd[:, kt, :], kt == 0,
                               kt == 1, after=(tl, b.free))
                    b.free = [cp("act", kn[:, m, :], b.ap, after=t)]
                t, _ = lin_tok(s, tl, 512, 512, 2, 1024, lambda kt: kvd[:, kt, :], vt, "dve")
                s.free = [t]
                rt = ar.take(S)
                for src in (qr[:, 0, :], qr[:, 1, :], kr):
                    b = bank()
                    t = mm(b.ap, c("rot32"), src, after=(b.free, P.last("dve")))
                    t2 = tt("dve", rt, b.ap, sin32, ALU.mult, after=t)
                    b.free = [t2]
                    tt("dve", src, src, cos32, ALU.mult)
                    tt("dve", src, src, rt, ALU.add)
                P.barrier()
                at = Attn(ar)
                for h in range(8):
                    hp, lo, ro = h // 2, 64 * (h % 2), 32 * (h % 4)

                    def scores(o, qt, kl, after, h=h, hp=hp, lo=lo, ro=ro):
                        mm(o, qn[lo:lo + 64, hp, qt * 128:(qt + 1) * 128], kn[lo:lo + 64, hp, 0:kl], True, False, after)
                        return mm(o, qr[ro:ro + 32, h // 4, qt * 128:(qt + 1) * 128], kr[ro:ro + 32, 0:kl], False, True)

                    def mask(ps, Sb, m, qt, kl, after):
                        tm = c("causal")[:, (3 - qt) * 128:512]
                        return P.op("dve", lambda g: g.tensor_tensor_reduce(
                            Sb, ps[:, 0:kl], tm, float(-1.0 / np.sqrt(96.0)), 3.0e38, ALU.add, ALU.min, m), after)

                    at.head(scores, mask, lambda qt: 128 * (qt + 1), lambda k, h=h: vt[:, k, h * 64:(h + 1) * 64],
                            h % 2, lambda ps, t, hp=hp: cp("act", ymla[:, hp, :], ps, after=t))
                P.barrier()
            if stop in ("rwkv", "mla", "b1"):
                pass
            else:
                ar.at = mrg_at
                mrg = t3(ar.take(8 * S), 8)
                gb = [t3(ar.take(4 * S), 4) for _ in range(2)]
                tb = [ar.take(S) for _ in range(2)]
                gbt = [[], []]
                tbt = [[], []]
                for j in range(2):
                    for br, y in ((0, yrw), (1, ymla)):
                        for i in range(2):
                            lin([W2[10 + 4 * br + 2 * j + i, 0]], h_of, 256, 8,
                                lambda m, ps, t, br=br, i=i: act(gb[br][:, 2 * i + m, :], ps, ACT.Sigmoid,
                                                                after=(t, gbt[br])))
                        t_g = P.last("act")

                        def ev_m(m, ps, t, br=br, j=j, t_g=t_g):
                            if br == 0:
                                return tt("dve", mrg[:, 4 * j + m, :], ps, gb[0][:, m, :], ALU.mult, after=(t, t_g))
                            r = tt("dve", tb[m % 2], ps, gb[1][:, m, :], ALU.mult, after=(t, t_g))
                            tt("dve", mrg[:, 4 * j + m, :], mrg[:, 4 * j + m, :], tb[m % 2], ALU.add)
                            return r

                        lin([I["wb"][br, j]], lambda kt, y=y: y[:, kt, :], 512, 4, ev_m)
                        gbt[br] = [P.last("dve")]
                t_m = P.last("dve")

                def ev_res2(mt):
                    return lambda m, ps, t: tt("dve", Xt[:, 2 * mt + m, :], Xt[:, 2 * mt + m, :], ps, ALU.add, after=t)

                for j in range(4):
                    lin([I["w_out2"][j, 0]], lambda kt: mrg[:, kt, :], 256, 8, ev_res2(j), after=t_m)
                P.barrier()
            if stop in ("rwkv", "mla", "b1", "mid"):
                pass
            else:
                ar = Arena(0, ARENA)
                scratch, rs = ar.take(2 * S), ar.take(S)
                t_h = rms(Ht, Xt, 8, D, "ffg", scratch, rs)
                ar.at = 0
                P.barrier()
                lg, bb = ar.take(144), ar.take(36)
                lg3 = t3(lg, 4)
                t_bb = P.dma("act", bb, I["br"].partition_broadcast(128), "const", after=P.barrier())
                s, tl = load(I["wr"])
                t, _ = lin_tok(s, tl, 0, 36, 8, 36, h_of, lg3, "act")
                s.free = [t]
                tt("dve", lg3, lg3, bcast(bb, 1, 4), ALU.add, after=(P.last("act"), t_bb))
                gl, fl_, pen = t3(ar.take(16), 4), t3(ar.take(128), 4), t3(ar.take(16), 4)
                cand, oh1, oh2, Gt = (t3(ar.take(128), 4) for _ in range(4))
                cg, mx, gm, gs, m1, m2, ee, g1, g2 = (ar.take(16 if i == 0 else 4) for i in range(9))
                cg = t3(cg, 4)
                b4 = lambda x, n: bcast(x, 2, n)

                def red(o, a, op):
                    return P.op("dve", lambda g: g.tensor_reduce(o, a, AX_X, op))

                def one_hot(dst, src, top, tmp_, n):
                    red(top, src, ALU.max)
                    tt("dve", tmp_, src, b4(top, n), ALU.is_equal)
                    tt("dve", tmp_, tmp_, bcast(c("iota")[:, 0:n], 1, 4), ALU.mult)
                    red(mx, tmp_, ALU.max)
                    return tt("dve", dst, tmp_, b4(mx, n), ALU.is_equal)

                cp("dve", gl, lg3[:, :, 0:4])
                cp("dve", fl_, lg3[:, :, 4:36])
                one_hot(pen, gl, gm, cg, 4)
                t = tt("dve", gl, gl, b4(gm, 4), ALU.subtract)
                t = act(gl, gl, ACT.Exp, after=t)
                P.fence["dve"] = [t]
                red(gs, gl, ALU.add)
                P.op("dve", lambda g: g.reciprocal(gs, gs))
                ts("dve", pen, pen, -1.0, BIG, ALU.add, ALU.mult)
                f16 = fl_.rearrange("p a (g e) -> p (a g) e", e=8)
                tt("dve", f16, f16, bcast(pen.rearrange("p a g -> p (a g)"), 2, 8), ALU.add)
                one_hot(oh1, fl_, m1, cand, 32)
                stt(fl_, oh1, -BIG, fl_, ALU.mult, ALU.add)
                one_hot(oh2, fl_, m2, cand, 32)
                t = tt("dve", ee, m2, m1, ALU.subtract)
                t = act(ee, ee, ACT.Exp, after=t)
                ts("dve", g1, ee, 1.0, None, ALU.add, after=t)
                P.op("dve", lambda g: g.reciprocal(g1, g1))
                tt("dve", g1, g1, gs, ALU.mult)
                tt("dve", g2, g1, ee, ALU.mult)
                tt("dve", Gt, oh1, b4(g1, 32), ALU.mult)
                tt("dve", oh2, oh2, b4(g2, 32), ALU.mult)
                t_g = tt("dve", Gt, Gt, oh2, ALU.add)
                GT = ar.take(S)
                b = bank()
                for k in range(4):
                    t = tr(b.ap[0:32, k * 128:(k + 1) * 128], Gt[:, k, :], after=(t_g, b.free))
                b.free = [cp("dve", GT[0:32, :], b.ap[0:32, :], after=t)]
                t_gt = P.last("dve")
                sg = [ar.take(S) for _ in range(2)]
                hg = [t3(ar.take(2 * S), 2) for _ in range(2)]
                hgt = [[], []]
                for e_ in range(32):
                    bg = bank()
                    t_b = mm(bg.ap, bcast(c("ident")[0:32, e_], 1, 128), GT[0:32, :], after=(t_gt, bg.free))
                    hb = hg[e_ % 2]

                    def ev_g(m, ps, t, hb=hb, e_=e_):
                        ta = act(sg[m], ps, ACT.Sigmoid, after=(t, hgt[e_ % 2]))
                        return tt("dve", hb[:, m, :], ps, sg[m], ALU.mult, after=(ta, hgt[e_ % 2]))

                    def ev_u(m, ps, t, hb=hb, bg=bg, t_b=t_b):
                        r = tt("dve", hb[:, m, :], hb[:, m, :], ps, ALU.mult, after=t)
                        bg.free = [tt("dve", hb[:, m, :], hb[:, m, :], bg.ap, ALU.mult, after=t_b)]
                        return r

                    lin([I["w_gu"][e_, 0]], h_of, 256, 8, ev_g)
                    lin([I["w_gu"][e_, 1]], h_of, 256, 8, ev_u)
                    t_hb = P.last("dve")
                    s, tl = load(I["w_dn"][e_])
                    for m in range(8):
                        b = bank()
                        for kt in range(2):
                            t = mm(b.ap, s.ap[:, kt * 1024 + m * 128:kt * 1024 + (m + 1) * 128], hb[:, kt, :],
                                   kt == 0, kt == 1, after=(tl, t_hb, b.free))
                        b.free = [tt("dve", Xt[:, m, :], Xt[:, m, :], b.ap, ALU.add, after=t)]
                    s.free = [t]
                    hgt[e_ % 2] = [t, P.last("dve")]
                P.barrier()
                ar.at = 0
                rms(Xt, Xt, 8, D, "fing", ar.take(2 * S), ar.take(S))
                P.barrier()
        t_end = P.barrier()
        P.fence = {}
        for kt in range(8):
            t = P.dma("sp", out[kt * 128:(kt + 1) * 128, :], Xt[:, kt, :], "out", after=t_end)
        total = t
        P.q["sp"].append((lambda e: None, [total], None))
        P.settle()
        finish(nc, ctx, P, sem_of)
    return nc


def finish(nc, ctx, P, sem_of):
    block = ctx.enter_context(nc.Block())
    end = P.q["sp"].pop()
    end[1][0].used = True

    @block.sync
    def _(eng):
        P.run("sp", eng, sem_of)
        eng.wait_ge(sem_of("out"), end[1][0].value)

    @block.scalar
    def _(eng):
        P.run("act", eng, sem_of)

    @block.gpsimd
    def _(eng):
        P.run("pool", eng, sem_of)

    @block.vector
    def _(eng):
        P.run("dve", eng, sem_of)

    @block.tensor
    def _(eng):
        P.run("pe", eng, sem_of)


def constants():
    f = np.float32
    C = np.zeros((128, NC32), f)

    def put(name, x):
        o, w = CO[name]
        C[:, o:o + w] = x

    i = np.arange(128)
    put("ident", np.eye(128))
    put("ones", 1.0)
    put("ones64", (i[:, None] // 64 == i[None] // 64))
    for name, w in (("rot64", 64), ("rot32", 32)):
        R = np.zeros((128, 128))
        for m in range(128):
            g, r = m // w * w, m % w
            if r < w // 2:
                R[g + r + w // 2, m] = -1.0
            else:
                R[g + r - w // 2, m] = 1.0
        put(name, R)
    d = np.arange(64)
    ang = 2 * np.pi * np.outer(d, d) / 64
    sc = 1.0 / np.sqrt(512.0 * 64.0)
    put("cd", np.kron(np.eye(2), np.cos(ang) * sc))
    put("sd", np.kron(np.eye(2), -np.sin(ang) * sc))
    delta = np.abs(i[:, None] + 384 - np.arange(896)[None])
    count = (delta <= 64) * 1.0 + ((delta <= 256) & (delta % 4 == 0)) + (delta % 16 == 0)
    put("tmask", np.where(count > 0, 8.0 * np.log(np.maximum(count, 1)), -BIG))
    put("causal", np.where(np.arange(512)[None] - 384 <= i[:, None], 0.0, -BIG))
    put("strict", i[:, None] < i[None])
    put("incl", i[:, None] <= i[None])
    iv = (f(10000.0) ** (-np.arange(0, 64, 2, dtype=f) / f(64))).astype(f)
    put("invf64", np.tile(iv, 4)[:, None])
    iv = (f(10000.0) ** (-np.arange(0, 32, 2, dtype=f) / f(32))).astype(f)
    put("invf32", np.tile(iv, 8)[:, None])
    put("iota", 32.0 - np.arange(32)[None])
    M = np.zeros((128, 14, 128), f)
    for l in range(7):
        same = (i[:, None] >> (l + 1)) == (i[None] >> (l + 1))
        m = same & ((i[:, None] >> l) % 2 == 0) & ((i[None] >> l) % 2 == 1)
        M[:, l] = m
        M[:, 7 + l] = m.T
    p = np.arange(512)
    a = 2 * np.pi * (np.outer(p, p) % 512) / 512
    dft = np.stack([np.cos(a), np.sin(a)]).astype(f).reshape(2, 4, 128, 512).transpose(0, 2, 1, 3)
    return {"c32": C, "m32": M.reshape(128, -1), "dft": np.ascontiguousarray(dft.reshape(2, 128, 2048))}


def lay(w, kt, nc_):
    K, N = w.shape
    return np.ascontiguousarray(
        w.reshape(K // (128 * kt), kt, 128, N // nc_, nc_).transpose(3, 0, 2, 1, 4).reshape(
            N // nc_, K // (128 * kt), 128, kt * nc_))


def cols(x):
    return np.ascontiguousarray(x.reshape(-1, 128).T)


def layout(inp):
    g = {k: np.asarray(x) for k, x in inp.items()}
    a = constants()
    a["x"] = np.ascontiguousarray(g["x"][0].T.reshape(8, 128, 512))
    a["pos1"] = np.ascontiguousarray(g["positions"][0])
    a["w_in"] = np.stack([lay(g["w_in"][i], 8, 256) for i in range(2)])
    a["w_out"] = np.stack([lay(g["w_out"][i], 8, 256) for i in range(2)])
    a["w_up"] = np.stack([lay(g["w_up"][i], 8, 256) for i in range(2)])
    a["w_down"] = np.stack([lay(g["w_down"][i], 8, 256) for i in range(2)])
    q = {k[:-2]: x[0] for k, x in g.items() if k.endswith("_2")}
    a["pos2"] = np.ascontiguousarray(g["positions_2"][0])
    w = q["w_in"]
    a["w_in2"] = lay(np.concatenate([w[:, :2432]] + [w[:, 2432:2464]] * 4 + [w[:, 2464:]], 1), 8, 256)
    a["wa_up"] = np.concatenate([q["rw_w_up"], q["rw_a_up"]], 0)
    a["g_up"] = np.ascontiguousarray(q["rw_g_up"])
    wq = q["mla_w_q_up"].reshape(384, 8, 96)
    a["qn_up"] = lay(wq[:, :, :64].reshape(384, 512), 3, 512)[0, 0]
    a["qr_up"] = lay(wq[:, :, 64:].reshape(384, 256), 3, 256)[0, 0]
    wk = q["mla_w_kv_up"].reshape(256, 8, 128)
    a["kv_up"] = lay(np.concatenate([wk[:, :, :64].reshape(256, 512), wk[:, :, 64:].reshape(256, 512)], 1), 2, 1024)[0, 0]
    a["wb"] = np.stack([lay(q["w_branch_rw"], 4, 512)[:, 0], lay(q["w_branch_mla"], 4, 512)[:, 0]])
    a["w_out2"] = lay(q["w_out"], 8, 256)
    a["wr"] = lay(np.concatenate([q["moe_w_group"], q["moe_w_router"]], 1), 8, 36)[0, 0]
    a["br"] = np.concatenate([q["moe_b_group"], q["moe_b_router"]])
    w = q["moe_w_gu"].reshape(32, 8, 128, 2, 256).transpose(0, 3, 2, 1, 4)
    a["w_gu"] = np.ascontiguousarray(w).reshape(32, 2, 128, 2048)
    a["w_dn"] = np.ascontiguousarray(q["moe_w_down"].reshape(32, 2, 128, 1024).transpose(0, 2, 1, 3)).reshape(32, 128, 2048)
    vec = {"an0": g["attn_norm_w"][0], "an1": g["attn_norm_w"][1], "mn0": g["mlp_norm_w"][0],
           "mn1": g["mlp_norm_w"][1], "fn1": g["final_norm_w"], "lb": g["hgrn_lower_bounds"],
           "mixg": g["mix_norm_g_2"], "mu": g["rw_mu_2"], "w0": g["rw_w0_2"], "a0": g["rw_a0_2"],
           "kk": g["rw_k_k_2"], "ka": g["rw_k_a_2"], "rk": g["rw_r_k_2"], "gnw": g["rw_gn_w_2"],
           "gnb": g["rw_gn_b_2"], "gqa": g["mla_g_qa_2"], "gkva": g["mla_g_kva_2"],
           "ffg": g["ffn_norm_g_2"], "fing": g["final_norm_g_2"]}
    Vv = np.zeros((128, NV), np.float32)
    for k, x in vec.items():
        o, w = VO[k]
        Vv[:, o:o + w] = cols(x)
    a["vecs"] = Vv
    return a


def kernel(**inputs):
    import concourse.bacc as _bacc
    from concourse.bass_utils import run_bass_kernel_spmd as _run

    nc = _bacc.Bacc("TRN2", target_bir_lowering=False, num_devices=1)
    arrays = layout(inputs)
    I = {k: nc.dram_tensor("in_" + k, a.shape, mybir.dt.from_np(a.dtype), kind="ExternalInput").ap()
         for k, a in arrays.items()}
    out = nc.dram_tensor("out_0", (D, S), F32, kind="ExternalOutput").ap()
    build(nc, I, out)
    r = _run(nc, [{"in_" + k: a for k, a in arrays.items()}], core_ids=[0])
    return np.ascontiguousarray(r.results[0]["out_0"].T)[None]
```

```python
from contextlib import ExitStack

import numpy as np
import concourse.bass as bass
from concourse import mybir

F32 = mybir.dt.float32
I32 = mybir.dt.int32
U8 = mybir.dt.uint8
U32 = mybir.dt.uint32
ALU = mybir.AluOpType
ACT = mybir.ActivationFunctionType
AX_X = mybir.AxisListType.X

S = 512
D = 1024
SLOT = 2048
NSLOT = 4
ARENA = 31352
BIG = 1.0e30

CO = {}
_n = 0
for _name, _w in (("ident", 128), ("ones", 128), ("ones64", 128), ("rot64", 128), ("rot32", 128),
                  ("cd", 128), ("sd", 128), ("tmask", 896), ("causal", 512), ("strict", 128),
                  ("incl", 128), ("invf64", 1), ("invf32", 1), ("iota", 32), ("io128", 128), ("tok", 4), ("tok2", 4)):
    CO[_name] = (_n, _w)
    _n += _w
NC32 = _n

VO = {}
_n = 0
for _name, _w in (("an0", 8), ("an1", 8), ("mn0", 8), ("mn1", 8), ("fn1", 8), ("lb", 8),
                  ("mixg", 8), ("mu", 14), ("w0", 4), ("a0", 4), ("kk", 4), ("ka", 4), ("rk", 4),
                  ("gnw", 4), ("gnb", 4), ("gqa", 3), ("gkva", 2), ("ffg", 8), ("fing", 8)):
    VO[_name] = (_n, _w)
    _n += _w
NV = _n


class Tok:

    def __init__(self, sem, value=None):
        self.sem, self.value, self.used = sem, value, False


class Prog:

    def __init__(self, sems):
        self.sems = sems
        self.q = {e: [] for e in sems}
        self.q["sp"] = []
        self.q["sp2"] = []
        self.fence = {}
        self.tail = {}
        self.dma_count = {}
        self.serial = False
        self.prev = None

    def last(self, e):
        return self.tail.get(e)

    def streams(self, *gens):
        ends = self.ends()
        state = [[0.0, i, g, dict(self.tail), {e: list(ends) for e in self.sems}] for i, g in enumerate(gens)]
        done = []
        while state:
            st = min(state)[:2]
            st = next(x for x in state if x[1] == st[1])
            self.tail, self.fence = st[3], st[4]
            try:
                st[0] += next(st[2])
            except StopIteration:
                state.remove(st)
                done.append(st)
            st[3], st[4] = self.tail, self.fence
        ends = [t for st in done for t in st[3].values()]
        self.tail = done[-1][3]
        self.fence = {e: list(ends) for e in self.sems}

    def ends(self):
        return [self.tail[e] for e in ("pe", "act", "dve", "pool") if e in self.tail]

    def op(self, e, fn, after=()):
        need = [t for t in flat(after) if t is not None]
        if self.serial and self.prev is not None:
            need.append(self.prev)
        elif e in ("act", "dve", "pool") and e in self.tail:
            need.append(self.tail[e])
        need += self.fence.pop(e, [])
        t = Tok(e)
        self.q[e].append((fn, need, t))
        self.prev = t
        self.tail[e] = t
        return t

    def dma(self, e, out, in_, sem, after=()):
        self.dma_count[sem] = self.dma_count.get(sem, 0) + 16
        t = Tok(sem, self.dma_count[sem])
        self.q[e].append((lambda eng: eng.dma_start(out, in_), [x for x in flat(after) if x is not None], t))
        return t

    def swdge(self, fn, sem, after):
        self.dma_count[sem] = self.dma_count.get(sem, 0) + 16
        e = "pool2" if self.serial else "pool"
        need = [x for x in flat(after) if x is not None]
        if self.serial and self.prev is not None:
            need.append(self.prev)
        else:
            need += [self.tail[e]] if e in self.tail else []
            need += self.fence.pop(e, [])
        t = Tok(sem, self.dma_count[sem])
        self.q[e].append((fn, need, t))
        self.prev = t
        return t

    def section(self, other, flag, after):
        end = other.prev
        for e in ("pe", "act", "dve", "pool", "sp"):
            self.q[e].append((("section", other, flag, end), list(after), Tok("none", 0)))
            self.fence.pop(e, None)
            self.tail.pop(e, None)

    def fence_all(self):
        return self.fence.get("pe", [])

    def barrier(self):
        ends = self.ends()
        for e in ("pe", "act", "dve", "pool"):
            self.fence[e] = list(ends)
        return ends

    def settle(self):
        for e in self.q:
            for _, need, _ in self.q[e]:
                for t in need:
                    t.used = True
        if self.prev is not None:
            self.prev.used = True
        for e in self.q:
            for fn, _, _ in self.q[e]:
                if type(fn) is tuple:
                    fn[1].settle()
        for e in self.sems:
            n = 0
            for _, _, t in self.q[e]:
                if t.sem == e:
                    n += t.used
                    t.value = n

    def run(self, e, eng, sem_of):
        seen = {}
        for fn, need, t in self.q[e]:
            most = {}
            for x in need:
                most[x.sem] = max(most.get(x.sem, 0), x.value)
            for s, v in most.items():
                if seen.get(s, 0) < v:
                    eng.wait_ge(sem_of(s), v)
                    seen[s] = v
            if type(fn) is tuple:
                _, other, flag, end = fn
                many = eng.value_load(flag, min_val=0, max_val=7)
                with eng.If(many > 0):
                    other.run(e + "2", eng, sem_of)
                    eng.wait_ge(sem_of(end.sem), end.value)
                continue
            ins = fn(eng)
            if t.sem != e:
                ins.then_inc(sem_of(t.sem), 16)
            elif t.used:
                ins.then_inc(sem_of(t.sem), 1)


def flat(x):
    if x is None or isinstance(x, Tok):
        return [x]
    out = []
    for y in x:
        out += flat(y)
    return out


class Room:

    def __init__(self, ap, sem=None):
        self.ap, self.sem, self._free, self.busy = ap, sem, [], False

    @property
    def free(self):
        return self._free

    @free.setter
    def free(self, tokens):
        self._free, self.busy = tokens, False


def bcast(ap, axis, n):
    a = ap.unsqueeze(axis)
    shape = list(a.shape)
    shape[axis] = n
    return a.broadcast_to(shape)


def build(nc, I, out, stop=None, dumps=None):
    ctx = ExitStack()
    with ctx:
        def sb(name, n, dt=F32):
            return ctx.enter_context(nc.sbuf_tensor(name, [128, n], dt))

        semh = {}

        def sem_of(s):
            if s not in semh:
                raise KeyError(s)
            return semh[s]

        for s in ["pe", "act", "dve", "pool", "const", "out"] + [f"ring{i}" for i in range(NSLOT)] + [
                "pe2", "act2", "dve2", "pool2", "hd", "o", "g0", "g1", "g2", "y0", "y1", "y2", "Y0", "Y1", "Y2", "Y3"]:
            semh[s] = ctx.enter_context(nc.semaphore("s_" + s))
        P = Prog(["pe", "act", "dve", "pool"])

        C = sb("C", NC32)
        V = sb("V", NV)
        M8 = sb("M8", 14 * 512, U8)
        X = sb("X", 8 * S)
        H = sb("H", 8 * S)
        ring = sb("ring", NSLOT * SLOT)
        A = sb("A", ARENA)
        small = sb("small", 384)
        hdram = nc.dram_tensor("h_rows", (S, D), F32).ap()
        ydram = nc.dram_tensor("y_rows", (2 * S, D), F32).ap()
        psum = ctx.enter_context(nc.psum_tensor("psum", [128, 8, 512], F32))

        def c(name):
            o, w = CO[name]
            return C[:, o:o + w]

        def v(name, i=0, n=1):
            o, w = VO[name]
            return V[:, o + i:o + i + n]

        slots = [Room(ring[:, i * SLOT:(i + 1) * SLOT], f"ring{i}") for i in range(NSLOT)]
        banks = [Room(psum[:, i, :]) for i in range(8)]
        turn = {"slot": 0, "bank": 0}
        held = set()

        def load(src):
            for _ in range(NSLOT):
                s = slots[turn["slot"] % NSLOT]
                turn["slot"] += 1
                if not s.busy:
                    break
            assert not s.busy
            s.busy = True
            t = P.dma("sp", s.ap[:, 0:src.shape[-1]], src, s.sem, s.free)
            return s, t

        def bank(hold=False):
            for _ in range(9):
                i = turn["bank"] % 8
                turn["bank"] += 1
                if i not in held and not banks[i].busy:
                    break
            assert i not in held and not banks[i].busy
            banks[i].busy = not hold
            if hold:
                held.add(i)
            return banks[i]

        def release(b):
            held.discard(banks.index(b))

        def mm(o, l, r, start=True, stop=True, after=()):
            return P.op("pe", lambda e: e.matmul(o, l, r, start=start, stop=stop), after)

        def tr(o, i, after=()):
            return P.op("pe", lambda e: e.matmul(o, i, c("ident")[0:i.shape[0], 0:i.shape[0]], is_transpose=True,
                                                 start=True, stop=True), after)

        def act(o, i, f, scale=1.0, bias=None, accum=None, after=()):
            kw = {}
            if bias is not None:
                kw["bias"] = bias
            if accum is not None:
                kw["accum_out"] = accum
            return P.op("act", lambda e: e.activation(o, i, f, scale=scale, **kw), after)

        def tt(e, o, a, b, op, after=()):
            return P.op(e, lambda g: g.tensor_tensor(o, a, b, op), after)

        def ts(e, o, a, s1, s2, op0, op1=None, after=()):
            if op1 is None:
                return P.op(e, lambda g: g.tensor_scalar(o, a, s1, None, op0), after)
            return P.op(e, lambda g: g.tensor_scalar(o, a, s1, s2, op0, op1), after)

        def stt(o, a, s, b, op0, op1, after=()):
            return P.op("dve", lambda g: g.scalar_tensor_tensor(o, a, s, b, op0, op1), after)

        def cp(e, o, a, after=()):
            if e == "act":
                return act(o, a, ACT.Copy, after=after)
            return P.op(e, lambda g: g.tensor_copy(o, a), after)

        def setv(e, o, x, after=()):
            return P.op(e, lambda g: g.memset(o, x), after)

        class Arena:
            def __init__(self, lo, hi):
                self.at, self.hi = lo, hi

            def take(self, n):
                assert self.at + n <= self.hi, (self.at, n, self.hi)
                a = A[:, self.at:self.at + n]
                self.at += n
                return a

        def t3(ap, n):
            return ap.rearrange("p (a b) -> p a b", a=n)

        Xt, Ht = t3(X[:, :], 8), t3(H[:, :], 8)

        t_const = [P.dma("act", C[:, :], I["c32"], "const"), P.dma("act", V[:, :], I["vecs"], "const"),
                   P.dma("act", A[:, 0:1792], I["m32"], "const")]
        for kt in range(8):
            t_const.append(P.dma("act", Xt[:, kt, :], I["x"][kt], "const"))
        t_const = t_const[-1]
        consts_at = t_const
        for e in ("pe", "act", "dve", "pool"):
            P.fence[e] = [t_const]
        eps = small[:, 0:1]
        halfpi = small[:, 1:2]
        gneps = small[:, 2:3]
        one_row = small[:, 3:4]
        cp("dve", M8[:, :].rearrange("p (l c t) -> p l c t", l=14, c=4),
           bcast(A[:, 0:1792].rearrange("p (l t) -> p l t", l=14), 2, 4))
        setv("pool", eps, 1e-6)
        setv("pool", gneps, 64e-5)
        setv("pool", one_row, 1.0)
        P.barrier()

        def rms(dst, src, nt, width, wname, scratch, rs, after=()):
            b = bank()
            t = None
            for i in range(nt):
                q = scratch[:, (i % 2) * S:(i % 2 + 1) * S]
                ta = act(q, src[:, i, :], ACT.Square, after=(after, t_mm[i - 2] if i >= 2 else None))
                if i == 0:
                    t_mm = []
                t_mm.append(mm(b.ap, c("ones"), q, i == 0, i == nt - 1, after=(ta, b.free if i == 0 else ())))
            ta = act(rs, b.ap, ACT.Sqrt, scale=1.0 / width, bias=eps, after=t_mm[-1])
            b.free = [ta]
            t = P.op("dve", lambda g: g.reciprocal(rs, rs), ta)
            for i in range(nt):
                t = stt(dst[:, i, :], src[:, i, :], v(wname, i), rs, ALU.mult, ALU.mult, after=after)
            return t

        def lin(chunks, act_of, nc_, kts, evac, after=()):
            per = nc_ // 128
            bs = [bank() for _ in range(per)]
            for j, src in enumerate(chunks):
                s, tl = load(src)
                for m in range(per):
                    for kt in range(kts):
                        t = mm(bs[m].ap, s.ap[:, kt * nc_ + m * 128:kt * nc_ + (m + 1) * 128], act_of(j * kts + kt),
                               j == 0 and kt == 0, j == len(chunks) - 1 and kt == kts - 1,
                               after=(tl, after, bs[m].free if j == 0 and kt == 0 else ()))
                s.free = [t]
                if j < len(chunks) - 1:
                    continue
                for m in range(per):
                    bs[m].free = [evac(m, bs[m].ap, t)]

        def lin_tok(s, tl, off, width, kts, nc_, act_of, dst, eng, after=()):
            for tk in range(4):
                b = bank()
                for kt in range(kts):
                    t = mm(b.ap[:, 0:width], act_of(kt)[:, tk * 128:(tk + 1) * 128],
                           s.ap[:, kt * nc_ + off:kt * nc_ + off + width], kt == 0, kt == kts - 1,
                           after=(tl, after, b.free if kt == 0 else ()))
                b.free = [cp(eng, dst[:, tk, :], b.ap[:, 0:width], after=t)]
            return t, b.free

        def tables(pos, invf, cosT, sinT, ar):
            pi = ar.take(S)
            ang, n, r = ar.take(S), ar.take(S), ar.take(S)
            tp = P.dma("act", pi.bitcast(I32), pos.partition_broadcast(128), "const", after=P.barrier())
            cp("dve", ang, pi.bitcast(I32), after=tp)
            ts("dve", ang, ang, invf, None, ALU.mult)
            MAG = 12582912.0
            for dst, q in ((sinT, 0.0), (cosT, 0.25)):
                ts("dve", n, ang, float(1 / (2 * np.pi)), float(q), ALU.mult, ALU.add)
                ts("dve", n, n, MAG, None, ALU.add)
                ts("dve", n, n, MAG, None, ALU.subtract)
                C1 = 6.28125
                C2 = float(np.float32(2 * np.pi - C1))
                C2 = float(np.float32(np.round(C2 * 2 ** 20) / 2 ** 20))
                C3 = float(2 * np.pi - C1 - C2)
                stt(r, n, -C1, ang, ALU.mult, ALU.add)
                stt(r, n, -C2, r, ALU.mult, ALU.add)
                stt(r, n, -C3, r, ALU.mult, ALU.add)
                if q:
                    ts("dve", r, r, float(np.pi / 2), None, ALU.add)
                t = ts("dve", r, r, 3.1415925, -3.1415925, ALU.min, ALU.max)
                t2 = act(dst, r, ACT.Sin, after=t)
                P.fence["dve"] = [t2]
            return t2

        def attention(ar, nh, scores, mask_of, klen, vtok, dst_evac, spare=()):
            NS = 4
            Sb = list(spare) + [ar.take(S) for _ in range(NS - len(spare))]
            PT = [t3(ar.take(4 * S), 4) for _ in range(2)]
            ms, rs_, ris = (ar.take(32) for _ in range(3))
            t_max, t_exp, t_nrm, t_tr, t_pt, t_pv = {}, {}, {}, {}, {}, {}
            out_ = {}

            def col(x, i):
                return x[:, i % 32:i % 32 + 1]

            def first(i):
                h, qt = divmod(i, 4)
                kl = klen(qt)
                b = bank()
                t = scores(h, b.ap[:, 0:kl], qt, kl, b.free)
                t = mask_of(b.ap, Sb[i % NS][:, 0:kl], col(ms, i), qt, kl, (t, t_tr.get(i - NS)))
                b.free = [t]
                t_exp[i] = act(Sb[i % NS][:, 0:kl], Sb[i % NS][:, 0:kl], ACT.Exp, scale=-1.0, bias=col(ms, i),
                               accum=col(rs_, i), after=t)

            def second(i):
                kl = klen(i % 4)
                x = Sb[i % NS][:, 0:kl]
                ri, r_ = col(ris, i), col(rs_, i)
                P.op("dve", lambda g: g.reciprocal(ri, r_), t_exp[i])
                t_nrm[i] = ts("dve", x, x, ri, None, ALU.mult)

            def third(i):
                h, qt = divmod(i, 4)
                n = klen(qt) // 128
                x = Sb[i % NS]
                b = bank()
                for k in range(n):
                    t = tr(b.ap[:, k * 128:(k + 1) * 128], x[:, k * 128:(k + 1) * 128], after=(t_nrm[i], b.free))
                t_tr[i] = t
                t_pt[i] = cp("act" if qt % 2 else "dve", PT[h % 2][:, 0:n, qt * 128:(qt + 1) * 128],
                             t3(b.ap[:, 0:n * 128], n), after=(t, t_pv.get(h - 2)))
                b.free = [t_pt[i]]

            def values(h):
                if h % 2 == 0:
                    out_[0] = bank(hold=True)
                bo = out_[0]
                o = bo.ap[64 * (h % 2):64 * (h % 2) + 64, :]
                for k in range(4):
                    q0 = min(q for q in range(4) if klen(q) > k * 128)
                    t = mm(o[:, q0 * 128:S], vtok(h, k), PT[h % 2][:, k, q0 * 128:S], k == 0, k == 3,
                           after=([t_pt[4 * h + q] for q in range(4)], bo.free if k == 0 and h % 2 == 0 else ()))
                t_pv[h] = t
                if h % 2:
                    bo.free = [dst_evac(h // 2, bo.ap, t)]
                    release(bo)

            n = 4 * nh
            for i in range(n + 4):
                if i < n:
                    first(i)
                if 1 <= i <= n:
                    second(i - 1)
                if 2 <= i < n + 2:
                    third(i - 2)
                if i >= 6 and (i - 6) % 4 == 0 or i == n + 3:
                    h = (i - 6) // 4 if i < n + 3 else nh - 1
                    if h not in t_pv and h < nh:
                        values(h)
                yield 2.3

        tabs = Arena(0, 1024)
        cos64, sin64 = tabs.take(S), tabs.take(S)
        tables(I["pos1"], c("invf64"), cos64, sin64, Arena(1024, 3072))
        P.barrier()

        lbv = t3(v("lb", 0, 8), 2)
        lm, le0, le1, ls = (small[:, 112 + 4 * i:116 + 4 * i] for i in range(4))
        lbs = [small[:, 128:132], small[:, 132:136]]
        oml = [small[:, 136:140], small[:, 140:144]]
        tt("dve", lm, lbv[:, 0, :], lbv[:, 1, :], ALU.max)
        tt("dve", le0, lbv[:, 0, :], lm, ALU.subtract)
        t = tt("dve", le1, lbv[:, 1, :], lm, ALU.subtract)
        act(le0, le0, ACT.Exp, after=t)
        t = act(le1, le1, ACT.Exp)
        tt("dve", ls, le0, le1, ALU.add, after=t)
        P.op("dve", lambda g: g.reciprocal(ls, ls))
        tt("dve", le0, le0, ls, ALU.mult)
        tt("dve", le1, le1, ls, ALU.mult)
        tt("dve", lbs[0], le0, le0, ALU.subtract)
        tt("dve", lbs[1], le0, le1, ALU.add)
        tt("dve", lbs[1], lbs[1], le0, ALU.subtract)
        for i in range(2):
            ts("dve", oml[i], lbs[i], -1.0, 1.0, ALU.mult, ALU.add)
        P.barrier()

        for layer in range(2):
            ar = Arena(1024, ARENA)
            scratch, rs = ar.take(2 * S), ar.take(S)
            t_h = rms(Ht, Xt, 8, D, f"an{layer}", scratch, rs)
            if stop == f"norm{layer}":
                break
            aq, ai, k2 = ar.take(2 * S), ar.take(4 * 256), ar.take(4 * S)
            ag, L, oc = ar.take(2 * S), ar.take(4 * S), None
            u, cq, ck, cv = ar.take(4 * 256), ar.take(4 * S), ar.take(4 * S), ar.take(4 * S)
            aq3, k3, L3, ag3 = t3(aq, 2), t3(k2, 4), t3(L, 4), t3(ag, 2)
            ai3, u3, cq3, ck3, cv3 = t3(ai, 4), t3(u, 4), t3(cq, 4), t3(ck, 4), t3(cv, 4)
            W = I["w_in"][layer]
            h_of = lambda kt: Ht[:, kt, :]
            tmp_at = ar.at
            sg = [scratch[:, 0:S], scratch[:, S:2 * S]]
            sgt = [[], []]

            def ev_silu(dst):
                def f(m, ps, t):
                    ta = act(sg[m], ps, ACT.Sigmoid, after=(t, sgt[m]))
                    t = tt("dve", dst[:, m, :], ps, sg[m], ALU.mult, after=ta)
                    sgt[m] = [t]
                    return t
                return f

            def ev_gate(dr):
                def f(m, ps, t):
                    j = dr * 2 + m
                    ta = act(sg[m], ps, ACT.Sigmoid, after=(t, sgt[m]))
                    ts("dve", sg[m], sg[m], oml[layer][:, j:j + 1], lbs[layer][:, j:j + 1], ALU.mult, ALU.add,
                       after=ta)
                    ts("dve", k3[:, j, :], sg[m], -1.0, 1.0, ALU.mult, ALU.add)
                    t = ts("dve", L3[:, j, :], sg[m], 2.0 ** -63, None, ALU.max)
                    sgt[m] = [t]
                    return ta
                return f

            for dr in range(2):
                lin([W[2 + dr, 0]], h_of, 256, 8, ev_gate(dr), after=t_h)
            lin([W[0, 0]], h_of, 256, 8, ev_silu(aq3))
            lin([W[4, 0]], h_of, 256, 8, ev_silu(ag3))
            s, tl = load(W[1, 0])
            t, t_ai = lin_tok(s, tl, 0, 256, 8, 256, h_of, ai3, "act")
            s.free = [t]
            s, tl = load(W[5, 0])
            t, t_u = lin_tok(s, tl, 0, 256, 8, 256, h_of, u3, "act")
            s.free = [t]

            def ev_copy(dst, base):
                return lambda m, ps, t: cp("act", dst[:, base + m, :], ps, after=t)

            oab = ar.take(2 * S)

            def recurrence():
                act(L, L, ACT.Ln, after=P.last("dve"))
                B = ar.take(4 * 516)
                B3 = B.rearrange("p (g j) -> p g j", j=129)
                E, Kls, Qls = L[:, 0:2 * S], (L[:, 2 * S:4 * S], ar.take(2 * S)), (ar.take(S), ar.take(S))
                Kt, Sc = ar.take(2 * S), ar.take(4 * S)
                St, dec = ar.take(4 * 2 * 64), small[:, 160:168]
                setv("pool", B3[:, :, 0:1], 0.0)
                ones_b = c("ones")
                t_b = (P.last("pool"), P.last("act"))
                for g in range(16):
                    j, ch = g // 4, g % 4
                    t_b = P.op("dve", lambda e, g=g, j=j, ch=ch, B3=B3, L3=L3: e.tensor_tensor_scan(
                        B3[:, g, 1:129], ones_b, L3[:, j, ch * 128:(ch + 1) * 128], 0.0, ALU.mult, ALU.add), after=t_b)
                yield 12.0
                P.barrier()
                q8 = aq.rearrange("p (g t) -> p g t", t=128)
                E8 = E.rearrange("p (g t) -> p g t", t=128)
                ob = [bank(hold=True) for _ in range(2)]
                t_o = None
                for dr in range(2):
                    k8 = k2[:, dr * 2 * S:(dr + 1) * 2 * S].rearrange("p (g t) -> p g t", t=128)
                    Bd = B3[:, dr * 8:dr * 8 + 8, :]
                    sh = 1 - dr
                    ml = lambda l: M8[:, (dr * 7 + l) * 512:(dr * 7 + l + 1) * 512]

                    def halves(ap, l, second, lo=0):
                        w = 2 ** l
                        return ap[:, :, lo:lo + 128].rearrange("p g (n two w) -> p g n two w", two=2, w=w)[
                            :, :, :, 1 if second else 0, :]

                    def decayed(l):
                        w = 2 ** l
                        K_, Q_ = Kls[l % 2], Qls[l % 2]
                        mid = Bd[:, :, w:w + 128 - 2 * w + 1:2 * w] if l < 6 else Bd[:, :, 64:65]
                        mid = bcast(mid, 3, w)
                        tt("dve", halves(E8, l, False), mid, halves(Bd, l, False, sh), ALU.subtract,
                           after=P.last("pool"))
                        t = tt("dve", halves(E8, l, True), halves(Bd, l, True, sh), mid, ALU.subtract)
                        t_e = act(E, E, ACT.Exp, after=t)
                        t_k = tt("pool", K_, E, k2[:, dr * 2 * S:(dr + 1) * 2 * S], ALU.mult,
                                 after=(t_e, t_use.get(l - 2)))
                        t_q = tt("dve", Q_.rearrange("p (g n w) -> p g n w", g=8, w=w), halves(q8, l, dr == 0),
                                 halves(E8, l, dr == 0), ALU.mult, after=(t_e, t_use.get(l - 2)))
                        return t_k, t_q

                    t_use = {-2: t_o, -1: t_o}
                    ready = {-1: t_b}
                    for l in range(-1, 7):
                        if l < 6:
                            ready[l + 1] = decayed(l + 1)
                            yield 5.0
                        n = 64 if l >= 0 else 128
                        for h in range(4):
                            hp, lo = h // 2, 64 * (h % 2)
                            b = bank()
                            for ch in range(4):
                                if l >= 0:
                                    kk = Kls[l % 2][lo:lo + 64, (hp * 4 + ch) * 128:(hp * 4 + ch + 1) * 128]
                                    qq = Qls[l % 2][lo:lo + 64, (hp * 4 + ch) * 64:(hp * 4 + ch + 1) * 64]
                                else:
                                    kk, qq = k8[lo:lo + 64, hp * 4 + ch, :], q8[lo:lo + 64, hp * 4 + ch, :]
                                t = mm(b.ap[:, ch * n:(ch + 1) * n], kk, qq, after=(ready[l], b.free))
                            if l < 0:
                                t = tt("dve", t3(Sc[:, h * S:(h + 1) * S], 4), t3(b.ap, 4),
                                       bcast(c("ident"), 1, 4), ALU.mult, after=(t, t_o))
                            else:
                                w = 2 ** l
                                f = lambda ap: ap.rearrange("p (n two w) -> p n two w", two=2, w=w)[
                                    :, :, 1 if dr == 0 else 0, :]
                                o_, m_ = f(Sc[:, h * S:(h + 1) * S]), f(ml(l))
                                d_ = b.ap[:, 0:256].rearrange("p (n w) -> p n w", w=w)
                                t = P.op("dve", lambda g, o_=o_, m_=m_, d_=d_: g.copy_predicated(o_, m_, d_), t)
                            b.free = [t]
                        t_use[l] = P.last("pe")
                        yield 4.0
                    t_o = P.last("pe")
                    Kl, Kl8 = Kls[1], Kls[1].rearrange("p (g t) -> p g t", t=128)
                    t_sc = P.last("dve")
                    tot = bcast(Bd[:, :, 128:129].squeeze(2), 2, 128)
                    fl = (Bd[:, :, 1:129], Bd[:, :, 0:128])
                    if dr == 0:
                        t = tt("dve", E8, tot, fl[0], ALU.subtract)
                        t_e = act(E, E, ACT.Exp, after=t)
                    else:
                        t_e = act(E8, fl[1], ACT.Exp, after=P.last("dve"))
                    t_k = tt("pool", Kl, E, k2[:, dr * 2 * S:(dr + 1) * 2 * S], ALU.mult, after=(t_e, t_o))
                    t_dec = act(dec, Bd[:, :, 128:129].squeeze(2), ACT.Exp)
                    if dr == 0:
                        t_e = act(E8, fl[0], ACT.Exp, after=t_k)
                    else:
                        t = tt("dve", E8, tot, fl[1], ALU.subtract, after=t_k)
                        t_e = act(E, E, ACT.Exp, after=t)
                    t_q = tt("dve", E, E, aq, ALU.mult, after=t_e)
                    yield 5.0
                    for hp in range(2):
                        b = bank()
                        for ch in range(4):
                            t = tr(b.ap[:, ch * 128:(ch + 1) * 128], Kl8[:, hp * 4 + ch, :], after=(t_k, b.free))
                        b.free = [cp("act", Kt.rearrange("p (c a f) -> p a c f", c=4, a=2)[:, hp], t3(b.ap, 4), after=t)]
                    t_kt = P.last("act")
                    St4 = St.rearrange("p (c a f) -> p c a f", c=4, a=2)
                    order = [0, 1, 2, 3] if dr == 0 else [3, 2, 1, 0]
                    b = bank()
                    for ch in order[:3]:
                        for h in range(4):
                            hp, lo = h // 2, 64 * (h % 2)
                            t = mm(b.ap[lo:lo + 64, (ch * 2 + hp) * 64:(ch * 2 + hp + 1) * 64],
                                   Kt[:, (ch * 2 + hp) * 128 + lo:(ch * 2 + hp) * 128 + lo + 64],
                                   ai3[:, ch, h * 64:(h + 1) * 64], after=(t_kt, b.free))
                    bs = b.ap.rearrange("p (c a f) -> p c a f", c=4, a=2)
                    t = cp("dve", St4[:, order[1]], bs[:, order[0]], after=(t, t_dec))
                    for i in (1, 2):
                        for hp in range(2):
                            t = stt(St4[:, order[i + 1], hp, :], St4[:, order[i], hp, :],
                                    dec[:, hp * 4 + order[i]:hp * 4 + order[i] + 1], bs[:, order[i], hp, :],
                                    ALU.mult, ALU.add)
                    b.free = [t]
                    t_st = t
                    yield 3.0
                    for hp in range(2):
                        for hh in range(2):
                            h, lo = hp * 2 + hh, 64 * hh
                            for ch in range(4):
                                cs = slice(ch * 128, (ch + 1) * 128)
                                inter = ch != order[0]
                                o_ = ob[hp].ap[lo:lo + 64, cs]
                                t = mm(o_, ai3[:, ch, h * 64:(h + 1) * 64],
                                       Sc[:, h * S + ch * 128:h * S + (ch + 1) * 128], True, not inter,
                                       after=(t_sc, t_st, t_q, ob[hp].free))
                                if inter:
                                    t = mm(o_, St4[lo:lo + 64, ch, hp, :], E8[lo:lo + 64, hp * 4 + ch, :], False, True)
                    t_o = t
                    if dr == 0:
                        ar_o = [oab[:, 0:S], oab[:, S:2 * S]]
                        for hp in range(2):
                            ob[hp].free = [cp("act", ar_o[hp], ob[hp].ap, after=t)]
                    else:
                        for hp in range(2):
                            t = tt("dve", ar_o[hp], ar_o[hp], ob[hp].ap, ALU.add, after=t_o)
                            ob[hp].free = [t]
                            release(ob[hp])
                    P.barrier()
                    yield 4.0
                for hp in range(2):
                    sq, r_ = E[:, 0:S], E[:, S:2 * S]
                    t = act(sq, ar_o[hp], ACT.Square, after=P.last("dve"))
                    b = bank()
                    t = mm(b.ap, c("ones64"), sq, after=(t, b.free))
                    t = act(r_, b.ap, ACT.Sqrt, scale=1.0 / 64, bias=eps, after=t)
                    b.free = [t]
                    P.op("dve", lambda g, r_=r_: g.reciprocal(r_, r_), t)
                    tt("dve", r_, r_, ar_o[hp], ALU.mult)
                    t = tt("dve", ar_o[hp], r_, ag3[:, hp, :], ALU.mult)
                    P.fence["act"] = [t]
                P.barrier()


            def windows():
                for j in range(2):
                    lin([W[6 + j, 0]], h_of, 256, 8, ev_copy(cq3, 2 * j))
                    yield 13.6
                for j in range(2):
                    lin([W[8 + j, 0]], h_of, 256, 8, ev_copy(ck3, 2 * j))
                    yield 13.6
                for j in range(2):
                    s, tl = load(W[10 + j, 0])
                    t, t_cv = lin_tok(s, tl, 0, 256, 8, 256, h_of, cv3[:, :, 256 * j:256 * j + 256], "act")
                    s.free = [t]
                    yield 13.6
                w_at = ar.at
                bre, bim = [bank() for _ in range(2)], [bank() for _ in range(2)]
                us = [ar.take(S) for _ in range(4)]
                for part, bs in ((0, bre), (1, bim)):
                    s, tl = load(I["dft"][part])
                    for dt_ in range(2):
                        for k in range(4):
                            t = mm(bs[dt_].ap, u3[:, k, dt_ * 128:(dt_ + 1) * 128], s.ap[:, k * S:(k + 1) * S],
                                   k == 0, k == 3, after=(tl, bs[dt_].free))
                        bs[dt_].free = [cp("act", us[part * 2 + dt_], bs[dt_].ap, after=t)]
                    s.free = [t]
                    yield 7.0
                for dt_ in range(2):
                    b = bank()
                    mm(b.ap, c("cd"), us[dt_], True, False, after=(bre[dt_].free, b.free))
                    t = mm(b.ap, c("sd"), us[2 + dt_], False, True, after=bim[dt_].free)
                    b.free = [cp("act", Ht[:, 2 + dt_, :], b.ap, after=t)]
                P.barrier()
                ar.at = w_at
                rt = [ar.take(S) for _ in range(2)]
                rtt = [[], []]
                n = 0
                for src in (cq3, ck3):
                    for m in range(4):
                        b = bank()
                        t = mm(b.ap, c("rot64"), src[:, m, :], after=b.free)
                        t = tt("dve", rt[n % 2], b.ap, sin64, ALU.mult, after=(t, rtt[n % 2]))
                        b.free = [t]
                        t2 = tt("pool", src[:, m, :], src[:, m, :], cos64, ALU.mult, after=P.last("pe"))
                        t = tt("dve", src[:, m, :], src[:, m, :], rt[n % 2], ALU.add, after=t2)
                        n += 1
                    yield 6.0
                t_rot = P.last("dve")
                P.barrier()
                ar.at = w_at

                def scores(h, o, qt, kl, after):
                    hp, lo = h // 2, 64 * (h % 2)
                    return mm(o, cq3[lo:lo + 64, hp, qt * 128:(qt + 1) * 128], ck3[lo:lo + 64, hp, :],
                              after=(after, t_rot))

                def mask(ps, Sb, m, qt, kl, after):
                    tm = c("tmask")[:, (3 - qt) * 128:(3 - qt) * 128 + S]
                    return P.op("dve", lambda g: g.tensor_tensor_reduce(
                        Sb, ps[:, 0:kl], tm, -0.125, 3.0e38, ALU.add, ALU.min, m), after)

                yield from attention(ar, 8, scores, mask, lambda qt: S, lambda h, k: cv3[:, k, h * 64:(h + 1) * 64],
                                     lambda hp, ps, t: cp("act", Ht[:, 4 + hp, :], ps, after=t), (u[:, 0:S], u[:, S:2 * S]))

            P.streams(recurrence(), windows())
            for hp in range(2):
                t = cp("dve", Ht[:, hp, :], oab[:, hp * S:(hp + 1) * S])
            P.barrier()
            if stop == f"mix{layer}":
                break

            def ev_res(mt):
                return lambda m, ps, t: tt("dve", Xt[:, 2 * mt + m, :], Xt[:, 2 * mt + m, :], ps, ALU.add, after=t)

            for j in range(4):
                lin([I["w_out"][layer][j, 0]], h_of, 256, 8, ev_res(j))
            P.barrier()
            if stop == f"res{layer}":
                break

            ar = Arena(1024, ARENA)
            scratch, rs = ar.take(2 * S), ar.take(S)
            hid = t3(ar.take(32 * S), 32)
            rl = [ar.take(S) for _ in range(2)]
            rlt = [[], []]
            t_h = rms(Ht, Xt, 8, D, f"mn{layer}", scratch, rs)

            def ev_hid(j):
                def f(m, ps, t):
                    ta = act(rl[m], ps, ACT.Relu, after=(t, rlt[m]))
                    t = tt("dve", hid[:, 2 * j + m, :], rl[m], rl[m], ALU.mult, after=ta)
                    rlt[m] = [t]
                    return ta
                return f

            for j in range(16):
                lin([I["w_up"][layer][j, 0]], h_of, 256, 8, ev_hid(j), after=t_h)
            t_hid = P.last("dve")
            for j in range(4):
                lin([I["w_down"][layer][j, k] for k in range(4)], lambda kt: hid[:, kt, :], 256, 8, ev_res(j),
                    after=t_hid)
            P.barrier()
            if stop == f"ffn{layer}":
                break
        else:
            ar = Arena(1024, ARENA)
            rms(Xt, Xt, 8, D, "fn1", ar.take(2 * S), ar.take(S))
            P.barrier()
            if stop != "b1":
                second = True
                tabs = Arena(0, 1024)
                cos32, sin32 = tabs.take(S), tabs.take(S)
                tables(I["pos2"], c("invf32"), cos32, sin32, Arena(1024, 3072))
                P.barrier()
                ar = Arena(1024, ARENA)
                yrw, ymla = t3(ar.take(4 * S), 4), None
                rw_at = ar.at
                scratch, rs = ar.take(2 * S), ar.take(S)
                t_h = rms(Ht, Xt, 8, D, "mixg", scratch, rs)
                P.barrier()
                ar.at = rw_at
                h_of = lambda kt: Ht[:, kt, :]
                W2 = I["w_in2"]

                sgd = ar.take(S)
                Z = t3(ar.take(12 * S), 12)
                zr, zk, zv = Z[:, 0:4], Z[:, 4:8], Z[:, 8:12]
                aa, kkv = t3(ar.take(4 * S), 4), t3(ar.take(4 * S), 4)
                keep_at = ar.at
                cb = [ar.take(S + 1) for _ in range(2)]
                df = [ar.take(S) for _ in range(2)]
                zwa = ar.take(S)
                for m in range(2):
                    setv("pool", cb[m][:, 0:1], 0.0)
                t_z0 = P.last("pool")
                cbt = [[], []]

                def ev_shift(j):
                    def f(m, ps, t):
                        i = 2 * j + m
                        dst = Z[:, i, :] if i < 12 else (zwa if i == 12 else sgd)
                        ta = cp("act", cb[m][:, 1:S + 1], ps, after=(t, cbt[m]))
                        tt("dve", df[m], cb[m][:, 0:S], cb[m][:, 1:S + 1], ALU.subtract, after=(ta, t_z0))
                        t = stt(dst, df[m], v("mu", i), cb[m][:, 1:S + 1], ALU.mult, ALU.add)
                        cbt[m] = [t]
                        return ta
                    return f

                for j in range(7):
                    lin([W2[j, 0]], h_of, 256, 8, ev_shift(j))
                t_z = P.last("dve")
                act(zwa[0:64, :], zwa[0:64, :], ACT.Tanh, after=t_z)
                t_wa = act(sgd, sgd, ACT.Sigmoid)
                Bw = ar.take(4 * 516)
                E1, E2 = ar.take(4 * 516), ar.take(4 * 516)
                sgw = [df[0], df[1]]
                B3, E13, E23 = (x.rearrange("p (g j) -> p g j", j=129) for x in (Bw, E1, E2))
                setv("pool", B3[:, :, 0:1], 0.0)
                t_b0 = P.last("pool")
                s, tl = load(I["wa_up"])
                sct = [[], []]
                for j in range(4):
                    b = bank()
                    t = mm(b.ap, s.ap[0:64, j * 128:(j + 1) * 128], zwa[0:64, :], after=(tl, t_wa, b.free))
                    ta = act(sgw[j % 2], b.ap, ACT.Sigmoid, bias=v("w0", j), after=(t, sct[j % 2]))
                    b.free = [ta]
                    for ch in range(4):
                        t = P.op("dve", lambda e, j=j, ch=ch: e.tensor_tensor_scan(
                            B3[:, j * 4 + ch, 1:129], c("ones"), sgw[j % 2][:, ch * 128:(ch + 1) * 128], 0.0,
                            ALU.mult, ALU.add), after=(ta, t_b0))
                    sct[j % 2] = [t]
                for j in range(4):
                    b = bank()
                    t = mm(b.ap, s.ap[64:128, j * 128:(j + 1) * 128], zwa[64:128, :], after=b.free)
                    b.free = [act(aa[:, j, :], b.ap, ACT.Sigmoid, bias=v("a0", j), after=t)]
                s.free = [t]
                t_aa = P.last("act")
                for j in range(4):
                    ts("dve", kkv[:, j, :], zk[:, j, :], v("kk", j), None, ALU.mult)
                    t = tt("dve", df[0], kkv[:, j, :], kkv[:, j, :], ALU.mult, after=t_aa)
                    b = bank()
                    t = mm(b.ap, c("ones64"), df[0], after=(t, b.free))
                    t = act(df[1], b.ap, ACT.Sqrt, after=t)
                    b.free = [t]
                    ts("dve", df[1], df[1], 1e-12, None, ALU.max, after=t)
                    P.op("dve", lambda g: g.reciprocal(df[1], df[1]))
                    tt("dve", kkv[:, j, :], kkv[:, j, :], df[1], ALU.mult)
                    ts("dve", df[0], aa[:, j, :], -1.0, v("ka", j), ALU.add, ALU.mult)
                    stt(zk[:, j, :], df[0], 1.0, zk[:, j, :], ALU.add, ALU.mult)
                    stt(aa[:, j, :], kkv[:, j, :], -1.0, aa[:, j, :], ALU.mult, ALU.mult)
                LD = float(-np.exp(-0.5))
                midc = small[:, 160:176]
                cp("dve", midc, B3[:, :, 64:65].squeeze(2))
                t = tt("dve", B3, B3, bcast(midc, 2, 129), ALU.subtract)
                act(E1, Bw, ACT.Exp, scale=LD, after=t)
                t_e = act(E2, Bw, ACT.Exp, scale=-LD)
                sp = lambda x: x.rearrange("p a (c t) -> p (a c) t", c=4)
                tt("dve", sp(zr), sp(zr), E13[:, :, 1:129], ALU.mult, after=t_e)
                tt("dve", sp(kkv), sp(kkv), E13[:, :, 0:128], ALU.mult)
                tt("dve", sp(zk), sp(zk), E23[:, :, 1:129], ALU.mult)
                tt("dve", sp(aa), sp(aa), E23[:, :, 1:129], ALU.mult)
                e_in, e_out, e_all = small[:, 176:192], small[:, 192:208], small[:, 208:224]
                cp("dve", e_in, E23[:, :, 0:1].squeeze(2))
                cp("dve", e_out, E13[:, :, 128:129].squeeze(2))
                tt("dve", e_all, e_in, e_out, ALU.mult)
                P.barrier()

                ar.at = keep_at
                tok = [ar.take(S) for _ in range(3)]
                G = []
                for g in range(2):
                    G.append({n: ar.take(S) for n in ("AT", "X", "XT", "T1", "ak", "rb", "rk")})
                rhs, sa = ar.take(S), ar.take(S)
                St, S0 = ar.take(256), ar.take(256)
                St3, S03 = t3(St, 4), t3(S0, 4)
                tmp = rhs[:, 0:256]
                setv("pool", St, 0.0)
                t_s = P.last("pool")
                eq = lambda x, ch: x.rearrange("p (a c) -> p a c", c=4)[:, :, ch]
                done = []
                for ch in range(4):
                    cs = slice(ch * 128, (ch + 1) * 128)
                    for i, src in enumerate((aa, zk, zv)):
                        b = bank()
                        for j in range(4):
                            t = tr(b.ap[:, j * 128:(j + 1) * 128], src[:, j, cs], after=(b.free, done))
                        b.free = [cp("act", tok[i], b.ap, after=(t, done))]
                    t_tok = P.last("act")

                    def pairs(g, l, r, after):
                        b = bank()
                        for i in range(4):
                            j, lo = i, 64 * g
                            t = mm(b.ap[:, i * 128:(i + 1) * 128], l[lo:lo + 64, j, cs], r[lo:lo + 64, j, cs],
                                   after=(after, b.free))
                        return b, t

                    def masked(o, b, t, name, after):
                        b.free = [tt("dve", t3(o, 4), t3(b.ap, 4), bcast(c(name), 1, 4), ALU.mult, after=(t, after))]

                    def pred(o, l, ps, t):
                        return P.op("dve", lambda e: e.copy_predicated(o, M8[:, l * 512:(l + 1) * 512], ps), t)

                    for g in range(2):
                        g_ = G[g]
                        b, t = pairs(g, aa, kkv, done)
                        masked(g_["AT"], b, t, "strict", done)
                        cp("dve", t3(g_["XT"], 4), bcast(c("ident"), 1, 4))
                        pred(g_["XT"], 0, b.ap, None)
                        b.free = [P.last("dve")]
                        b, t = pairs(g, kkv, aa, done)
                        cp("dve", t3(g_["X"], 4), bcast(c("ident"), 1, 4))
                        b.free = [pred(g_["X"], 7, b.ap, t)]
                        for name, l, r, mk in (("ak", zk, kkv, "strict"), ("rb", aa, zr, "incl"), ("rk", zk, zr, "incl")):
                            b, t = pairs(g, l, r, done)
                            masked(g_[name], b, t, mk, done)
                    tx = [P.last("dve")] * 2
                    for l in range(1, 7):
                        t1 = [None, None]
                        for g in range(2):
                            g_ = G[g]
                            b = bank()
                            for i in range(4):
                                k = slice(i * 128, (i + 1) * 128)
                                t = mm(b.ap[:, k], g_["AT"][:, k], g_["X"][:, k], after=(tx[g], b.free))
                            b.free = [cp("act", g_["T1"], b.ap, after=t)]
                            t1[g] = b.free
                        for g in range(2):
                            g_ = G[g]
                            b2 = bank()
                            for i in range(4):
                                k = slice(i * 128, (i + 1) * 128)
                                t2 = mm(b2.ap[:, k], g_["T1"][:, k], g_["XT"][:, k], after=(t1[g], b2.free))
                            if l < 6:
                                b = bank()
                                for i in range(4):
                                    k = slice(i * 128, (i + 1) * 128)
                                    t = mm(b.ap[:, k], g_["XT"][:, k], g_["T1"][:, k], after=(t1[g], b.free))
                                b.free = [pred(g_["X"], 7 + l, b.ap, t)]
                            b2.free = [pred(g_["XT"], l, b2.ap, (t2, t if l < 6 else None))]
                            tx[g] = b2.free
                    t_s0 = tt("dve", S03, St3, bcast(eq(e_in, ch), 2, 64), ALU.mult, after=(t_s, done))
                    t_r = []
                    for g in range(2):
                        b = bank()
                        lo = 64 * g
                        for j in range(4):
                            h, k = 2 * j + g, slice(j * 128, j * 128 + 128)
                            o = b.ap[:, j * 64:(j + 1) * 64]
                            mm(o, G[g]["ak"][:, k], tok[2][:, h * 64:(h + 1) * 64], True, False,
                               after=(t_tok, t_s0, b.free))
                            t = mm(o, kkv[lo:lo + 64, j, cs], S03[lo:lo + 64, j, :], False, True)
                        b.free = [cp("act", rhs.rearrange("p (j g f) -> p g j f", j=4, g=2)[:, g],
                                     t3(b.ap[:, 0:256], 4), after=t)]
                        t_r.append(b.free)
                    t = t_r
                    b = bank()
                    for h in range(8):
                        g_, k = G[h % 2], slice(h // 2 * 128, h // 2 * 128 + 128)
                        t2 = mm(b.ap[:, h * 64:(h + 1) * 64], g_["XT"][:, k], rhs[:, h * 64:(h + 1) * 64],
                                after=(t, tx, b.free))
                    b.free = [cp("act", sa, b.ap, after=t2)]
                    t_sa = b.free
                    b, by = bank(), bank()
                    for h in range(8):
                        g_, k, j, lo = G[h % 2], slice(h // 2 * 128, h // 2 * 128 + 128), h // 2, 64 * (h % 2)
                        hs = slice(h * 64, (h + 1) * 64)
                        o = b.ap[lo:lo + 64, j * 64:(j + 1) * 64]
                        mm(o, tok[0][:, hs], sa[:, hs], True, False, after=(t_sa, b.free))
                        t = mm(o, tok[1][:, hs], tok[2][:, hs], False, True)
                    for h in range(8):
                        g_, k, j, lo = G[h % 2], slice(h // 2 * 128, h // 2 * 128 + 128), h // 2, 64 * (h % 2)
                        hs = slice(h * 64, (h + 1) * 64)
                        o = by.ap[lo:lo + 64, j * 128:(j + 1) * 128]
                        mm(o, tok[2][:, hs], g_["rk"][:, k], True, False, after=by.free)
                        mm(o, sa[:, hs], g_["rb"][:, k], False, False)
                        t_y = mm(o, S03[lo:lo + 64, j, :], zr[lo:lo + 64, j, cs], False, True)
                    tt("dve", t3(tmp, 4), t3(b.ap[:, 0:256], 4), bcast(eq(e_out, ch), 2, 64), ALU.mult, after=t)
                    b.free = [P.last("dve")]
                    tt("dve", St3, St3, bcast(eq(e_all, ch), 2, 64), ALU.mult)
                    t_s = tt("dve", St, St, tmp, ALU.add)
                    by.free = [cp("act", yrw[:, :, cs], t3(by.ap, 4), after=t_y)]
                    done = [t_y, t_s, by.free]
                P.barrier()
                ar.at = keep_at
                w = [ar.take(S) for _ in range(8)]
                s, tl = load(I["g_up"])
                for j in range(4):
                    y_, (d_, q_, r_, p_) = yrw[:, j, :], w[4 * (j % 2):4 * (j % 2) + 4]
                    P.fence["dve"] = P.fence["act"] = P.fence["pool"] = P.barrier() if j > 1 else []
                    b = bank()
                    t = mm(b.ap, c("ones64"), y_, after=b.free)
                    t = stt(d_, b.ap, -1.0 / 64, y_, ALU.mult, ALU.add, after=t)
                    b.free = [t]
                    t = act(q_, d_, ACT.Square, after=t)
                    b = bank()
                    t = mm(b.ap, c("ones64"), q_, after=(t, b.free))
                    t = act(r_, b.ap, ACT.Sqrt, scale=1.0 / 64, bias=gneps, after=t)
                    b.free = [t]
                    P.op("dve", lambda g, r_=r_: g.reciprocal(r_, r_), t)
                    tt("dve", d_, d_, r_, ALU.mult)
                    ts("dve", d_, d_, v("gnw", j), v("gnb", j), ALU.mult, ALU.add)
                    t = stt(p_, zr[:, j, :], v("rk", j), zk[:, j, :], ALU.mult, ALU.mult)
                    b = bank()
                    t = mm(b.ap, c("ones64"), p_, after=(t, b.free))
                    t = tt("dve", p_, b.ap, zv[:, j, :], ALU.mult, after=t)
                    b.free = [t]
                    tt("dve", d_, d_, p_, ALU.add)
                    b = bank()
                    t = mm(b.ap, s.ap[:, j * 128:(j + 1) * 128], sgd, after=(tl, b.free))
                    t = tt("dve", y_, d_, b.ap, ALU.mult, after=t)
                    b.free = [t]
                s.free = [P.last("pe")]
                P.barrier()
            if stop == "rwkv":
                pass
            elif stop != "b1":
                ar.at = rw_at
                ymla = t3(ar.take(4 * S), 4)
                mrg_at = ar.at
                qd, kvd, kr = t3(ar.take(3 * S), 3), t3(ar.take(2 * S), 2), ar.take(S)
                scratch, rs = ar.take(2 * S), ar.take(S)
                lat = [qd[:, 0, :], qd[:, 1, :], qd[:, 2, :], kvd[:, 0, :], kvd[:, 1, :], kr]
                for j in range(3):
                    lin([W2[7 + j, 0]], h_of, 256, 8,
                        lambda m, ps, t, j=j: cp("act", lat[2 * j + m], ps, after=t))
                t_l = P.last("act")
                t_q = rms(qd, qd, 3, 384, "gqa", scratch, rs, after=t_l)
                P.barrier()
                t_kv = rms(kvd, kvd, 2, 256, "gkva", scratch, rs)
                P.barrier()
                qn, qr, kn, vt = t3(ar.take(4 * S), 4), t3(ar.take(2 * S), 2), t3(ar.take(4 * S), 4), t3(ar.take(4 * S), 4)
                lin_q = lambda kt: qd[:, kt, :]
                lin([I["qn_up"]], lin_q, 512, 3, lambda m, ps, t: cp("act", qn[:, m, :], ps, after=t))
                lin([I["qr_up"]], lin_q, 256, 3, lambda m, ps, t: cp("dve", qr[:, m, :], ps, after=t))
                s, tl = load(I["kv_up"])
                for m in range(4):
                    b = bank()
                    for kt in range(2):
                        t = mm(b.ap, s.ap[:, kt * 1024 + m * 128:kt * 1024 + (m + 1) * 128], kvd[:, kt, :], kt == 0,
                               kt == 1, after=(tl, b.free))
                    b.free = [cp("act", kn[:, m, :], b.ap, after=t)]
                t, _ = lin_tok(s, tl, 512, 512, 2, 1024, lambda kt: kvd[:, kt, :], vt, "dve")
                s.free = [t]
                rt = ar.take(S)
                for src in (qr[:, 0, :], qr[:, 1, :], kr):
                    b = bank()
                    t = mm(b.ap, c("rot32"), src, after=(b.free, P.last("dve")))
                    t2 = tt("dve", rt, b.ap, sin32, ALU.mult, after=t)
                    b.free = [t2]
                    tt("dve", src, src, cos32, ALU.mult)
                    tt("dve", src, src, rt, ALU.add)
                P.barrier()

                def scores(h, o, qt, kl, after):
                    hp, lo, ro = h // 2, 64 * (h % 2), 32 * (h % 4)
                    mm(o, qn[lo:lo + 64, hp, qt * 128:(qt + 1) * 128], kn[lo:lo + 64, hp, 0:kl], True, False, after)
                    return mm(o, qr[ro:ro + 32, h // 4, qt * 128:(qt + 1) * 128], kr[ro:ro + 32, 0:kl], False, True)

                def mask(ps, Sb, m, qt, kl, after):
                    tm = c("causal")[:, (3 - qt) * 128:512]
                    return P.op("dve", lambda g: g.tensor_tensor_reduce(
                        Sb, ps[:, 0:kl], tm, float(-1.0 / np.sqrt(96.0)), 3.0e38, ALU.add, ALU.min, m), after)

                for _ in attention(ar, 8, scores, mask, lambda qt: 128 * (qt + 1),
                                   lambda h, k: vt[:, k, h * 64:(h + 1) * 64],
                                   lambda hp, ps, t: cp("act", ymla[:, hp, :], ps, after=t)):
                    pass
                P.barrier()
            if stop in ("rwkv", "mla", "b1"):
                pass
            else:
                ar.at = mrg_at
                mrg = t3(ar.take(8 * S), 8)
                gb = [t3(ar.take(4 * S), 4) for _ in range(2)]
                tb = [ar.take(S) for _ in range(2)]
                gbt = [[], []]
                tbt = [[], []]
                for j in range(2):
                    for br, y in ((0, yrw), (1, ymla)):
                        for i in range(2):
                            lin([W2[10 + 4 * br + 2 * j + i, 0]], h_of, 256, 8,
                                lambda m, ps, t, br=br, i=i: act(gb[br][:, 2 * i + m, :], ps, ACT.Sigmoid,
                                                                after=(t, gbt[br])))
                        t_g = P.last("act")

                        def ev_m(m, ps, t, br=br, j=j, t_g=t_g):
                            if br == 0:
                                return tt("dve", mrg[:, 4 * j + m, :], ps, gb[0][:, m, :], ALU.mult, after=(t, t_g))
                            r = tt("dve", tb[m % 2], ps, gb[1][:, m, :], ALU.mult, after=(t, t_g))
                            tt("dve", mrg[:, 4 * j + m, :], mrg[:, 4 * j + m, :], tb[m % 2], ALU.add)
                            return r

                        lin([I["wb"][br, j]], lambda kt, y=y: y[:, kt, :], 512, 4, ev_m)
                        gbt[br] = [P.last("dve")]
                t_m = P.last("dve")

                def ev_res2(mt):
                    return lambda m, ps, t: tt("dve", Xt[:, 2 * mt + m, :], Xt[:, 2 * mt + m, :], ps, ALU.add, after=t)

                for j in range(4):
                    lin([I["w_out2"][j, 0]], lambda kt: mrg[:, kt, :], 256, 8, ev_res2(j), after=t_m)
                P.barrier()
            if stop in ("rwkv", "mla", "b1", "mid"):
                pass
            else:
                ar = Arena(0, ARENA)
                scratch, rs = ar.take(2 * S), ar.take(S)
                t_h = rms(Ht, Xt, 8, D, "ffg", scratch, rs)
                ar.at = 0
                P.barrier()
                lg, bb = ar.take(144), ar.take(36)
                lg3 = t3(lg, 4)
                t_bb = P.dma("act", bb, I["br"].partition_broadcast(128), "const", after=P.barrier())
                s, tl = load(I["wr"])
                t, _ = lin_tok(s, tl, 0, 36, 8, 36, h_of, lg3, "act")
                s.free = [t]
                tt("dve", lg3, lg3, bcast(bb, 1, 4), ALU.add, after=(P.last("act"), t_bb))
                gl, fl_, pen = t3(ar.take(16), 4), t3(ar.take(128), 4), t3(ar.take(16), 4)
                cand, oh1, oh2, Gt = (t3(ar.take(128), 4) for _ in range(4))
                cg, mx, gm, gs, m1, m2, ee, g1, g2 = (ar.take(16 if i == 0 else 4) for i in range(9))
                cg = t3(cg, 4)
                b4 = lambda x, n: bcast(x, 2, n)

                htok = t3(ar.take(4 * D), 4)
                for k in range(4):
                    for f2 in range(2):
                        b = bank()
                        for f in range(4):
                            t = tr(b.ap[:, f * 128:(f + 1) * 128], Ht[:, f2 * 4 + f, k * 128:(k + 1) * 128],
                                   after=(t_h, b.free))
                        b.free = [cp("act", htok[:, k, f2 * 512:(f2 + 1) * 512], b.ap, after=t)]
                    t_hd = P.dma("sp", hdram[k * 128:(k + 1) * 128, :], htok[:, k, :], "hd", after=b.free)

                def red(o, a, op):
                    return P.op("dve", lambda g: g.tensor_reduce(o, a, AX_X, op))

                def one_hot(dst, src, top, tmp_, n):
                    red(top, src, ALU.max)
                    tt("dve", tmp_, src, b4(top, n), ALU.is_equal)
                    tt("dve", tmp_, tmp_, bcast(c("iota")[:, 0:n], 1, 4), ALU.mult)
                    red(mx, tmp_, ALU.max)
                    return tt("dve", dst, tmp_, b4(mx, n), ALU.is_equal)

                cp("dve", gl, lg3[:, :, 0:4])
                cp("dve", fl_, lg3[:, :, 4:36])
                one_hot(pen, gl, gm, cg, 4)
                t = tt("dve", gl, gl, b4(gm, 4), ALU.subtract)
                t = act(gl, gl, ACT.Exp, after=t)
                P.fence["dve"] = [t]
                red(gs, gl, ALU.add)
                P.op("dve", lambda g: g.reciprocal(gs, gs))
                ts("dve", pen, pen, -1.0, BIG, ALU.add, ALU.mult)
                f16 = fl_.rearrange("p a (g e) -> p (a g) e", e=8)
                tt("dve", f16, f16, bcast(pen.rearrange("p a g -> p (a g)"), 2, 8), ALU.add)
                one_hot(oh1, fl_, m1, cand, 32)
                stt(fl_, oh1, -BIG, fl_, ALU.mult, ALU.add)
                one_hot(oh2, fl_, m2, cand, 32)
                t = tt("dve", ee, m2, m1, ALU.subtract)
                t = act(ee, ee, ACT.Exp, after=t)
                ts("dve", g1, ee, 1.0, None, ALU.add, after=t)
                P.op("dve", lambda g: g.reciprocal(g1, g1))
                tt("dve", g1, g1, gs, ALU.mult)
                tt("dve", g2, g1, ee, ALU.mult)
                Mk, pm, dst_, tkc = (t3(ar.take(128), 4) for _ in range(4))
                tab = ar.take(4 * 96).rearrange("p (k e r) -> p k e r", k=4, r=3)
                cnt = ar.take(32)
                t_mk = tt("dve", Mk, oh1, oh2, ALU.add)
                tt("dve", dst_, oh2, bcast(c("tok2"), 2, 32), ALU.add)
                tt("dve", Gt, oh1, b4(g1, 32), ALU.mult)
                tt("dve", oh2, oh2, b4(g2, 32), ALU.mult)
                tt("dve", Gt, Gt, oh2, ALU.add)
                cp("dve", tab[:, :, :, 0], bcast(c("tok"), 2, 32))
                cp("dve", tab[:, :, :, 1], dst_)
                t_tab = cp("dve", tab[:, :, :, 2], Gt)
                b = bank()
                for k in range(4):
                    for k2_ in range(k + 1):
                        t = mm(b.ap[:, k * 32:(k + 1) * 32], c("ones") if k2_ < k else c("strict"), Mk[:, k2_, :],
                               k2_ == 0, k2_ == k, after=(t_mk, b.free))
                for k in range(4):
                    t = mm(b.ap[:, 128:160], c("ones"), Mk[:, k, :], k == 0, k == 3)
                stt(pm, t3(b.ap[:, 0:128], 4), 1.0, Mk, ALU.add, ALU.mult, after=t)
                ts("dve", pm, pm, -1.0, None, ALU.add)
                b.free = [cp("dve", cnt, b.ap[:, 128:160])]
                ne, uc, ux, tw = (ar.take(32) for _ in range(4))
                flag = small[:, 250:251].bitcast(U32)
                ts("dve", ne, cnt, 128.5, None, ALU.is_gt)
                for lim in (256.5, 384.5):
                    ts("dve", tw, cnt, lim, None, ALU.is_gt)
                    tt("dve", ne, ne, tw, ALU.add)
                P.op("dve", lambda g: g.tensor_tensor_scan(uc, c("ones")[:, 0:32], ne, 0.0, ALU.mult, ALU.add))
                tt("dve", ux, uc, ne, ALU.subtract)
                t_flag = cp("dve", flag, uc[:, 31:32])

                Pm = [ar.take(S) for _ in range(2)]
                idx = ar.take(32).bitcast(U32)
                dix = ar.take(32).bitcast(U32)
                gsl = ar.take(32)
                b = bank()
                tp = [[], []]
                for e_ in range(32):
                    t = tt("dve", t3(Pm[e_ % 2], 4), bcast(c("io128"), 1, 4), bcast(pm[:, :, e_], 2, 128),
                           ALU.is_equal, after=tp[e_ % 2])
                    for k in range(4):
                        t2 = mm(b.ap[:, e_ * 3:e_ * 3 + 3], Pm[e_ % 2][:, k * 128:(k + 1) * 128], tab[:, k, e_, :],
                                k == 0, k == 3, after=(t, t_tab, b.free))
                    tp[e_ % 2] = [t2]
                bv = b.ap[:, 0:96].rearrange("p (e r) -> p e r", r=3)
                t_idx = cp("dve", idx, bv[:, :, 0], after=t2)
                t_dix = ts("dve", dix, bv[:, :, 1], 4096.0, None, ALU.add)
                t_gsl = cp("dve", gsl, bv[:, :, 2])
                b.free = [t_gsl]

                NB = 3
                Xg = [ar.take(D) for _ in range(NB)]
                XT = [t3(ar.take(D), 8) for _ in range(2)]
                sgm = [ar.take(256) for _ in range(2)]
                hu = [ar.take(256) for _ in range(2)]
                hT = [ar.take(256) for _ in range(2)]
                Yb = [ar.take(D) for _ in range(NB)]

                def gather(Pq, o, tab_, ix, sem, after):
                    return Pq.swdge(lambda g: g.indirect_dma_start(
                        o, None, tab_, bass.IndirectOffsetOnAxis(ix, 0), bounds_check=tab_.shape[0] - 1,
                        oob_is_err=False), sem, after)

                def scatter(Pq, y, ix, sem, after):
                    return Pq.swdge(lambda g: g.indirect_dma_start(
                        ydram, bass.IndirectOffsetOnAxis(ix, 0), y, None, bounds_check=2 * S - 1,
                        oob_is_err=False), sem, after)

                st = {"g": {}, "B": {}, "C": {}, "D": {}, "E": {}, "S": {}}

                def st_gather(e_):
                    st["g"][e_] = gather(P, Xg[e_ % NB], hdram, idx[:, e_:e_ + 1], f"g{e_ % NB}",
                                         (t_hd, t_idx, st["B"].get(e_ - NB, [None])[0]))

                def st_turn(e_):
                    for f2 in range(2):
                        b = bank()
                        for f in range(4):
                            t = tr(b.ap[:, f * 128:(f + 1) * 128], Xg[e_ % NB][:, (f2 * 4 + f) * 128:(f2 * 4 + f + 1) * 128],
                                   after=(st["g"][e_], b.free))
                        b.free = [cp("dve" if f2 else "act", XT[e_ % 2][:, f2 * 4:f2 * 4 + 4, :], t3(b.ap, 4),
                                     after=(t, st["C"].get(e_ - 2, [None])[0]))]
                        if f2 == 0:
                            first = b.free
                    st["B"][e_] = [t, first, b.free]

                def st_up(e_):
                    b = bank()
                    for j in range(2):
                        s, tl = load(I["w_gu"][e_, j])
                        for kt in range(4):
                            t = mm(b.ap, XT[e_ % 2][:, j * 4 + kt, :], s.ap[:, kt * 512:(kt + 1) * 512],
                                   j + kt == 0, j == 1 and kt == 3, after=(tl, st["B"][e_], b.free))
                        s.free = [t]
                    ta = act(sgm[e_ % 2], b.ap[:, 0:256], ACT.Sigmoid, after=(t, st["C"].get(e_ - 2)))
                    tt("dve", hu[e_ % 2], b.ap[:, 0:256], sgm[e_ % 2], ALU.mult, after=(ta, st["D"].get(e_ - 2)))
                    t2 = tt("dve", hu[e_ % 2], hu[e_ % 2], b.ap[:, 256:512], ALU.mult)
                    b.free = [t2]
                    st["C"][e_] = [t, t2]

                def st_mid(e_):
                    b = bank()
                    for k in range(2):
                        t = tr(b.ap[:, k * 128:(k + 1) * 128], hu[e_ % 2][:, k * 128:(k + 1) * 128],
                               after=(st["C"][e_], b.free))
                    t2 = cp("act", hT[e_ % 2], b.ap[:, 0:256], after=(t, st["E"].get(e_ - 2)))
                    b.free = [t2]
                    st["D"][e_] = [t, t2]

                def st_down(e_):
                    s, tl = load(I["w_dn"][e_])
                    for n in range(2):
                        b = bank()
                        for kt in range(2):
                            t = mm(b.ap, hT[e_ % 2][:, kt * 128:(kt + 1) * 128],
                                   s.ap[:, kt * 1024 + n * 512:kt * 1024 + (n + 1) * 512], kt == 0, kt == 1,
                                   after=(tl, st["D"][e_], b.free))
                        o = Yb[e_ % NB][:, n * 512:(n + 1) * 512]
                        w_ = (t, t_gsl, st["S"].get(e_ - NB))
                        if n:
                            t2 = ts("dve", o, b.ap, gsl[:, e_:e_ + 1], None, ALU.mult, after=w_)
                        else:
                            t2 = act(o, b.ap, ACT.Copy, scale=gsl[:, e_:e_ + 1], after=w_)
                            t1 = t2
                        b.free = [t2]
                    s.free = [t]
                    st["E"][e_] = [t]
                    st["S"][e_] = scatter(P, Yb[e_ % NB], dix[:, e_:e_ + 1], f"y{e_ % NB}", (t1, t2, t_dix))

                st_gather(0)
                st_gather(1)
                st_turn(0)
                for e_ in range(32):
                    st_up(e_)
                    if e_ < 31:
                        st_turn(e_ + 1)
                    if e_ < 30:
                        st_gather(e_ + 2)
                    if e_:
                        st_down(e_ - 1)
                    st_mid(e_)
                st_down(31)

                P2 = Prog(["pe2", "act2", "dve2", "pool2"])
                P2.serial = True
                sel, posj, gj, rj = ar.take(32), ar.take(4), ar.take(4), ar.take(4)
                offs, eps_ = ar.take(1), ar.take(1)
                tj = t3(ar.take(128), 4)
                tabj = ar.take(12).rearrange("p (k r) -> p k r", k=4)
                wix = ar.take(3).bitcast(U32)
                ixj = ar.take(2).bitcast(U32)
                wgu_rows = I["w_gu"].rearrange("e j p n -> (e j p) n")
                wdn_rows = I["w_dn"].rearrange("e p n -> (e p) n")
                q2 = lambda e, fn: P2.op(e + "2", fn)
                dv = lambda name, *a: q2("dve", lambda g: {"tt": g.tensor_tensor, "ts": g.tensor_scalar,
                                                           "cp": g.tensor_copy, "red": g.tensor_reduce}[name](*a))
                for j in range(7):
                    dv("ts", sel, ux, float(j) + 0.5, None, ALU.is_lt)
                    dv("ts", tw, uc, float(j) + 0.5, None, ALU.is_gt)
                    dv("tt", sel, sel, tw, ALU.mult)
                    dv("tt", tw, sel, ux, ALU.mult)
                    dv("red", offs, tw, AX_X, ALU.add)
                    dv("ts", offs, offs, 128.0, -128.0 * (1 + j), ALU.mult, ALU.add)
                    dv("tt", tw, sel, c("iota"), ALU.mult)
                    dv("red", eps_, tw, AX_X, ALU.add)
                    dv("ts", eps_, eps_, -1.0, 32.0, ALU.mult, ALU.add)
                    dv("ts", eps_, eps_, 31.0, None, ALU.min)
                    for i, (m_, a_) in enumerate(((256.0, 0.0), (256.0, 128.0), (128.0, 0.0))):
                        dv("ts", tw[:, 0:1], eps_, m_, a_, ALU.mult, ALU.add)
                        dv("tt", wix[:, i:i + 1], tw[:, 0:1], c("tok")[:, 0:1], ALU.add)
                    for o_, src in ((posj, pm), (gj, Gt), (rj, dst_)):
                        dv("tt", tj, src, bcast(sel, 1, 4), ALU.mult)
                        dv("red", o_, tj, AX_X, ALU.add)
                    dv("ts", posj, posj, offs, None, ALU.add)
                    dv("cp", tabj[:, :, 0], c("tok"))
                    dv("cp", tabj[:, :, 1], rj)
                    dv("cp", tabj[:, :, 2], gj)
                    dv("tt", t3(Pm[0], 4), bcast(c("io128"), 1, 4), bcast(posj, 2, 128), ALU.is_equal)
                    ps = psum
                    for k in range(4):
                        q2("pe", lambda e, k=k: e.matmul(ps[:, 0, 0:3], Pm[0][:, k * 128:(k + 1) * 128], tabj[:, k, :],
                                                         start=k == 0, stop=k == 3))
                    dv("cp", ixj[:, 0:1], ps[:, 0, 0:1])
                    dv("ts", ixj[:, 1:2], ps[:, 0, 1:2], 4096.0, None, ALU.add)
                    dv("cp", gsl[:, 0:1], ps[:, 0, 2:3])
                    gather(P2, Xg[0], hdram, ixj[:, 0:1], "o", None)
                    for i, rows in enumerate((wgu_rows, wgu_rows, wdn_rows)):
                        gather(P2, slots[i].ap, rows, wix[:, i:i + 1], "o", None)
                    for f in range(8):
                        q2("pe", lambda e, f=f: e.matmul(ps[:, f // 4, f % 4 * 128:f % 4 * 128 + 128],
                                                         Xg[0][:, f * 128:(f + 1) * 128], c("ident"), start=True,
                                                         stop=True, is_transpose=True))
                    for f2 in range(2):
                        dv("cp", XT[0][:, f2 * 4:f2 * 4 + 4, :], t3(ps[:, f2, :], 4))
                    for kt in range(8):
                        q2("pe", lambda e, kt=kt: e.matmul(ps[:, 2, :], XT[0][:, kt, :],
                                                           slots[kt // 4].ap[:, kt % 4 * 512:kt % 4 * 512 + 512],
                                                           start=kt == 0, stop=kt == 7))
                    q2("act", lambda e: e.activation(sgm[0], ps[:, 2, 0:256], ACT.Sigmoid))
                    dv("tt", hu[0], ps[:, 2, 0:256], sgm[0], ALU.mult)
                    dv("tt", hu[0], hu[0], ps[:, 2, 256:512], ALU.mult)
                    for k in range(2):
                        q2("pe", lambda e, k=k: e.matmul(ps[:, 3, k * 128:(k + 1) * 128], hu[0][:, k * 128:(k + 1) * 128],
                                                         c("ident"), start=True, stop=True, is_transpose=True))
                    dv("cp", hT[0], ps[:, 3, 0:256])
                    for n in range(2):
                        for kt in range(2):
                            q2("pe", lambda e, n=n, kt=kt: e.matmul(
                                ps[:, 4 + n, :], hT[0][:, kt * 128:(kt + 1) * 128],
                                slots[2].ap[:, kt * 1024 + n * 512:kt * 1024 + (n + 1) * 512], start=kt == 0,
                                stop=kt == 1))
                    for n in range(2):
                        dv("ts", Yb[0][:, n * 512:(n + 1) * 512], ps[:, 4 + n, :], gsl[:, 0:1], None, ALU.mult)
                    scatter(P2, Yb[0], ixj[:, 1:2], "o", None)
                waits_y = [st["S"][31], st["S"][30], st["S"][29]]
                P.section(P2, flag[0:1, 0:1], list(P.barrier()) + waits_y)

                ar.at = 0
                P.barrier()
                Y2 = [ar.take(2 * D) for _ in range(4)]
                for k in range(4):
                    ty = P.dma("sp", Y2[k], ydram[k * 256:(k + 1) * 256, :].rearrange("(p r) n -> p (r n)", r=2), f"Y{k}",
                               after=(P.fence_all(), waits_y))
                    t = tt("dve", Y2[k][:, 0:D], Y2[k][:, 0:D], Y2[k][:, D:2 * D], ALU.add, after=ty)
                    for f2 in range(2):
                        b = bank()
                        for f in range(4):
                            t2 = tr(b.ap[:, f * 128:(f + 1) * 128], Y2[k][:, (f2 * 4 + f) * 128:(f2 * 4 + f + 1) * 128],
                                    after=(t, b.free))
                        xo = Xt[:, f2 * 4:f2 * 4 + 4, k * 128:(k + 1) * 128]
                        b.free = [tt("dve", xo, xo, t3(b.ap, 4), ALU.add, after=t2)]
                P.barrier()
                rms(Xt, Xt, 8, D, "fing", ar.take(2 * S), ar.take(S))
                P.barrier()
        t_end = P.barrier()
        P.fence = {}
        for kt in range(8):
            t = P.dma("sp", out[kt * 128:(kt + 1) * 128, :], Xt[:, kt, :], "out", after=t_end)
        total = t
        P.q["sp"].append((lambda e: None, [total], None))
        P.settle()
        finish(nc, ctx, P, sem_of)
    return nc


def finish(nc, ctx, P, sem_of):
    block = ctx.enter_context(nc.Block())
    end = P.q["sp"].pop()
    end[1][0].used = True

    @block.sync
    def _(eng):
        P.run("sp", eng, sem_of)
        eng.wait_ge(sem_of("out"), end[1][0].value)

    @block.scalar
    def _(eng):
        P.run("act", eng, sem_of)

    @block.gpsimd
    def _(eng):
        P.run("pool", eng, sem_of)

    @block.vector
    def _(eng):
        P.run("dve", eng, sem_of)

    @block.tensor
    def _(eng):
        P.run("pe", eng, sem_of)


def constants():
    f = np.float32
    C = np.zeros((128, NC32), f)

    def put(name, x):
        o, w = CO[name]
        C[:, o:o + w] = x

    i = np.arange(128)
    put("ident", np.eye(128))
    put("ones", 1.0)
    put("ones64", (i[:, None] // 64 == i[None] // 64))
    for name, w in (("rot64", 64), ("rot32", 32)):
        R = np.zeros((128, 128))
        for m in range(128):
            g, r = m // w * w, m % w
            if r < w // 2:
                R[g + r + w // 2, m] = -1.0
            else:
                R[g + r - w // 2, m] = 1.0
        put(name, R)
    d = np.arange(64)
    ang = 2 * np.pi * np.outer(d, d) / 64
    sc = 1.0 / np.sqrt(512.0 * 64.0)
    put("cd", np.kron(np.eye(2), np.cos(ang) * sc))
    put("sd", np.kron(np.eye(2), -np.sin(ang) * sc))
    delta = np.abs(i[:, None] + 384 - np.arange(896)[None])
    count = (delta <= 64) * 1.0 + ((delta <= 256) & (delta % 4 == 0)) + (delta % 16 == 0)
    put("tmask", np.where(count > 0, 8.0 * np.log(np.maximum(count, 1)), -BIG))
    put("causal", np.where(np.arange(512)[None] - 384 <= i[:, None], 0.0, -BIG))
    put("strict", i[:, None] < i[None])
    put("incl", i[:, None] <= i[None])
    iv = (f(10000.0) ** (-np.arange(0, 64, 2, dtype=f) / f(64))).astype(f)
    put("invf64", np.tile(iv, 4)[:, None])
    iv = (f(10000.0) ** (-np.arange(0, 32, 2, dtype=f) / f(32))).astype(f)
    put("invf32", np.tile(iv, 8)[:, None])
    put("iota", 32.0 - np.arange(32)[None])
    put("io128", i[None])
    put("tok", i[:, None] + 128 * np.arange(4)[None])
    put("tok2", 2 * (i[:, None] + 128 * np.arange(4)[None]) - 4096)
    M = np.zeros((128, 14, 128), f)
    for l in range(7):
        same = (i[:, None] >> (l + 1)) == (i[None] >> (l + 1))
        m = same & ((i[:, None] >> l) % 2 == 0) & ((i[None] >> l) % 2 == 1)
        M[:, l] = m
        M[:, 7 + l] = m.T
    p = np.arange(512)
    a = 2 * np.pi * (np.outer(p, p) % 512) / 512
    dft = np.stack([np.cos(a), np.sin(a)]).astype(f).reshape(2, 4, 128, 512).transpose(0, 2, 1, 3)
    return {"c32": C, "m32": M.reshape(128, -1), "dft": np.ascontiguousarray(dft.reshape(2, 128, 2048))}


def lay(w, kt, nc_):
    K, N = w.shape
    return np.ascontiguousarray(
        w.reshape(K // (128 * kt), kt, 128, N // nc_, nc_).transpose(3, 0, 2, 1, 4).reshape(
            N // nc_, K // (128 * kt), 128, kt * nc_))


def cols(x):
    return np.ascontiguousarray(x.reshape(-1, 128).T)


def layout(inp):
    g = {k: np.asarray(x) for k, x in inp.items()}
    a = constants()
    a["x"] = np.ascontiguousarray(g["x"][0].T.reshape(8, 128, 512))
    a["pos1"] = np.ascontiguousarray(g["positions"][0])
    a["w_in"] = np.stack([lay(g["w_in"][i], 8, 256) for i in range(2)])
    a["w_out"] = np.stack([lay(g["w_out"][i], 8, 256) for i in range(2)])
    a["w_up"] = np.stack([lay(g["w_up"][i], 8, 256) for i in range(2)])
    a["w_down"] = np.stack([lay(g["w_down"][i], 8, 256) for i in range(2)])
    q = {k[:-2]: x[0] for k, x in g.items() if k.endswith("_2")}
    a["pos2"] = np.ascontiguousarray(g["positions_2"][0])
    w = q["w_in"]
    a["w_in2"] = lay(np.concatenate([w[:, :2432]] + [w[:, 2432:2464]] * 4 + [w[:, 2464:]], 1), 8, 256)
    a["wa_up"] = np.concatenate([q["rw_w_up"], q["rw_a_up"]], 0)
    a["g_up"] = np.ascontiguousarray(q["rw_g_up"])
    wq = q["mla_w_q_up"].reshape(384, 8, 96)
    a["qn_up"] = lay(wq[:, :, :64].reshape(384, 512), 3, 512)[0, 0]
    a["qr_up"] = lay(wq[:, :, 64:].reshape(384, 256), 3, 256)[0, 0]
    wk = q["mla_w_kv_up"].reshape(256, 8, 128)
    a["kv_up"] = lay(np.concatenate([wk[:, :, :64].reshape(256, 512), wk[:, :, 64:].reshape(256, 512)], 1), 2, 1024)[0, 0]
    a["wb"] = np.stack([lay(q["w_branch_rw"], 4, 512)[:, 0], lay(q["w_branch_mla"], 4, 512)[:, 0]])
    a["w_out2"] = lay(q["w_out"], 8, 256)
    a["wr"] = lay(np.concatenate([q["moe_w_group"], q["moe_w_router"]], 1), 8, 36)[0, 0]
    a["br"] = np.concatenate([q["moe_b_group"], q["moe_b_router"]])
    w = q["moe_w_gu"].reshape(32, 2, 4, 128, 512).transpose(0, 1, 3, 2, 4)
    a["w_gu"] = np.ascontiguousarray(w).reshape(32, 2, 128, 2048)
    a["w_dn"] = np.ascontiguousarray(q["moe_w_down"].reshape(32, 2, 128, 1024).transpose(0, 2, 1, 3)).reshape(32, 128, 2048)
    vec = {"an0": g["attn_norm_w"][0], "an1": g["attn_norm_w"][1], "mn0": g["mlp_norm_w"][0],
           "mn1": g["mlp_norm_w"][1], "fn1": g["final_norm_w"], "lb": g["hgrn_lower_bounds"],
           "mixg": g["mix_norm_g_2"], "mu": g["rw_mu_2"], "w0": g["rw_w0_2"], "a0": g["rw_a0_2"],
           "kk": g["rw_k_k_2"], "ka": g["rw_k_a_2"], "rk": g["rw_r_k_2"], "gnw": g["rw_gn_w_2"],
           "gnb": g["rw_gn_b_2"], "gqa": g["mla_g_qa_2"], "gkva": g["mla_g_kva_2"],
           "ffg": g["ffn_norm_g_2"], "fing": g["final_norm_g_2"]}
    Vv = np.zeros((128, NV), np.float32)
    for k, x in vec.items():
        o, w = VO[k]
        Vv[:, o:o + w] = cols(x)
    a["vecs"] = Vv
    return a


def kernel(**inputs):
    import concourse.bacc as _bacc
    from concourse.bass_utils import run_bass_kernel_spmd as _run

    nc = _bacc.Bacc("TRN2", target_bir_lowering=False, num_devices=1)
    arrays = layout(inputs)
    I = {k: nc.dram_tensor("in_" + k, a.shape, mybir.dt.from_np(a.dtype), kind="ExternalInput").ap()
         for k, a in arrays.items()}
    out = nc.dram_tensor("out_0", (D, S), F32, kind="ExternalOutput").ap()
    build(nc, I, out)
    r = _run(nc, [{"in_" + k: a for k, a in arrays.items()}], core_ids=[0])
    return np.ascontiguousarray(r.results[0]["out_0"].T)[None]
```

```python
from contextlib import ExitStack

import numpy as np
import concourse.bass as bass
from concourse import mybir

F32 = mybir.dt.float32
F32R = mybir.dt.float32r
I32 = mybir.dt.int32
U8 = mybir.dt.uint8
U32 = mybir.dt.uint32
ALU = mybir.AluOpType
ACT = mybir.ActivationFunctionType
AX_X = mybir.AxisListType.X

S = 512
D = 1024
SLOT = 2048
NSLOT = 2
NUNIT = 3
UNIT = 1024
BIG = 1.0e30

CO = {}
_n = 0
for _name, _w in (("ident", 128), ("ones", 128), ("ones64", 128), ("rot64", 128), ("rot32", 128),
                  ("cd", 128), ("sd", 128), ("tmask", 896), ("causal", 512), ("strict", 128),
                  ("incl", 128), ("invf64", 1), ("invf32", 1), ("iota", 32), ("io128", 128), ("tok", 4), ("tok2", 4)):
    CO[_name] = (_n, _w)
    _n += _w
NC32 = _n

VO = {}
_n = 0
for _name, _w in (("an0", 8), ("an1", 8), ("mn0", 8), ("mn1", 8), ("fn1", 8), ("lb", 8),
                  ("mixg", 8), ("mu", 14), ("w0", 4), ("a0", 4), ("kk", 4), ("ka", 4), ("rk", 4),
                  ("gnw", 4), ("gnb", 4), ("gqa", 3), ("gkva", 2), ("ffg", 8), ("fing", 8)):
    VO[_name] = (_n, _w)
    _n += _w
NV = _n


class Tok:

    def __init__(self, sem, value=None):
        self.sem, self.value, self.used = sem, value, False


class Prog:

    def __init__(self, sems):
        self.sems = sems
        self.q = {e: [] for e in sems}
        self.q["sp"] = []
        self.q["sp2"] = []
        self.fence = {}
        self.tail = {}
        self.pend = []
        self.dma_count = {}
        self.serial = False
        self.prev = None

    def last(self, e):
        return self.tail.get(e)

    def streams(self, *gens):
        self.flush()
        ends = self.ends()
        state = [[0.0, i, g, dict(self.tail), {e: list(ends) for e in self.sems}, []] for i, g in enumerate(gens)]
        done = []
        while state:
            st = min(state)[:2]
            st = next(x for x in state if x[1] == st[1])
            self.tail, self.fence, self.pend = st[3], st[4], st[5]
            try:
                st[0] += next(st[2])
            except StopIteration:
                self.flush()
                state.remove(st)
                done.append(st)
            st[3], st[4], st[5] = self.tail, self.fence, self.pend
        ends = [t for st in done for t in st[3].values()]
        self.tail, self.pend = done[-1][3], []
        self.fence = {e: list(ends) for e in self.sems}

    def flush(self):
        while self.pend:
            self.pend.pop(0)()

    def ends(self):
        return [self.tail[e] for e in ("pe", "act", "dve", "pool") if e in self.tail]

    def op(self, e, fn, after=()):
        need = [t for t in flat(after) if t is not None]
        if self.serial and self.prev is not None:
            need.append(self.prev)
        elif e in ("act", "dve", "pool") and e in self.tail:
            need.append(self.tail[e])
        need += self.fence.pop(e, [])
        t = Tok(e)
        self.q[e].append((fn, need, t))
        self.prev = t
        self.tail[e] = t
        return t

    def dma(self, e, out, in_, sem, after=()):
        self.dma_count[sem] = self.dma_count.get(sem, 0) + 16
        t = Tok(sem, self.dma_count[sem])
        self.q[e].append((lambda eng: eng.dma_start(out, in_), [x for x in flat(after) if x is not None], t))
        return t

    def swdge(self, fn, sem, after):
        self.dma_count[sem] = self.dma_count.get(sem, 0) + 16
        e = "pool2" if self.serial else "pool"
        need = [x for x in flat(after) if x is not None]
        if self.serial and self.prev is not None:
            need.append(self.prev)
        else:
            need += [self.tail[e]] if e in self.tail else []
            need += self.fence.pop(e, [])
        t = Tok(sem, self.dma_count[sem])
        self.q[e].append((fn, need, t))
        self.prev = t
        return t

    def section(self, other, flag, after):
        end = other.prev
        for e in ("pe", "act", "dve", "pool", "sp"):
            self.q[e].append((("section", other, flag, end), list(after), Tok("none", 0)))
            self.fence.pop(e, None)
            self.tail.pop(e, None)

    def fence_all(self):
        return self.fence.get("pe", [])

    def barrier(self):
        self.flush()
        ends = self.ends()
        for e in ("pe", "act", "dve", "pool"):
            self.fence[e] = list(ends)
        return ends

    def settle(self):
        for e in self.q:
            for _, need, _ in self.q[e]:
                for t in need:
                    t.used = True
        if self.prev is not None:
            self.prev.used = True
        for e in self.q:
            for fn, _, _ in self.q[e]:
                if type(fn) is tuple:
                    fn[1].settle()
        for e in self.sems:
            n = 0
            for _, _, t in self.q[e]:
                if t.sem == e:
                    n += t.used
                    t.value = n

    def run(self, e, eng, sem_of):
        seen = {}
        for fn, need, t in self.q[e]:
            most = {}
            for x in need:
                most[x.sem] = max(most.get(x.sem, 0), x.value)
            for s, v in most.items():
                if seen.get(s, 0) < v:
                    eng.wait_ge(sem_of(s), v)
                    seen[s] = v
            if type(fn) is tuple:
                _, other, flag, end = fn
                many = eng.value_load(flag, min_val=0, max_val=7)
                with eng.If(many > 0):
                    other.run(e + "2", eng, sem_of)
                    eng.wait_ge(sem_of(end.sem), end.value)
                continue
            ins = fn(eng)
            if t.sem != e:
                ins.then_inc(sem_of(t.sem), 16)
            elif t.used:
                ins.then_inc(sem_of(t.sem), 1)


def flat(x):
    if x is None or isinstance(x, Tok):
        return [x]
    out = []
    for y in x:
        out += flat(y)
    return out


class Room:

    def __init__(self, ap, sem=None):
        self.ap, self.sem, self._free, self.busy = ap, sem, [], False

    @property
    def free(self):
        return self._free

    @free.setter
    def free(self, tokens):
        self._free, self.busy = tokens, False


def bcast(ap, axis, n):
    a = ap.unsqueeze(axis)
    shape = list(a.shape)
    shape[axis] = n
    return a.broadcast_to(shape)


def build(nc, I, out, stop=None, dumps=None):
    ctx = ExitStack()
    with ctx:
        def sb(name, n, dt=F32):
            return ctx.enter_context(nc.sbuf_tensor(name, [128, n], dt))

        semh = {}

        def sem_of(s):
            if s not in semh:
                raise KeyError(s)
            return semh[s]

        for s in ["pe", "act", "dve", "pool", "const", "out"] + [f"ring{i}" for i in range(NSLOT + 4)] + [
                "k0", "k1", "kl", "kg", "pe2", "act2", "dve2", "pool2", "hd", "o", "g0", "g1", "g2", "y0", "y1", "y2", "Y0", "Y1", "Y2", "Y3"]:
            semh[s] = ctx.enter_context(nc.semaphore("s_" + s))
        P = Prog(["pe", "act", "dve", "pool"])

        C = sb("C", NC32)
        V = sb("V", NV)
        M8 = sb("M8", 14 * 128, U8)
        X = sb("X", 8 * S)
        TAB = sb("TAB", 2 * S)
        ring = sb("ring", NSLOT * SLOT)
        small = sb("small", 384)
        RSb = sb("RS", S)
        RS = RSb[:, :]
        psum = ctx.enter_context(nc.psum_tensor("psum", [128, 8, 512], F32))
        fast = ctx.enter_context(ExitStack())
        HH, HL = (fast.enter_context(nc.sbuf_tensor(n, [128, 8 * S], F32R)) for n in ("HH", "HL"))
        WH, WL = (fast.enter_context(nc.sbuf_tensor(n, [128, NUNIT * UNIT], F32R)) for n in ("WH", "WL"))
        room = {}
        ctx.callback(lambda: room["stack"].close())

        def phase(name, n, nr=0, extra=0, products=True):
            nonlocal A, R
            ended = []
            if room:
                ended = P.barrier()
                room.pop("stack").close()
            if not products:
                fast.close()
            st = room["stack"] = ExitStack()
            A = st.enter_context(nc.sbuf_tensor("A_" + name, [128, n], F32))
            room["n"] = n
            R = st.enter_context(nc.sbuf_tensor("R_" + name, [128, nr], F32R)) if nr else None
            del slots[NSLOT:]
            for i in range(extra):
                more = st.enter_context(nc.sbuf_tensor(f"ring_{name}{i}", [128, SLOT], F32))
                slots.append(Room(more[:, :], f"ring{NSLOT + i}"))
                slots[-1].free = ended

        A = R = None
        slots = [Room(ring[:, i * SLOT:(i + 1) * SLOT], f"ring{i}") for i in range(NSLOT)]
        phase("start", 2048)
        hdram = nc.dram_tensor("h_rows", (S, D), F32).ap()
        kept = nc.dram_tensor("kept", (22, 128, S), F32).ap()
        ydram = nc.dram_tensor("y_rows", (2 * S, D), F32).ap()

        def c(name):
            o, w = CO[name]
            return C[:, o:o + w]

        def v(name, i=0, n=1):
            o, w = VO[name]
            return V[:, o + i:o + i + n]

        units = [(Room(WH[:, i * UNIT:(i + 1) * UNIT]), WL[:, i * UNIT:(i + 1) * UNIT]) for i in range(NUNIT)]
        banks = [Room(psum[:, i, :]) for i in range(8)]
        turn = {"slot": 0, "bank": 0, "unit": 0}
        held = set()

        def load(src):
            for _ in range(len(slots)):
                s = slots[turn["slot"] % len(slots)]
                turn["slot"] += 1
                if not s.busy:
                    break
            assert not s.busy
            s.busy = True
            t = P.dma("sp", s.ap[:, 0:src.shape[-1]], src, s.sem, s.free)
            return s, t

        def bank(hold=False):
            for _ in range(9):
                i = turn["bank"] % 8
                turn["bank"] += 1
                if i not in held and not banks[i].busy:
                    break
            assert i not in held and not banks[i].busy
            banks[i].busy = not hold
            if hold:
                held.add(i)
            return banks[i]

        def release(b):
            held.discard(banks.index(b))

        def mm(o, l, r, start=True, stop=True, after=()):
            return P.op("pe", lambda e: e.matmul(o, l, r, start=start, stop=stop), after)

        def tr(o, i, after=()):
            return P.op("pe", lambda e: e.matmul(o, i, c("ident")[0:i.shape[0], 0:i.shape[0]], is_transpose=True,
                                                 start=True, stop=True), after)

        def act(o, i, f, scale=1.0, bias=None, accum=None, after=()):
            kw = {}
            if bias is not None:
                kw["bias"] = bias
            if accum is not None:
                kw["accum_out"] = accum
            return P.op("act", lambda e: e.activation(o, i, f, scale=scale, **kw), after)

        def tt(e, o, a, b, op, after=()):
            return P.op(e, lambda g: g.tensor_tensor(o, a, b, op), after)

        def ts(e, o, a, s1, s2, op0, op1=None, after=()):
            if op1 is None:
                return P.op(e, lambda g: g.tensor_scalar(o, a, s1, None, op0), after)
            return P.op(e, lambda g: g.tensor_scalar(o, a, s1, s2, op0, op1), after)

        def stt(o, a, s, b, op0, op1, after=()):
            return P.op("dve", lambda g: g.scalar_tensor_tensor(o, a, s, b, op0, op1), after)

        def cp(e, o, a, after=()):
            if e == "act":
                return act(o, a, ACT.Copy, after=after)
            return P.op(e, lambda g: g.tensor_copy(o, a), after)

        def setv(e, o, x, after=()):
            return P.op(e, lambda g: g.memset(o, x), after)

        class Arena:
            def __init__(self, lo, hi):
                self.at, self.hi = lo, hi

            def take(self, n):
                assert self.at + n <= self.hi, (self.at, n, self.hi)
                a = A[:, self.at:self.at + n]
                self.at += n
                return a

        def t3(ap, n):
            return ap.rearrange("p (a b) -> p a b", a=n)

        Xt = t3(X[:, :], 8)
        HHt, HLt = t3(HH[:, :], 8), t3(HL[:, :], 8)

        t_const = [P.dma("act", C[:, :], I["c32"], "const"), P.dma("act", V[:, :], I["vecs"], "const"),
                   P.dma("act", A[:, 0:1792], I["m32"], "const")]
        for kt in range(8):
            t_const.append(P.dma("act", Xt[:, kt, :], I["x"][kt], "const"))
        t_const = t_const[-1]
        consts_at = t_const
        for e in ("pe", "act", "dve", "pool"):
            P.fence[e] = [t_const]
        eps = small[:, 0:1]
        halfpi = small[:, 1:2]
        gneps = small[:, 2:3]
        one_row = small[:, 3:4]
        cp("dve", M8[:, :], A[:, 0:1792])
        setv("pool", eps, 1e-6)
        setv("pool", gneps, 64e-5)
        setv("pool", one_row, 1.0)
        P.barrier()

        def stats(src, nt, width, scratch, rs, after=()):
            b = bank()
            t_mm = []
            for i in range(nt):
                q = scratch[:, (i % 2) * S:(i % 2 + 1) * S]
                ta = act(q, src[:, i, :], ACT.Square, after=(after, t_mm[i - 2] if i >= 2 else None))
                t_mm.append(mm(b.ap, c("ones"), q, i == 0, i == nt - 1, after=(ta, b.free if i == 0 else ())))
            ta = act(rs, b.ap, ACT.Sqrt, scale=1.0 / width, bias=eps, after=t_mm[-1])
            b.free = [ta]
            return P.op("dve", lambda g: g.reciprocal(rs, rs), ta)

        def rms(dst, src, nt, width, wname, scratch, rs, after=()):
            stats(src, nt, width, scratch, rs, after)
            for i in range(nt):
                t = stt(dst[:, i, :], src[:, i, :], v(wname, i), rs, ALU.mult, ALU.mult, after=after)
            return t

        def split(hi, lo, src, after=()):
            ta = act(hi, src, ACT.Copy, after=after)
            return tt("dve", lo, src, hi.bitcast(F32), ALU.subtract, after=ta)

        def rms_split(src, wname, scratch, rs, ready=False):
            if not ready:
                stats(src, 8, D, scratch, rs)
            tmp = [scratch[:, 0:S], scratch[:, S:2 * S]]
            ends, prev = [], None
            for i in range(9):
                if i < 8:
                    t = stt(tmp[i % 2], src[:, i, :], v(wname, i), rs, ALU.mult, ALU.mult)
                    ta = act(HHt[:, i, :], tmp[i % 2], ACT.Copy, after=t)
                if i:
                    ends.append(tt("dve", HLt[:, i - 1, :], tmp[(i - 1) % 2], HHt[:, i - 1, :].bitcast(F32),
                                   ALU.subtract, after=prev))
                prev = ta
            return ends

        def norm_ahead(sq, src=None):
            if src is not None:
                ahead.append(weights(src))
            P.flush()
            b = bank()
            for i, (x, after) in enumerate(((RS, sums["pool"]), (sq[:, 0:S], sums["last", 0]),
                                            (sq[:, S:2 * S], sums["last", 1]))):
                t = mm(b.ap, c("ones"), x, i == 0, i == 2, (after, b.free if i == 0 else ()))
            sums.clear()
            t = act(RS, b.ap, ACT.Sqrt, scale=1.0 / D, bias=eps, after=t)
            b.free = [t]
            P.op("dve", lambda g: g.reciprocal(RS, RS), t)

        ahead = []

        def residual(mt, sq=None):
            def f(m, ps, t):
                i = 2 * mt + m
                t = tt("dve", Xt[:, i, :], Xt[:, i, :], ps, ALU.add, after=t)
                if sq is not None:
                    q = sq[:, m * S:(m + 1) * S]
                    if i == 0:
                        sums["pool"] = act(RS, Xt[:, 0, :], ACT.Square, after=t)
                    else:
                        ta = act(q, Xt[:, i, :], ACT.Square, after=(t, sums.get(m)))
                        if i < 6:
                            sums["pool"] = sums[m] = tt("pool", RS, RS, q, ALU.add, after=(ta, sums["pool"]))
                        else:
                            sums["last", m] = ta
                return t
            return f

        sums, ready = {}, []

        def weights(src):
            s, tl = load(src)
            out = []
            for u in range(2):
                rm, lo = units[turn["unit"] % NUNIT]
                turn["unit"] += 1
                assert not rm.busy
                rm.busy = True
                t = split(rm.ap, lo, s.ap[:, u * UNIT:(u + 1) * UNIT], (tl, rm.free))
                out.append((rm, lo, t))
            s.free = [t]
            return out

        def products(o, wh, wl, xh, xl, first, last, after=()):
            mm(o, wh, xh, first, False, after)
            mm(o, wh, xl, False, False)
            return mm(o, wl, xh, False, last)

        def lin_steps(chunks, act_of, nc_, kts, evac, after=(), cost=2.6):
            per, ku = nc_ // 128, kts // 2
            us = ahead.pop() if ahead else weights(chunks[0])
            P.flush()
            bs = [bank() for _ in range(per)]
            for j in range(len(chunks)):
                us = us if j == 0 else weights(chunks[j])
                for u, (rm, lo, tw_) in enumerate(us):
                    for m in range(per):
                        for k in range(ku):
                            cs_ = slice(k * nc_ + m * 128, k * nc_ + (m + 1) * 128)
                            kt = j * kts + u * ku + k
                            xh, xl = act_of(kt)
                            f_ = j + u + k == 0
                            t = products(bs[m].ap, rm.ap[:, cs_], lo[:, cs_], xh, xl, f_,
                                         j == len(chunks) - 1 and u == 1 and k == ku - 1,
                                         (tw_, after(kt) if callable(after) else after, bs[m].free if f_ else ()))
                        if m < per - 1:
                            yield cost
                    rm.free = [t]
                    if u == 0 or j < len(chunks) - 1:
                        yield cost

            def out_():
                for m in range(per):
                    bs[m].free = [evac(m, bs[m].ap, t)]

            P.pend.append(out_)
            yield cost

        def lin(*a, **kw):
            for _ in lin_steps(*a, **kw):
                pass

        def lin_rows(src, act_of, dst, eng):
            us = weights(src)
            P.flush()
            for tk in range(4):
                b = bank()
                for u, (rm, lo, tw_) in enumerate(us):
                    for k in range(4):
                        xh, xl = (x[:, tk * 128:(tk + 1) * 128] for x in act_of(u * 4 + k))
                        wh, wl = rm.ap[:, k * 256:(k + 1) * 256], lo[:, k * 256:(k + 1) * 256]
                        o = b.ap[:, 0:256]
                        mm(o, xh, wh, u + k == 0, False, (tw_, b.free))
                        mm(o, xl, wh, False, False)
                        t = mm(o, xh, wl, False, u == 1 and k == 3)

                def out_(b=b, tk=tk, t=t):
                    b.free = [cp(eng, dst[:, tk, :], b.ap[:, 0:256], after=t)]

                if tk < 3:
                    out_()
                else:
                    P.pend.append(out_)
            for rm, _, _ in us:
                rm.free = [t]

        def lin32(chunks, act_of, nc_, kts, evac, after=()):
            per = nc_ // 128
            bs = [bank() for _ in range(per)]
            for j, src in enumerate(chunks):
                s, tl = load(src)
                for m in range(per):
                    for kt in range(kts):
                        t = mm(bs[m].ap, s.ap[:, kt * nc_ + m * 128:kt * nc_ + (m + 1) * 128], act_of(j * kts + kt),
                               j == 0 and kt == 0, j == len(chunks) - 1 and kt == kts - 1,
                               after=(tl, after, bs[m].free if j == 0 and kt == 0 else ()))
                s.free = [t]
                if j < len(chunks) - 1:
                    continue
                for m in range(per):
                    bs[m].free = [evac(m, bs[m].ap, t)]

        def lin_tok(s, tl, off, width, kts, nc_, act_of, dst, eng, after=()):
            for tk in range(4):
                b = bank()
                for kt in range(kts):
                    t = mm(b.ap[:, 0:width], act_of(kt)[:, tk * 128:(tk + 1) * 128],
                           s.ap[:, kt * nc_ + off:kt * nc_ + off + width], kt == 0, kt == kts - 1,
                           after=(tl, after, b.free if kt == 0 else ()))
                b.free = [cp(eng, dst[:, tk, :], b.ap[:, 0:width], after=t)]
            return t, b.free

        def tables(pos, invf, cosT, sinT, ar):
            pi = ar.take(S)
            ang, n, r = ar.take(S), ar.take(S), ar.take(S)
            tp = P.dma("act", pi.bitcast(I32), pos.partition_broadcast(128), "const", after=P.barrier())
            cp("dve", ang, pi.bitcast(I32), after=tp)
            ts("dve", ang, ang, invf, None, ALU.mult)
            MAG = 12582912.0
            for dst, q in ((sinT, 0.0), (cosT, 0.25)):
                ts("dve", n, ang, float(1 / (2 * np.pi)), float(q), ALU.mult, ALU.add)
                ts("dve", n, n, MAG, None, ALU.add)
                ts("dve", n, n, MAG, None, ALU.subtract)
                C1 = 6.28125
                C2 = float(np.float32(2 * np.pi - C1))
                C2 = float(np.float32(np.round(C2 * 2 ** 20) / 2 ** 20))
                C3 = float(2 * np.pi - C1 - C2)
                stt(r, n, -C1, ang, ALU.mult, ALU.add)
                stt(r, n, -C2, r, ALU.mult, ALU.add)
                stt(r, n, -C3, r, ALU.mult, ALU.add)
                if q:
                    ts("dve", r, r, float(np.pi / 2), None, ALU.add)
                t = ts("dve", r, r, 3.1415925, -3.1415925, ALU.min, ALU.max)
                t2 = act(dst, r, ACT.Sin, after=t)
                P.fence["dve"] = [t2]
            return t2

        def attention(ar, nh, scores, mask_of, klen, vtok, dst_evac, spare=(), pts=()):
            NS = 4
            Sb = list(spare) + [ar.take(S) for _ in range(NS - len(spare))]
            NP = 3
            PT = list(pts) or [ar.take(S) for _ in range(NP)]
            ms, rs_, ris = (ar.take(32) for _ in range(3))
            t_exp, t_nrm, t_tr, t_pt, t_pv = {}, {}, {}, {}, {}
            out_ = {}

            def col(x, i):
                return x[:, i % 32:i % 32 + 1]

            def first(i):
                h, qt = divmod(i, 4)
                kl = klen(qt)
                b = bank()
                t = scores(h, b.ap[:, 0:kl], qt, kl, b.free)
                t = mask_of(b.ap, Sb[i % NS][:, 0:kl], col(ms, i), qt, kl, (t, t_tr.get(i - NS)))
                b.free = [t]
                t_exp[i] = act(Sb[i % NS][:, 0:kl], Sb[i % NS][:, 0:kl], ACT.Exp, scale=-1.0, bias=col(ms, i),
                               accum=col(rs_, i), after=t)

            def second(i):
                kl = klen(i % 4)
                x = Sb[i % NS][:, 0:kl]
                ri, r_ = col(ris, i), col(rs_, i)
                P.op("dve", lambda g: g.reciprocal(ri, r_), t_exp[i])
                t_nrm[i] = ts("dve", x, x, ri, None, ALU.mult)

            def third(i):
                n = klen(i % 4) // 128
                x = Sb[i % NS]
                b = bank()
                for k in range(n):
                    t = tr(b.ap[:, k * 128:(k + 1) * 128], x[:, k * 128:(k + 1) * 128], after=(t_nrm[i], b.free))
                t_tr[i] = t
                t_pt[i] = cp("act" if i % 2 else "dve", PT[i % NP][:, 0:n * 128], b.ap[:, 0:n * 128],
                             after=(t, t_pv.get(i - NP)))
                b.free = [t_pt[i]]

            def values(i):
                h, qt = divmod(i, 4)
                if i % 8 == 0:
                    out_[0] = bank(hold=True)
                bo = out_[0]
                o = bo.ap[64 * (h % 2):64 * (h % 2) + 64, qt * 128:(qt + 1) * 128]
                n = klen(qt) // 128
                for k in range(n):
                    t = mm(o, vtok(h, k), PT[i % NP][:, k * 128:(k + 1) * 128], k == 0, k == n - 1,
                           after=(t_pt[i], bo.free if i % 8 == 0 else ()))
                t_pv[i] = t
                if i % 8 == 7:
                    bo.free = [dst_evac(h // 2, bo.ap, t)]
                    release(bo)

            n = 4 * nh
            for i in range(n + 3):
                if i < n:
                    first(i)
                if 1 <= i <= n:
                    second(i - 1)
                if 2 <= i < n + 2:
                    third(i - 2)
                if i >= 3:
                    values(i - 3)
                yield 2.3

        LC = 3.4
        cos64, sin64 = TAB[:, 0:S], TAB[:, S:2 * S]

        lbv = t3(v("lb", 0, 8), 2)
        lm, le0, le1, ls = (small[:, 112 + 4 * i:116 + 4 * i] for i in range(4))
        lbs = [small[:, 128:132], small[:, 132:136]]
        oml = [small[:, 136:140], small[:, 140:144]]
        tt("dve", lm, lbv[:, 0, :], lbv[:, 1, :], ALU.max)
        tt("dve", le0, lbv[:, 0, :], lm, ALU.subtract)
        t = tt("dve", le1, lbv[:, 1, :], lm, ALU.subtract)
        act(le0, le0, ACT.Exp, after=t)
        t = act(le1, le1, ACT.Exp)
        tt("dve", ls, le0, le1, ALU.add, after=t)
        P.op("dve", lambda g: g.reciprocal(ls, ls))
        tt("dve", le0, le0, ls, ALU.mult)
        tt("dve", le1, le1, ls, ALU.mult)
        tt("dve", lbs[0], le0, le0, ALU.subtract)
        tt("dve", lbs[1], le0, le1, ALU.add)
        tt("dve", lbs[1], lbs[1], le0, ALU.subtract)
        for i in range(2):
            ts("dve", oml[i], lbs[i], -1.0, 1.0, ALU.mult, ALU.add)
        P.barrier()

        for layer in range(2):
            phase(f"mix{layer}", 25216)
            ar = Arena(0, 25216)
            scratch, rs = ar.take(2 * S), RS
            if layer == 0:
                ahead.append(weights(I["w_in"][0][2, 0]))
            ends = rms_split(Xt, f"an{layer}", scratch, rs, layer > 0)
            if stop == f"norm{layer}":
                break
            t_h = lambda kt: ends[kt]
            aq, ai, k2 = ar.take(2 * S), ar.take(4 * 256), ar.take(4 * S)
            ag, L, oc = ar.take(2 * S), ar.take(4 * S), None
            u, cq, ck, cv = ar.take(4 * 256), ar.take(4 * S), ar.take(4 * S), ar.take(4 * S)
            aq3, k3, L3, ag3 = t3(aq, 2), t3(k2, 4), t3(L, 4), t3(ag, 2)
            ai3, u3, cq3, ck3, cv3 = t3(ai, 4), t3(u, 4), t3(cq, 4), t3(ck, 4), t3(cv, 4)
            W = I["w_in"][layer]
            h_of = lambda kt: (HHt[:, kt, :], HLt[:, kt, :])
            tmp_at = ar.at
            sg = [scratch[:, 0:S], scratch[:, S:2 * S]]
            sgt = [[], []]

            def ev_silu(dst):
                def f(m, ps, t):
                    ta = act(sg[m], ps, ACT.Sigmoid, after=(t, sgt[m]))
                    t = tt("dve", dst[:, m, :], ps, sg[m], ALU.mult, after=ta)
                    sgt[m] = [t]
                    return t
                return f

            def ev_gate(dr):
                def f(m, ps, t):
                    j = dr * 2 + m
                    ta = act(sg[m], ps, ACT.Sigmoid, after=(t, sgt[m]))
                    ts("dve", sg[m], sg[m], oml[layer][:, j:j + 1], lbs[layer][:, j:j + 1], ALU.mult, ALU.add,
                       after=ta)
                    ts("dve", k3[:, j, :], sg[m], -1.0, 1.0, ALU.mult, ALU.add)
                    t = ts("dve", L3[:, j, :], sg[m], 2.0 ** -63, None, ALU.max)
                    sgt[m] = [t]
                    return ta
                return f

            for dr in range(2):
                lin([W[2 + dr, 0]], h_of, 256, 8, ev_gate(dr), after=t_h)
            lin([W[0, 0]], h_of, 256, 8, ev_silu(aq3))
            lin([W[4, 0]], h_of, 256, 8, ev_silu(ag3))
            lin_rows(W[1, 0], h_of, ai3, "act")

            def ev_copy(dst, base):
                return lambda m, ps, t: cp("act", dst[:, base + m, :], ps, after=t)

            oab = k2[:, 0:2 * S]

            def recurrence():
                act(L, L, ACT.Ln, after=P.last("dve"))
                B = ar.take(4 * 516)
                B3 = B.rearrange("p (g j) -> p g j", j=129)
                E, Kls, Qls = L[:, 0:2 * S], (L[:, 2 * S:4 * S], ar.take(2 * S)), (rs, ar.take(S))
                Kt, Sc = ar.take(2 * S), ar.take(4 * S)
                St, dec = ar.take(4 * 2 * 64), small[:, 160:168]
                setv("pool", B3[:, :, 0:1], 0.0)
                ones_b = c("ones")
                t_b = (P.last("pool"), P.last("act"))
                for g in range(16):
                    j, ch = g // 4, g % 4
                    t_b = P.op("dve", lambda e, g=g, j=j, ch=ch, B3=B3, L3=L3: e.tensor_tensor_scan(
                        B3[:, g, 1:129], ones_b, L3[:, j, ch * 128:(ch + 1) * 128], 0.0, ALU.mult, ALU.add), after=t_b)
                yield 12.0
                P.barrier()
                q8 = aq.rearrange("p (g t) -> p g t", t=128)
                E8 = E.rearrange("p (g t) -> p g t", t=128)
                ob = [bank(hold=True) for _ in range(2)]
                t_o = None
                for dr in range(2):
                    k8 = k2[:, dr * 2 * S:(dr + 1) * 2 * S].rearrange("p (g t) -> p g t", t=128)
                    Bd = B3[:, dr * 8:dr * 8 + 8, :]
                    sh = 1 - dr
                    ml = lambda l: M8[:, (dr * 7 + l) * 128:(dr * 7 + l + 1) * 128]

                    def halves(ap, l, second, lo=0):
                        w = 2 ** l
                        return ap[:, :, lo:lo + 128].rearrange("p g (n two w) -> p g n two w", two=2, w=w)[
                            :, :, :, 1 if second else 0, :]

                    def decayed(l):
                        w = 2 ** l
                        K_, Q_ = Kls[l % 2], Qls[l % 2]
                        mid = Bd[:, :, w:w + 128 - 2 * w + 1:2 * w] if l < 6 else Bd[:, :, 64:65]
                        mid = bcast(mid, 3, w)
                        tt("dve", halves(E8, l, False), mid, halves(Bd, l, False, sh), ALU.subtract,
                           after=P.last("pool"))
                        t = tt("dve", halves(E8, l, True), halves(Bd, l, True, sh), mid, ALU.subtract)
                        t_e = act(E, E, ACT.Exp, after=t)
                        t_k = tt("pool", K_, E, k2[:, dr * 2 * S:(dr + 1) * 2 * S], ALU.mult,
                                 after=(t_e, t_use.get(l - 2)))
                        t_q = tt("dve", Q_.rearrange("p (g n w) -> p g n w", g=8, w=w), halves(q8, l, dr == 0),
                                 halves(E8, l, dr == 0), ALU.mult, after=(t_e, t_use.get(l - 2)))
                        return t_k, t_q

                    t_use = {-2: t_o, -1: t_o}
                    ready = {-1: t_b}
                    for l in range(-1, 7):
                        if l < 6:
                            ready[l + 1] = decayed(l + 1)
                            yield 5.0
                        n = 64 if l >= 0 else 128
                        for h in range(4):
                            hp, lo = h // 2, 64 * (h % 2)
                            b = bank()
                            for ch in range(4):
                                if l >= 0:
                                    kk = Kls[l % 2][lo:lo + 64, (hp * 4 + ch) * 128:(hp * 4 + ch + 1) * 128]
                                    qq = Qls[l % 2][lo:lo + 64, (hp * 4 + ch) * 64:(hp * 4 + ch + 1) * 64]
                                else:
                                    kk, qq = k8[lo:lo + 64, hp * 4 + ch, :], q8[lo:lo + 64, hp * 4 + ch, :]
                                t = mm(b.ap[:, ch * n:(ch + 1) * n], kk, qq, after=(ready[l], b.free))
                            if l < 0:
                                t = tt("dve", t3(Sc[:, h * S:(h + 1) * S], 4), t3(b.ap, 4),
                                       bcast(c("ident"), 1, 4), ALU.mult, after=(t, t_o))
                            else:
                                w = 2 ** l
                                f = lambda ap, nc4: ap.rearrange("p (c n two w) -> p c n two w", c=nc4, two=2, w=w)[
                                    :, :, :, 1 if dr == 0 else 0, :]
                                o_, m_ = f(Sc[:, h * S:(h + 1) * S], 4), bcast(f(ml(l), 1).squeeze(1), 1, 4)
                                d_ = b.ap[:, 0:256].rearrange("p (c n w) -> p c n w", c=4, w=w)
                                t = P.op("dve", lambda g, o_=o_, m_=m_, d_=d_: g.copy_predicated(o_, m_, d_), t)
                            b.free = [t]
                        t_use[l] = P.last("pe")
                        yield 4.0
                    t_o = P.last("pe")
                    Kl, Kl8 = Kls[1], Kls[1].rearrange("p (g t) -> p g t", t=128)
                    t_sc = P.last("dve")
                    tot = bcast(Bd[:, :, 128:129].squeeze(2), 2, 128)
                    fl = (Bd[:, :, 1:129], Bd[:, :, 0:128])
                    if dr == 0:
                        t = tt("dve", E8, tot, fl[0], ALU.subtract)
                        t_e = act(E, E, ACT.Exp, after=t)
                    else:
                        t_e = act(E8, fl[1], ACT.Exp, after=P.last("dve"))
                    t_k = tt("pool", Kl, E, k2[:, dr * 2 * S:(dr + 1) * 2 * S], ALU.mult, after=(t_e, t_o))
                    t_dec = act(dec, Bd[:, :, 128:129].squeeze(2), ACT.Exp)
                    if dr == 0:
                        t_e = act(E8, fl[0], ACT.Exp, after=t_k)
                    else:
                        t = tt("dve", E8, tot, fl[1], ALU.subtract, after=t_k)
                        t_e = act(E, E, ACT.Exp, after=t)
                    t_q = tt("dve", E, E, aq, ALU.mult, after=t_e)
                    yield 5.0
                    for hp in range(2):
                        b = bank()
                        for ch in range(4):
                            t = tr(b.ap[:, ch * 128:(ch + 1) * 128], Kl8[:, hp * 4 + ch, :], after=(t_k, b.free))
                        b.free = [cp("act", Kt.rearrange("p (c a f) -> p a c f", c=4, a=2)[:, hp], t3(b.ap, 4), after=t)]
                    t_kt = P.last("act")
                    St4 = St.rearrange("p (c a f) -> p c a f", c=4, a=2)
                    order = [0, 1, 2, 3] if dr == 0 else [3, 2, 1, 0]
                    b = bank()
                    for ch in order[:3]:
                        for h in range(4):
                            hp, lo = h // 2, 64 * (h % 2)
                            t = mm(b.ap[lo:lo + 64, (ch * 2 + hp) * 64:(ch * 2 + hp + 1) * 64],
                                   Kt[:, (ch * 2 + hp) * 128 + lo:(ch * 2 + hp) * 128 + lo + 64],
                                   ai3[:, ch, h * 64:(h + 1) * 64], after=(t_kt, b.free))
                    bs = b.ap.rearrange("p (c a f) -> p c a f", c=4, a=2)
                    t = cp("dve", St4[:, order[1]], bs[:, order[0]], after=(t, t_dec))
                    for i in (1, 2):
                        for hp in range(2):
                            t = stt(St4[:, order[i + 1], hp, :], St4[:, order[i], hp, :],
                                    dec[:, hp * 4 + order[i]:hp * 4 + order[i] + 1], bs[:, order[i], hp, :],
                                    ALU.mult, ALU.add)
                    b.free = [t]
                    t_st = t
                    yield 3.0
                    for hp in range(2):
                        for hh in range(2):
                            h, lo = hp * 2 + hh, 64 * hh
                            for ch in range(4):
                                cs = slice(ch * 128, (ch + 1) * 128)
                                inter = ch != order[0]
                                o_ = ob[hp].ap[lo:lo + 64, cs]
                                t = mm(o_, ai3[:, ch, h * 64:(h + 1) * 64],
                                       Sc[:, h * S + ch * 128:h * S + (ch + 1) * 128], True, not inter,
                                       after=(t_sc, t_st, t_q, ob[hp].free))
                                if inter:
                                    t = mm(o_, St4[lo:lo + 64, ch, hp, :], E8[lo:lo + 64, hp * 4 + ch, :], False, True)
                    t_o = t
                    if dr == 0:
                        ar_o = [oab[:, 0:S], oab[:, S:2 * S]]
                        for hp in range(2):
                            ob[hp].free = [cp("act", ar_o[hp], ob[hp].ap, after=t)]
                    else:
                        for hp in range(2):
                            t = tt("dve", ar_o[hp], ar_o[hp], ob[hp].ap, ALU.add, after=t_o)
                            ob[hp].free = [t]
                            release(ob[hp])
                    P.barrier()
                    yield 4.0
                for hp in range(2):
                    sq, r_ = E[:, 0:S], E[:, S:2 * S]
                    t = act(sq, ar_o[hp], ACT.Square, after=P.last("dve"))
                    b = bank()
                    t = mm(b.ap, c("ones64"), sq, after=(t, b.free))
                    t = act(r_, b.ap, ACT.Sqrt, scale=1.0 / 64, bias=eps, after=t)
                    b.free = [t]
                    P.op("dve", lambda g, r_=r_: g.reciprocal(r_, r_), t)
                    tt("dve", r_, r_, ar_o[hp], ALU.mult)
                    t = tt("dve", ar_o[hp], r_, ag3[:, hp, :], ALU.mult)
                    P.fence["act"] = [t]
                P.barrier()


            def windows():
                for j in range(2):
                    yield from lin_steps([W[6 + j, 0]], h_of, 256, 8, ev_copy(cq3, 2 * j), cost=LC)
                for j in range(2):
                    yield from lin_steps([W[8 + j, 0]], h_of, 256, 8, ev_copy(ck3, 2 * j), cost=LC)
                lin_rows(W[5, 0], h_of, u3, "act")
                yield 4 * LC
                for j in range(2):
                    lin_rows(W[10 + j, 0], h_of, cv3[:, :, 256 * j:256 * j + 256], "act")
                    yield 4 * LC
                w_at = ar.at
                P.barrier()
                bre, bim = [bank() for _ in range(2)], [bank() for _ in range(2)]
                us = [ar.take(S) for _ in range(4)]
                for part, bs in ((0, bre), (1, bim)):
                    s, tl = load(I["dft"][part])
                    for dt_ in range(2):
                        for k in range(4):
                            t = mm(bs[dt_].ap, u3[:, k, dt_ * 128:(dt_ + 1) * 128], s.ap[:, k * S:(k + 1) * S],
                                   k == 0, k == 3, after=(tl, bs[dt_].free))
                        bs[dt_].free = [cp("act", us[part * 2 + dt_], bs[dt_].ap, after=t)]
                    s.free = [t]
                    yield 7.0
                for dt_ in range(2):
                    b = bank()
                    mm(b.ap, c("cd"), us[dt_], True, False, after=(bre[dt_].free, b.free))
                    t = mm(b.ap, c("sd"), us[2 + dt_], False, True, after=bim[dt_].free)
                    b.free = [split(HHt[:, 2 + dt_, :], HLt[:, 2 + dt_, :], b.ap, t)]
                P.barrier()
                ar.at = w_at
                if layer == 0:
                    tables(I["pos1"], c("invf64"), cos64, sin64, ar)
                    P.barrier()
                    ar.at = w_at
                    yield 12.0
                rt = [ar.take(S) for _ in range(2)]
                rtt = [[], []]
                n = 0
                for src in (cq3, ck3):
                    for m in range(4):
                        b = bank()
                        t = mm(b.ap, c("rot64"), src[:, m, :], after=b.free)
                        t = tt("dve", rt[n % 2], b.ap, sin64, ALU.mult, after=(t, rtt[n % 2]))
                        b.free = [t]
                        t2 = tt("pool", src[:, m, :], src[:, m, :], cos64, ALU.mult, after=P.last("pe"))
                        t = tt("dve", src[:, m, :], src[:, m, :], rt[n % 2], ALU.add, after=t2)
                        n += 1
                    yield 6.0
                t_rot = P.last("dve")
                P.barrier()
                ar.at = w_at

                def scores(h, o, qt, kl, after):
                    hp, lo = h // 2, 64 * (h % 2)
                    return mm(o, cq3[lo:lo + 64, hp, qt * 128:(qt + 1) * 128], ck3[lo:lo + 64, hp, :],
                              after=(after, t_rot))

                def mask(ps, Sb, m, qt, kl, after):
                    tm = c("tmask")[:, (3 - qt) * 128:(3 - qt) * 128 + S]
                    return P.op("dve", lambda g: g.tensor_tensor_reduce(
                        Sb, ps[:, 0:kl], tm, -0.125, 3.0e38, ALU.add, ALU.min, m), after)

                yield from attention(ar, 8, scores, mask, lambda qt: S, lambda h, k: cv3[:, k, h * 64:(h + 1) * 64],
                                     lambda hp, ps, t: split(HHt[:, 4 + hp, :], HLt[:, 4 + hp, :], ps, t), (u[:, 0:S], u[:, S:2 * S]))

            P.streams(recurrence(), windows())
            for hp in range(2):
                split(HHt[:, hp, :], HLt[:, hp, :], oab[:, hp * S:(hp + 1) * S])
            P.barrier()
            if stop == f"mix{layer}":
                break

            for j in range(4):
                lin([I["w_out"][layer][j, 0]], h_of, 256, 8, residual(j, scratch))
            norm_ahead(scratch, I["w_up"][layer][0, 0])
            if stop == f"res{layer}":
                break

            phase(f"ffn{layer}", 5 * S, 32 * S, extra=2)
            ar = Arena(0, 5 * S)
            scratch, rs = ar.take(2 * S), RS
            hh, hl = t3(R[:, 0:16 * S], 16), t3(R[:, 16 * S:32 * S], 16)
            rl = [ar.take(S) for _ in range(2)]
            rlt = [[], []]
            ends = rms_split(Xt, f"mn{layer}", scratch, rs, True)
            t_h = lambda kt: ends[kt]

            def ev_hid(j):
                def f(m, ps, t):
                    ta = act(rl[m], ps, ACT.Relu, after=(t, rlt[m]))
                    t = tt("dve", rl[m], rl[m], rl[m], ALU.mult, after=ta)
                    rlt[m] = [split(hh[:, 2 * j + m, :], hl[:, 2 * j + m, :], rl[m], (t, t_down))]
                    return ta
                return f

            t_down = None
            for half in range(2):
                for j in range(8):
                    lin([I["w_up"][layer][8 * half + j, 0]], h_of, 256, 8, ev_hid(j), after=t_h)
                P.flush()
                t_hid = P.last("dve")
                for j in range(4):
                    lin([I["w_down"][layer][j, 2 * half + k] for k in range(2)],
                        lambda kt: (hh[:, kt, :], hl[:, kt, :]), 256, 8, residual(j, scratch if half else None), after=t_hid)
                t_down = P.last("pe")
            norm_ahead(scratch, I["w_in"][1][2, 0] if layer == 0 else None)
            if stop == f"ffn{layer}":
                break
        else:
            phase("second", 25344)
            ar = Arena(0, 25344)
            for i in range(8):
                stt(Xt[:, i, :], Xt[:, i, :], v("fn1", i), RS, ALU.mult, ALU.mult)
            P.barrier()
            if stop != "b1":
                cos32, sin32 = TAB[:, 0:S], TAB[:, S:2 * S]
                ar = Arena(0, 25344)
                yrw, ymla = t3(ar.take(4 * S), 4), None
                rw_at = ar.at
                ahead.append(weights(I["w_in2"][0, 0]))
                ar.at = ar.hi - 2 * S
                ends = rms_split(Xt, "mixg", ar.take(2 * S), RS)
                t_h = lambda kt: ends[kt]
                ar.at = rw_at
                h_of = lambda kt: (HHt[:, kt, :], HLt[:, kt, :])
                W2 = I["w_in2"]

                sgd = ar.take(S)
                Z = t3(ar.take(12 * S), 12)
                zr, zk, zv = Z[:, 0:4], Z[:, 4:8], Z[:, 8:12]
                aa, kkv = t3(ar.take(4 * S), 4), t3(ar.take(4 * S), 4)
                keep_at = ar.at
                cb = [ar.take(S + 1) for _ in range(2)]
                df = [ar.take(S) for _ in range(2)]
                zwa = ar.take(S)
                for m in range(2):
                    setv("pool", cb[m][:, 0:1], 0.0)
                t_z0 = P.last("pool")
                cbt = [[], []]

                def ev_shift(j):
                    def f(m, ps, t):
                        i = 2 * j + m
                        dst = Z[:, i, :] if i < 12 else (zwa if i == 12 else sgd)
                        ta = cp("act", cb[m][:, 1:S + 1], ps, after=(t, cbt[m]))
                        tt("dve", df[m], cb[m][:, 0:S], cb[m][:, 1:S + 1], ALU.subtract, after=(ta, t_z0))
                        t = stt(dst, df[m], v("mu", i), cb[m][:, 1:S + 1], ALU.mult, ALU.add)
                        cbt[m] = [t]
                        return ta
                    return f

                for j in range(7):
                    lin([W2[j, 0]], h_of, 256, 8, ev_shift(j), after=t_h if j == 0 else ())
                P.flush()
                t_z = P.last("dve")
                def rwkv():
                    act(zwa[0:64, :], zwa[0:64, :], ACT.Tanh, after=t_z)
                    t_wa = act(sgd, sgd, ACT.Sigmoid)
                    Bw = ar.take(4 * 516)
                    E1, E2 = ar.take(4 * 516), ar.take(4 * 516)
                    sgw = [df[0], df[1]]
                    B3, E13, E23 = (x.rearrange("p (g j) -> p g j", j=129) for x in (Bw, E1, E2))
                    setv("pool", B3[:, :, 0:1], 0.0)
                    t_b0 = P.last("pool")
                    s, tl = load(I["wa_up"])
                    sct = [[], []]
                    for j in range(4):
                        b = bank()
                        t = mm(b.ap, s.ap[0:64, j * 128:(j + 1) * 128], zwa[0:64, :], after=(tl, t_wa, b.free))
                        ta = act(sgw[j % 2], b.ap, ACT.Sigmoid, bias=v("w0", j), after=(t, sct[j % 2]))
                        b.free = [ta]
                        for ch in range(4):
                            t = P.op("dve", lambda e, j=j, ch=ch: e.tensor_tensor_scan(
                                B3[:, j * 4 + ch, 1:129], c("ones"), sgw[j % 2][:, ch * 128:(ch + 1) * 128], 0.0,
                                ALU.mult, ALU.add), after=(ta, t_b0))
                        sct[j % 2] = [t]
                        yield 3.0
                    for j in range(4):
                        b = bank()
                        t = mm(b.ap, s.ap[64:128, j * 128:(j + 1) * 128], zwa[64:128, :], after=b.free)
                        b.free = [act(aa[:, j, :], b.ap, ACT.Sigmoid, bias=v("a0", j), after=t)]
                    s.free = [t]
                    t_aa = P.last("act")
                    for j in range(4):
                        ts("dve", kkv[:, j, :], zk[:, j, :], v("kk", j), None, ALU.mult)
                        t = tt("dve", df[0], kkv[:, j, :], kkv[:, j, :], ALU.mult, after=t_aa)
                        b = bank()
                        t = mm(b.ap, c("ones64"), df[0], after=(t, b.free))
                        t = act(df[1], b.ap, ACT.Sqrt, after=t)
                        b.free = [t]
                        ts("dve", df[1], df[1], 1e-12, None, ALU.max, after=t)
                        P.op("dve", lambda g: g.reciprocal(df[1], df[1]))
                        tt("dve", kkv[:, j, :], kkv[:, j, :], df[1], ALU.mult)
                        ts("dve", df[0], aa[:, j, :], -1.0, v("ka", j), ALU.add, ALU.mult)
                        stt(zk[:, j, :], df[0], 1.0, zk[:, j, :], ALU.add, ALU.mult)
                        stt(aa[:, j, :], kkv[:, j, :], -1.0, aa[:, j, :], ALU.mult, ALU.mult)
                        yield 8.0
                    LD = float(-np.exp(-0.5))
                    midc = small[:, 160:176]
                    cp("dve", midc, B3[:, :, 64:65].squeeze(2))
                    t = tt("dve", B3, B3, bcast(midc, 2, 129), ALU.subtract)
                    act(E1, Bw, ACT.Exp, scale=LD, after=t)
                    t_e = act(E2, Bw, ACT.Exp, scale=-LD)
                    sp = lambda x: x.rearrange("p a (c t) -> p (a c) t", c=4)
                    tt("dve", sp(zr), sp(zr), E13[:, :, 1:129], ALU.mult, after=t_e)
                    tt("dve", sp(kkv), sp(kkv), E13[:, :, 0:128], ALU.mult)
                    tt("dve", sp(zk), sp(zk), E23[:, :, 1:129], ALU.mult)
                    tt("dve", sp(aa), sp(aa), E23[:, :, 1:129], ALU.mult)
                    e_in, e_out, e_all = small[:, 176:192], small[:, 192:208], small[:, 208:224]
                    cp("dve", e_in, E23[:, :, 0:1].squeeze(2))
                    cp("dve", e_out, E13[:, :, 128:129].squeeze(2))
                    tt("dve", e_all, e_in, e_out, ALU.mult)
                    yield 15.0
                    P.barrier()

                    ar.at = keep_at
                    tok = [ar.take(S) for _ in range(3)]
                    G = []
                    for g in range(2):
                        G.append({n: ar.take(S) for n in ("AT", "X", "XT", "T1", "ak", "rb", "rk")})
                    rhs, sa = ar.take(S), ar.take(S)
                    St, S0 = ar.take(256), ar.take(256)
                    St3, S03 = t3(St, 4), t3(S0, 4)
                    tmp = rhs[:, 0:256]
                    setv("pool", St, 0.0)
                    t_s = P.last("pool")
                    eq = lambda x, ch: x.rearrange("p (a c) -> p a c", c=4)[:, :, ch]
                    done = []
                    for ch in range(4):
                        cs = slice(ch * 128, (ch + 1) * 128)
                        for i, src in enumerate((aa, zk, zv)):
                            b = bank()
                            for j in range(4):
                                t = tr(b.ap[:, j * 128:(j + 1) * 128], src[:, j, cs], after=(b.free, done))
                            b.free = [cp("act", tok[i], b.ap, after=(t, done))]
                        t_tok = P.last("act")

                        def pairs(g, l, r, after):
                            b = bank()
                            for i in range(4):
                                j, lo = i, 64 * g
                                t = mm(b.ap[:, i * 128:(i + 1) * 128], l[lo:lo + 64, j, cs], r[lo:lo + 64, j, cs],
                                       after=(after, b.free))
                            return b, t

                        def masked(o, b, t, name, after):
                            b.free = [tt("dve", t3(o, 4), t3(b.ap, 4), bcast(c(name), 1, 4), ALU.mult, after=(t, after))]

                        def pred(o, l, ps, t):
                            return P.op("dve", lambda e: e.copy_predicated(
                                t3(o, 4), bcast(M8[:, l * 128:(l + 1) * 128], 1, 4), t3(ps, 4)), t)

                        for g in range(2):
                            g_ = G[g]
                            b, t = pairs(g, aa, kkv, done)
                            masked(g_["AT"], b, t, "strict", done)
                            cp("dve", t3(g_["XT"], 4), bcast(c("ident"), 1, 4))
                            pred(g_["XT"], 0, b.ap, None)
                            b.free = [P.last("dve")]
                            b, t = pairs(g, kkv, aa, done)
                            cp("dve", t3(g_["X"], 4), bcast(c("ident"), 1, 4))
                            b.free = [pred(g_["X"], 7, b.ap, t)]
                            for name, l, r, mk in (("ak", zk, kkv, "strict"), ("rb", aa, zr, "incl"), ("rk", zk, zr, "incl")):
                                b, t = pairs(g, l, r, done)
                                masked(g_[name], b, t, mk, done)
                        tx = [P.last("dve")] * 2
                        yield 4.0
                        for l in range(1, 7):
                            t1 = [None, None]
                            for g in range(2):
                                g_ = G[g]
                                b = bank()
                                for i in range(4):
                                    k = slice(i * 128, (i + 1) * 128)
                                    t = mm(b.ap[:, k], g_["AT"][:, k], g_["X"][:, k], after=(tx[g], b.free))
                                b.free = [cp("act", g_["T1"], b.ap, after=t)]
                                t1[g] = b.free
                            for g in range(2):
                                g_ = G[g]
                                b2 = bank()
                                for i in range(4):
                                    k = slice(i * 128, (i + 1) * 128)
                                    t2 = mm(b2.ap[:, k], g_["T1"][:, k], g_["XT"][:, k], after=(t1[g], b2.free))
                                if l < 6:
                                    b = bank()
                                    for i in range(4):
                                        k = slice(i * 128, (i + 1) * 128)
                                        t = mm(b.ap[:, k], g_["XT"][:, k], g_["T1"][:, k], after=(t1[g], b.free))
                                    b.free = [pred(g_["X"], 7 + l, b.ap, t)]
                                b2.free = [pred(g_["XT"], l, b2.ap, (t2, t if l < 6 else None))]
                                tx[g] = b2.free
                            yield 2.5
                        t_s0 = tt("dve", S03, St3, bcast(eq(e_in, ch), 2, 64), ALU.mult, after=(t_s, done))
                        t_r = []
                        for g in range(2):
                            b = bank()
                            lo = 64 * g
                            for j in range(4):
                                h, k = 2 * j + g, slice(j * 128, j * 128 + 128)
                                o = b.ap[:, j * 64:(j + 1) * 64]
                                mm(o, G[g]["ak"][:, k], tok[2][:, h * 64:(h + 1) * 64], True, False,
                                   after=(t_tok, t_s0, b.free))
                                t = mm(o, kkv[lo:lo + 64, j, cs], S03[lo:lo + 64, j, :], False, True)
                            b.free = [cp("act", rhs.rearrange("p (j g f) -> p g j f", j=4, g=2)[:, g],
                                         t3(b.ap[:, 0:256], 4), after=t)]
                            t_r.append(b.free)
                        t = t_r
                        b = bank()
                        for h in range(8):
                            g_, k = G[h % 2], slice(h // 2 * 128, h // 2 * 128 + 128)
                            t2 = mm(b.ap[:, h * 64:(h + 1) * 64], g_["XT"][:, k], rhs[:, h * 64:(h + 1) * 64],
                                    after=(t, tx, b.free))
                        b.free = [cp("act", sa, b.ap, after=t2)]
                        t_sa = b.free
                        yield 4.0
                        b, by = bank(), bank()
                        for h in range(8):
                            g_, k, j, lo = G[h % 2], slice(h // 2 * 128, h // 2 * 128 + 128), h // 2, 64 * (h % 2)
                            hs = slice(h * 64, (h + 1) * 64)
                            o = b.ap[lo:lo + 64, j * 64:(j + 1) * 64]
                            mm(o, tok[0][:, hs], sa[:, hs], True, False, after=(t_sa, b.free))
                            t = mm(o, tok[1][:, hs], tok[2][:, hs], False, True)
                        for h in range(8):
                            g_, k, j, lo = G[h % 2], slice(h // 2 * 128, h // 2 * 128 + 128), h // 2, 64 * (h % 2)
                            hs = slice(h * 64, (h + 1) * 64)
                            o = by.ap[lo:lo + 64, j * 128:(j + 1) * 128]
                            mm(o, tok[2][:, hs], g_["rk"][:, k], True, False, after=by.free)
                            mm(o, sa[:, hs], g_["rb"][:, k], False, False)
                            t_y = mm(o, S03[lo:lo + 64, j, :], zr[lo:lo + 64, j, cs], False, True)
                        tt("dve", t3(tmp, 4), t3(b.ap[:, 0:256], 4), bcast(eq(e_out, ch), 2, 64), ALU.mult, after=t)
                        b.free = [P.last("dve")]
                        tt("dve", St3, St3, bcast(eq(e_all, ch), 2, 64), ALU.mult)
                        t_s = tt("dve", St, St, tmp, ALU.add)
                        by.free = [cp("act", yrw[:, :, cs], t3(by.ap, 4), after=t_y)]
                        done = [t_y, t_s, by.free]
                        yield 4.0
                    P.barrier()
                    ar.at = keep_at
                    w = [ar.take(S) for _ in range(8)]
                    s, tl = load(I["g_up"])
                    for j in range(4):
                        y_, (d_, q_, r_, p_) = yrw[:, j, :], w[4 * (j % 2):4 * (j % 2) + 4]
                        P.fence["dve"] = P.fence["act"] = P.fence["pool"] = P.barrier() if j > 1 else []
                        b = bank()
                        t = mm(b.ap, c("ones64"), y_, after=b.free)
                        t = stt(d_, b.ap, -1.0 / 64, y_, ALU.mult, ALU.add, after=t)
                        b.free = [t]
                        t = act(q_, d_, ACT.Square, after=t)
                        b = bank()
                        t = mm(b.ap, c("ones64"), q_, after=(t, b.free))
                        t = act(r_, b.ap, ACT.Sqrt, scale=1.0 / 64, bias=gneps, after=t)
                        b.free = [t]
                        P.op("dve", lambda g, r_=r_: g.reciprocal(r_, r_), t)
                        tt("dve", d_, d_, r_, ALU.mult)
                        ts("dve", d_, d_, v("gnw", j), v("gnb", j), ALU.mult, ALU.add)
                        t = stt(p_, zr[:, j, :], v("rk", j), zk[:, j, :], ALU.mult, ALU.mult)
                        b = bank()
                        t = mm(b.ap, c("ones64"), p_, after=(t, b.free))
                        t = tt("dve", p_, b.ap, zv[:, j, :], ALU.mult, after=t)
                        b.free = [t]
                        tt("dve", d_, d_, p_, ALU.add)
                        b = bank()
                        t = mm(b.ap, s.ap[:, j * 128:(j + 1) * 128], sgd, after=(tl, b.free))
                        t = tt("dve", y_, d_, b.ap, ALU.mult, after=t)
                        b.free = [t]
                        yield 8.0
                    s.free = [P.last("pe")]
                    P.barrier()

                def beside():
                    tables(I["pos2"], c("invf32"), cos32, sin32, Arena(ar.hi - 4 * S, ar.hi))
                    P.barrier()
                    yield 5.0
                    keep = [A[:, ar.hi - (i + 1) * S:ar.hi - i * S] for i in range(2)]
                    sent = [None, None]

                    def ev(j, f):
                        def g(m, ps, t):
                            ta = act(keep[m], ps, f, after=(t, sent[m]))
                            sent[m] = P.dma("sp", kept[2 * j + m], keep[m], f"k{m}", after=ta)
                            return ta
                        return g

                    for j in range(3):
                        yield from lin_steps([W2[7 + j, 0]], h_of, 256, 8, ev(j, ACT.Copy), cost=FC)
                    for j in range(8):
                        yield from lin_steps([W2[10 + j, 0]], h_of, 256, 8, ev(3 + j, ACT.Sigmoid), cost=FC)
                    P.flush()
                    stored.extend(sent)

                FC = 3.9
                stored = []
                P.streams(rwkv(), beside())
            if stop == "rwkv":
                pass
            elif stop != "b1":
                ar.at = rw_at
                ymla = t3(ar.take(4 * S), 4)
                mrg_at = ar.at
                qd, kvd, kr = t3(ar.take(3 * S), 3), t3(ar.take(2 * S), 2), ar.take(S)
                scratch, rs = ar.take(2 * S), ar.take(S)
                lat = [qd[:, 0, :], qd[:, 1, :], qd[:, 2, :], kvd[:, 0, :], kvd[:, 1, :], kr]
                ended = P.barrier()
                for i in range(6):
                    t_l = P.dma("sp", lat[i], kept[i], "kl", after=(stored, ended))
                gb = A[:, ar.hi - 16 * S:ar.hi].rearrange("p (a b) -> p a b", a=16)
                for i in range(16):
                    t_gb = P.dma("act" if i % 2 else "sp", gb[:, i, :], kept[6 + i], "kg", after=(stored, ended))
                t_q = rms(qd, qd, 3, 384, "gqa", scratch, rs, after=t_l)
                P.barrier()
                t_kv = rms(kvd, kvd, 2, 256, "gkva", scratch, rs)
                P.barrier()
                qn, qr, kn, vt = t3(ar.take(4 * S), 4), t3(ar.take(2 * S), 2), t3(ar.take(4 * S), 4), t3(ar.take(4 * S), 4)
                lin_q = lambda kt: qd[:, kt, :]
                lin32([I["qn_up"]], lin_q, 512, 3, lambda m, ps, t: cp("act", qn[:, m, :], ps, after=t))
                lin32([I["qr_up"]], lin_q, 256, 3, lambda m, ps, t: cp("dve", qr[:, m, :], ps, after=t))
                s, tl = load(I["kv_up"])
                for m in range(4):
                    b = bank()
                    for kt in range(2):
                        t = mm(b.ap, s.ap[:, kt * 1024 + m * 128:kt * 1024 + (m + 1) * 128], kvd[:, kt, :], kt == 0,
                               kt == 1, after=(tl, b.free))
                    b.free = [cp("act", kn[:, m, :], b.ap, after=t)]
                t, _ = lin_tok(s, tl, 512, 512, 2, 1024, lambda kt: kvd[:, kt, :], vt, "dve")
                s.free = [t]
                rt = ar.take(S)
                for src in (qr[:, 0, :], qr[:, 1, :], kr):
                    b = bank()
                    t = mm(b.ap, c("rot32"), src, after=(b.free, P.last("dve")))
                    t2 = tt("dve", rt, b.ap, sin32, ALU.mult, after=t)
                    b.free = [t2]
                    tt("dve", src, src, cos32, ALU.mult)
                    tt("dve", src, src, rt, ALU.add)
                P.barrier()

                def scores(h, o, qt, kl, after):
                    hp, lo, ro = h // 2, 64 * (h % 2), 32 * (h % 4)
                    mm(o, qn[lo:lo + 64, hp, qt * 128:(qt + 1) * 128], kn[lo:lo + 64, hp, 0:kl], True, False, after)
                    return mm(o, qr[ro:ro + 32, h // 4, qt * 128:(qt + 1) * 128], kr[ro:ro + 32, 0:kl], False, True)

                def mask(ps, Sb, m, qt, kl, after):
                    tm = c("causal")[:, (3 - qt) * 128:512]
                    return P.op("dve", lambda g: g.tensor_tensor_reduce(
                        Sb, ps[:, 0:kl], tm, float(-1.0 / np.sqrt(96.0)), 3.0e38, ALU.add, ALU.min, m), after)

                for _ in attention(ar, 8, scores, mask, lambda qt: 128 * (qt + 1),
                                   lambda h, k: vt[:, k, h * 64:(h + 1) * 64],
                                   lambda hp, ps, t: cp("act", ymla[:, hp, :], ps, after=t),
                                   (scratch[:, 0:S], scratch[:, S:2 * S], rs, rt), [qd[:, i, :] for i in range(3)]):
                    pass
                P.barrier()
            if stop in ("rwkv", "mla", "b1"):
                pass
            else:
                ar.at = mrg_at
                tb = [ar.take(S) for _ in range(4)]
                tb2 = [ar.take(S) for _ in range(2)]
                def ev_rw(m, ps, t):
                    return tt("dve", tb[m], ps, gb[:, 4 * j + m, :], ALU.mult, after=(t, t_gb))

                def ev_mla(m, ps, t):
                    r_ = tt("dve", tb2[m % 2], ps, gb[:, 8 + 4 * j + m, :], ALU.mult, after=t)
                    t = tt("dve", tb[m], tb[m], tb2[m % 2], ALU.add)
                    split(HHt[:, 4 * j + m, :], HLt[:, 4 * j + m, :], tb[m], t)
                    return r_

                for j in range(2):
                    lin32([I["wb"][0, j]], lambda kt: yrw[:, kt, :], 512, 4, ev_rw)
                    lin32([I["wb"][1, j]], lambda kt: ymla[:, kt, :], 512, 4, ev_mla)
                t_m = P.last("dve")
                sq2 = ar.take(2 * S)

                for j in range(4):
                    lin([I["w_out2"][j, 0]], h_of, 256, 8, residual(j, sq2), after=t_m)
                P.barrier()
                norm_ahead(sq2)
            if stop in ("rwkv", "mla", "b1", "mid"):
                pass
            else:
                phase("moe", 26240, extra=4, products=False)
                ar = Arena(0, 26240)
                moe_at = ar.at
                Hb = ar.take(8 * S)
                Ht = t3(Hb, 8)
                for i in range(8):
                    t_h = stt(Ht[:, i, :], Xt[:, i, :], v("ffg", i), RS, ALU.mult, ALU.mult)
                h_of = lambda kt: Ht[:, kt, :]
                lg, bb = ar.take(144), ar.take(36)
                lg3 = t3(lg, 4)
                t_bb = P.dma("act", bb, I["br"].partition_broadcast(128), "const", after=P.barrier())
                s, tl = load(I["wr"])
                t, _ = lin_tok(s, tl, 0, 36, 8, 36, h_of, lg3, "act", after=t_h)
                s.free = [t]
                tt("dve", lg3, lg3, bcast(bb, 1, 4), ALU.add, after=(P.last("act"), t_bb))
                gl, fl_, pen = t3(ar.take(16), 4), t3(ar.take(128), 4), t3(ar.take(16), 4)
                cand, oh1, oh2, Gt = (t3(ar.take(128), 4) for _ in range(4))
                cg, mx, gm, gs, m1, m2, ee, g1, g2 = (ar.take(16 if i == 0 else 4) for i in range(9))
                cg = t3(cg, 4)
                b4 = lambda x, n: bcast(x, 2, n)

                htok = t3(ar.take(4 * D), 4)
                for k in range(4):
                    for f2 in range(2):
                        b = bank()
                        for f in range(4):
                            t = tr(b.ap[:, f * 128:(f + 1) * 128], Ht[:, f2 * 4 + f, k * 128:(k + 1) * 128],
                                   after=(t_h, b.free))
                        b.free = [cp("act", htok[:, k, f2 * 512:(f2 + 1) * 512], b.ap, after=t)]
                    t_hd = P.dma("sp", hdram[k * 128:(k + 1) * 128, :], htok[:, k, :], "hd", after=b.free)

                def red(o, a, op):
                    return P.op("dve", lambda g: g.tensor_reduce(o, a, AX_X, op))

                def one_hot(dst, src, top, tmp_, n):
                    red(top, src, ALU.max)
                    tt("dve", tmp_, src, b4(top, n), ALU.is_equal)
                    tt("dve", tmp_, tmp_, bcast(c("iota")[:, 0:n], 1, 4), ALU.mult)
                    red(mx, tmp_, ALU.max)
                    return tt("dve", dst, tmp_, b4(mx, n), ALU.is_equal)

                cp("dve", gl, lg3[:, :, 0:4])
                cp("dve", fl_, lg3[:, :, 4:36])
                one_hot(pen, gl, gm, cg, 4)
                t = tt("dve", gl, gl, b4(gm, 4), ALU.subtract)
                t = act(gl, gl, ACT.Exp, after=t)
                P.fence["dve"] = [t]
                red(gs, gl, ALU.add)
                P.op("dve", lambda g: g.reciprocal(gs, gs))
                ts("dve", pen, pen, -1.0, BIG, ALU.add, ALU.mult)
                f16 = fl_.rearrange("p a (g e) -> p (a g) e", e=8)
                tt("dve", f16, f16, bcast(pen.rearrange("p a g -> p (a g)"), 2, 8), ALU.add)
                one_hot(oh1, fl_, m1, cand, 32)
                stt(fl_, oh1, -BIG, fl_, ALU.mult, ALU.add)
                one_hot(oh2, fl_, m2, cand, 32)
                t = tt("dve", ee, m2, m1, ALU.subtract)
                t = act(ee, ee, ACT.Exp, after=t)
                ts("dve", g1, ee, 1.0, None, ALU.add, after=t)
                P.op("dve", lambda g: g.reciprocal(g1, g1))
                tt("dve", g1, g1, gs, ALU.mult)
                tt("dve", g2, g1, ee, ALU.mult)
                Mk, pm, dst_, tkc = (t3(ar.take(128), 4) for _ in range(4))
                tab = ar.take(4 * 96).rearrange("p (k e r) -> p k e r", k=4, r=3)
                cnt = ar.take(32)
                t_mk = tt("dve", Mk, oh1, oh2, ALU.add)
                tt("dve", dst_, oh2, bcast(c("tok2"), 2, 32), ALU.add)
                tt("dve", Gt, oh1, b4(g1, 32), ALU.mult)
                tt("dve", oh2, oh2, b4(g2, 32), ALU.mult)
                tt("dve", Gt, Gt, oh2, ALU.add)
                cp("dve", tab[:, :, :, 0], bcast(c("tok"), 2, 32))
                cp("dve", tab[:, :, :, 1], dst_)
                t_tab = cp("dve", tab[:, :, :, 2], Gt)
                b = bank()
                for k in range(4):
                    for k2_ in range(k + 1):
                        t = mm(b.ap[:, k * 32:(k + 1) * 32], c("ones") if k2_ < k else c("strict"), Mk[:, k2_, :],
                               k2_ == 0, k2_ == k, after=(t_mk, b.free))
                for k in range(4):
                    t = mm(b.ap[:, 128:160], c("ones"), Mk[:, k, :], k == 0, k == 3)
                stt(pm, t3(b.ap[:, 0:128], 4), 1.0, Mk, ALU.add, ALU.mult, after=t)
                ts("dve", pm, pm, -1.0, None, ALU.add)
                b.free = [cp("dve", cnt, b.ap[:, 128:160])]
                ne, uc, ux, tw = (ar.take(32) for _ in range(4))
                flag = small[:, 250:251].bitcast(U32)
                ts("dve", ne, cnt, 128.5, None, ALU.is_gt)
                for lim in (256.5, 384.5):
                    ts("dve", tw, cnt, lim, None, ALU.is_gt)
                    tt("dve", ne, ne, tw, ALU.add)
                P.op("dve", lambda g: g.tensor_tensor_scan(uc, c("ones")[:, 0:32], ne, 0.0, ALU.mult, ALU.add))
                tt("dve", ux, uc, ne, ALU.subtract)
                t_flag = cp("dve", flag, uc[:, 31:32])

                Pm = [ar.take(S) for _ in range(2)]
                idx = ar.take(32).bitcast(U32)
                dix = ar.take(32).bitcast(U32)
                gsl = ar.take(32)
                b = bank()
                tp = [[], []]
                for e_ in range(32):
                    t = tt("dve", t3(Pm[e_ % 2], 4), bcast(c("io128"), 1, 4), bcast(pm[:, :, e_], 2, 128),
                           ALU.is_equal, after=tp[e_ % 2])
                    for k in range(4):
                        t2 = mm(b.ap[:, e_ * 3:e_ * 3 + 3], Pm[e_ % 2][:, k * 128:(k + 1) * 128], tab[:, k, e_, :],
                                k == 0, k == 3, after=(t, t_tab, b.free))
                    tp[e_ % 2] = [t2]
                bv = b.ap[:, 0:96].rearrange("p (e r) -> p e r", r=3)
                t_idx = cp("dve", idx, bv[:, :, 0], after=t2)
                t_dix = ts("dve", dix, bv[:, :, 1], 4096.0, None, ALU.add)
                t_gsl = cp("dve", gsl, bv[:, :, 2])
                b.free = [t_gsl]

                NB = 3
                Xg = [ar.take(D) for _ in range(NB)]
                XT = [t3(ar.take(D), 8) for _ in range(2)]
                sgm = [ar.take(256) for _ in range(2)]
                hu = [ar.take(256) for _ in range(2)]
                hT = [ar.take(256) for _ in range(2)]
                Yb = [ar.take(D) for _ in range(NB)]

                def gather(Pq, o, tab_, ix, sem, after):
                    return Pq.swdge(lambda g: g.indirect_dma_start(
                        o, None, tab_, bass.IndirectOffsetOnAxis(ix, 0), bounds_check=tab_.shape[0] - 1,
                        oob_is_err=False), sem, after)

                def scatter(Pq, y, ix, sem, after):
                    return Pq.swdge(lambda g: g.indirect_dma_start(
                        ydram, bass.IndirectOffsetOnAxis(ix, 0), y, None, bounds_check=2 * S - 1,
                        oob_is_err=False), sem, after)

                st = {"g": {}, "B": {}, "C": {}, "D": {}, "E": {}, "S": {}}

                def st_gather(e_):
                    st["g"][e_] = gather(P, Xg[e_ % NB], hdram, idx[:, e_:e_ + 1], f"g{e_ % NB}",
                                         (t_hd, t_idx, st["B"].get(e_ - NB, [None])[0]))

                def st_turn(e_):
                    for f2 in range(2):
                        b = bank()
                        for f in range(4):
                            t = tr(b.ap[:, f * 128:(f + 1) * 128], Xg[e_ % NB][:, (f2 * 4 + f) * 128:(f2 * 4 + f + 1) * 128],
                                   after=(st["g"][e_], b.free))
                        b.free = [cp("dve" if f2 else "act", XT[e_ % 2][:, f2 * 4:f2 * 4 + 4, :], t3(b.ap, 4),
                                     after=(t, st["C"].get(e_ - 2, [None])[0]))]
                        if f2 == 0:
                            first = b.free
                    st["B"][e_] = [t, first, b.free]

                def st_up(e_):
                    b = bank()
                    for j in range(2):
                        s, tl = load(I["w_gu"][e_, j])
                        for kt in range(4):
                            t = mm(b.ap, XT[e_ % 2][:, j * 4 + kt, :], s.ap[:, kt * 512:(kt + 1) * 512],
                                   j + kt == 0, j == 1 and kt == 3, after=(tl, st["B"][e_], b.free))
                        s.free = [t]
                    ta = act(sgm[e_ % 2], b.ap[:, 0:256], ACT.Sigmoid, after=(t, st["C"].get(e_ - 2)))
                    tt("dve", hu[e_ % 2], b.ap[:, 0:256], sgm[e_ % 2], ALU.mult, after=(ta, st["D"].get(e_ - 2)))
                    t2 = tt("dve", hu[e_ % 2], hu[e_ % 2], b.ap[:, 256:512], ALU.mult)
                    b.free = [t2]
                    st["C"][e_] = [t, t2]

                def st_mid(e_):
                    b = bank()
                    for k in range(2):
                        t = tr(b.ap[:, k * 128:(k + 1) * 128], hu[e_ % 2][:, k * 128:(k + 1) * 128],
                               after=(st["C"][e_], b.free))
                    t2 = cp("act", hT[e_ % 2], b.ap[:, 0:256], after=(t, st["E"].get(e_ - 2)))
                    b.free = [t2]
                    st["D"][e_] = [t, t2]

                def st_down(e_):
                    s, tl = load(I["w_dn"][e_])
                    for n in range(2):
                        b = bank()
                        for kt in range(2):
                            t = mm(b.ap, hT[e_ % 2][:, kt * 128:(kt + 1) * 128],
                                   s.ap[:, kt * 1024 + n * 512:kt * 1024 + (n + 1) * 512], kt == 0, kt == 1,
                                   after=(tl, st["D"][e_], b.free))
                        o = Yb[e_ % NB][:, n * 512:(n + 1) * 512]
                        w_ = (t, t_gsl, st["S"].get(e_ - NB))
                        if n:
                            t2 = ts("dve", o, b.ap, gsl[:, e_:e_ + 1], None, ALU.mult, after=w_)
                        else:
                            t2 = act(o, b.ap, ACT.Copy, scale=gsl[:, e_:e_ + 1], after=w_)
                            t1 = t2
                        b.free = [t2]
                    s.free = [t]
                    st["E"][e_] = [t]
                    st["S"][e_] = scatter(P, Yb[e_ % NB], dix[:, e_:e_ + 1], f"y{e_ % NB}", (t1, t2, t_dix))

                st_gather(0)
                st_gather(1)
                st_turn(0)
                for e_ in range(32):
                    st_up(e_)
                    if e_ < 31:
                        st_turn(e_ + 1)
                    if e_ < 30:
                        st_gather(e_ + 2)
                    if e_:
                        st_down(e_ - 1)
                    st_mid(e_)
                st_down(31)

                P2 = Prog(["pe2", "act2", "dve2", "pool2"])
                P2.serial = True
                sel, posj, gj, rj = ar.take(32), ar.take(4), ar.take(4), ar.take(4)
                offs, eps_ = ar.take(1), ar.take(1)
                tj = t3(ar.take(128), 4)
                tabj = ar.take(12).rearrange("p (k r) -> p k r", k=4)
                wix = ar.take(3).bitcast(U32)
                ixj = ar.take(2).bitcast(U32)
                wgu_rows = I["w_gu"].rearrange("e j p n -> (e j p) n")
                wdn_rows = I["w_dn"].rearrange("e p n -> (e p) n")
                q2 = lambda e, fn: P2.op(e + "2", fn)
                dv = lambda name, *a: q2("dve", lambda g: {"tt": g.tensor_tensor, "ts": g.tensor_scalar,
                                                           "cp": g.tensor_copy, "red": g.tensor_reduce}[name](*a))
                for j in range(7):
                    dv("ts", sel, ux, float(j) + 0.5, None, ALU.is_lt)
                    dv("ts", tw, uc, float(j) + 0.5, None, ALU.is_gt)
                    dv("tt", sel, sel, tw, ALU.mult)
                    dv("tt", tw, sel, ux, ALU.mult)
                    dv("red", offs, tw, AX_X, ALU.add)
                    dv("ts", offs, offs, 128.0, -128.0 * (1 + j), ALU.mult, ALU.add)
                    dv("tt", tw, sel, c("iota"), ALU.mult)
                    dv("red", eps_, tw, AX_X, ALU.add)
                    dv("ts", eps_, eps_, -1.0, 32.0, ALU.mult, ALU.add)
                    dv("ts", eps_, eps_, 31.0, None, ALU.min)
                    for i, (m_, a_) in enumerate(((256.0, 0.0), (256.0, 128.0), (128.0, 0.0))):
                        dv("ts", tw[:, 0:1], eps_, m_, a_, ALU.mult, ALU.add)
                        dv("tt", wix[:, i:i + 1], tw[:, 0:1], c("tok")[:, 0:1], ALU.add)
                    for o_, src in ((posj, pm), (gj, Gt), (rj, dst_)):
                        dv("tt", tj, src, bcast(sel, 1, 4), ALU.mult)
                        dv("red", o_, tj, AX_X, ALU.add)
                    dv("ts", posj, posj, offs, None, ALU.add)
                    dv("cp", tabj[:, :, 0], c("tok"))
                    dv("cp", tabj[:, :, 1], rj)
                    dv("cp", tabj[:, :, 2], gj)
                    dv("tt", t3(Pm[0], 4), bcast(c("io128"), 1, 4), bcast(posj, 2, 128), ALU.is_equal)
                    ps = psum
                    for k in range(4):
                        q2("pe", lambda e, k=k: e.matmul(ps[:, 0, 0:3], Pm[0][:, k * 128:(k + 1) * 128], tabj[:, k, :],
                                                         start=k == 0, stop=k == 3))
                    dv("cp", ixj[:, 0:1], ps[:, 0, 0:1])
                    dv("ts", ixj[:, 1:2], ps[:, 0, 1:2], 4096.0, None, ALU.add)
                    dv("cp", gsl[:, 0:1], ps[:, 0, 2:3])
                    gather(P2, Xg[0], hdram, ixj[:, 0:1], "o", None)
                    for i, rows in enumerate((wgu_rows, wgu_rows, wdn_rows)):
                        gather(P2, slots[i].ap, rows, wix[:, i:i + 1], "o", None)
                    for f in range(8):
                        q2("pe", lambda e, f=f: e.matmul(ps[:, f // 4, f % 4 * 128:f % 4 * 128 + 128],
                                                         Xg[0][:, f * 128:(f + 1) * 128], c("ident"), start=True,
                                                         stop=True, is_transpose=True))
                    for f2 in range(2):
                        dv("cp", XT[0][:, f2 * 4:f2 * 4 + 4, :], t3(ps[:, f2, :], 4))
                    for kt in range(8):
                        q2("pe", lambda e, kt=kt: e.matmul(ps[:, 2, :], XT[0][:, kt, :],
                                                           slots[kt // 4].ap[:, kt % 4 * 512:kt % 4 * 512 + 512],
                                                           start=kt == 0, stop=kt == 7))
                    q2("act", lambda e: e.activation(sgm[0], ps[:, 2, 0:256], ACT.Sigmoid))
                    dv("tt", hu[0], ps[:, 2, 0:256], sgm[0], ALU.mult)
                    dv("tt", hu[0], hu[0], ps[:, 2, 256:512], ALU.mult)
                    for k in range(2):
                        q2("pe", lambda e, k=k: e.matmul(ps[:, 3, k * 128:(k + 1) * 128], hu[0][:, k * 128:(k + 1) * 128],
                                                         c("ident"), start=True, stop=True, is_transpose=True))
                    dv("cp", hT[0], ps[:, 3, 0:256])
                    for n in range(2):
                        for kt in range(2):
                            q2("pe", lambda e, n=n, kt=kt: e.matmul(
                                ps[:, 4 + n, :], hT[0][:, kt * 128:(kt + 1) * 128],
                                slots[2].ap[:, kt * 1024 + n * 512:kt * 1024 + (n + 1) * 512], start=kt == 0,
                                stop=kt == 1))
                    for n in range(2):
                        dv("ts", Yb[0][:, n * 512:(n + 1) * 512], ps[:, 4 + n, :], gsl[:, 0:1], None, ALU.mult)
                    scatter(P2, Yb[0], ixj[:, 1:2], "o", None)
                waits_y = [st["S"][31], st["S"][30], st["S"][29]]
                P.section(P2, flag[0:1, 0:1], list(P.barrier()) + waits_y)

                ar.at = moe_at
                P.barrier()
                Y2 = [ar.take(2 * D) for _ in range(4)]
                for k in range(4):
                    ty = P.dma("sp", Y2[k], ydram[k * 256:(k + 1) * 256, :].rearrange("(p r) n -> p (r n)", r=2), f"Y{k}",
                               after=(P.fence_all(), waits_y))
                    t = tt("dve", Y2[k][:, 0:D], Y2[k][:, 0:D], Y2[k][:, D:2 * D], ALU.add, after=ty)
                    for f2 in range(2):
                        b = bank()
                        for f in range(4):
                            t2 = tr(b.ap[:, f * 128:(f + 1) * 128], Y2[k][:, (f2 * 4 + f) * 128:(f2 * 4 + f + 1) * 128],
                                    after=(t, b.free))
                        xo = Xt[:, f2 * 4:f2 * 4 + 4, k * 128:(k + 1) * 128]
                        b.free = [tt("dve", xo, xo, t3(b.ap, 4), ALU.add, after=t2)]
                P.barrier()
                stats(Xt, 8, D, ar.take(2 * S), RS)
                for i in range(8):
                    ready.append(stt(Xt[:, i, :], Xt[:, i, :], v("fing", i), RS, ALU.mult, ALU.mult))
        t_end = P.barrier()
        P.fence = {}
        for kt in range(8):
            t = P.dma("sp", out[kt * 128:(kt + 1) * 128, :], Xt[:, kt, :], "out", after=ready[kt] if ready else t_end)
        total = t
        P.q["sp"].append((lambda e: None, [total], None))
        P.settle()
        finish(nc, ctx, P, sem_of)
    return nc


def finish(nc, ctx, P, sem_of):
    block = ctx.enter_context(nc.Block())
    end = P.q["sp"].pop()
    end[1][0].used = True

    @block.sync
    def _(eng):
        P.run("sp", eng, sem_of)
        eng.wait_ge(sem_of("out"), end[1][0].value)

    @block.scalar
    def _(eng):
        P.run("act", eng, sem_of)

    @block.gpsimd
    def _(eng):
        P.run("pool", eng, sem_of)

    @block.vector
    def _(eng):
        P.run("dve", eng, sem_of)

    @block.tensor
    def _(eng):
        P.run("pe", eng, sem_of)


def constants():
    f = np.float32
    C = np.zeros((128, NC32), f)

    def put(name, x):
        o, w = CO[name]
        C[:, o:o + w] = x

    i = np.arange(128)
    put("ident", np.eye(128))
    put("ones", 1.0)
    put("ones64", (i[:, None] // 64 == i[None] // 64))
    for name, w in (("rot64", 64), ("rot32", 32)):
        R = np.zeros((128, 128))
        for m in range(128):
            g, r = m // w * w, m % w
            if r < w // 2:
                R[g + r + w // 2, m] = -1.0
            else:
                R[g + r - w // 2, m] = 1.0
        put(name, R)
    d = np.arange(64)
    ang = 2 * np.pi * np.outer(d, d) / 64
    sc = 1.0 / np.sqrt(512.0 * 64.0)
    put("cd", np.kron(np.eye(2), np.cos(ang) * sc))
    put("sd", np.kron(np.eye(2), -np.sin(ang) * sc))
    delta = np.abs(i[:, None] + 384 - np.arange(896)[None])
    count = (delta <= 64) * 1.0 + ((delta <= 256) & (delta % 4 == 0)) + (delta % 16 == 0)
    put("tmask", np.where(count > 0, 8.0 * np.log(np.maximum(count, 1)), -BIG))
    put("causal", np.where(np.arange(512)[None] - 384 <= i[:, None], 0.0, -BIG))
    put("strict", i[:, None] < i[None])
    put("incl", i[:, None] <= i[None])
    iv = (f(10000.0) ** (-np.arange(0, 64, 2, dtype=f) / f(64))).astype(f)
    put("invf64", np.tile(iv, 4)[:, None])
    iv = (f(10000.0) ** (-np.arange(0, 32, 2, dtype=f) / f(32))).astype(f)
    put("invf32", np.tile(iv, 8)[:, None])
    put("iota", 32.0 - np.arange(32)[None])
    put("io128", i[None])
    put("tok", i[:, None] + 128 * np.arange(4)[None])
    put("tok2", 2 * (i[:, None] + 128 * np.arange(4)[None]) - 4096)
    M = np.zeros((128, 14, 128), f)
    for l in range(7):
        same = (i[:, None] >> (l + 1)) == (i[None] >> (l + 1))
        m = same & ((i[:, None] >> l) % 2 == 0) & ((i[None] >> l) % 2 == 1)
        M[:, l] = m
        M[:, 7 + l] = m.T
    p = np.arange(512)
    a = 2 * np.pi * (np.outer(p, p) % 512) / 512
    dft = np.stack([np.cos(a), np.sin(a)]).astype(f).reshape(2, 4, 128, 512).transpose(0, 2, 1, 3)
    return {"c32": C, "m32": M.reshape(128, -1), "dft": np.ascontiguousarray(dft.reshape(2, 128, 2048))}


def lay(w, kt, nc_):
    K, N = w.shape
    return np.ascontiguousarray(
        w.reshape(K // (128 * kt), kt, 128, N // nc_, nc_).transpose(3, 0, 2, 1, 4).reshape(
            N // nc_, K // (128 * kt), 128, kt * nc_))


def cols(x):
    return np.ascontiguousarray(x.reshape(-1, 128).T)


def layout(inp):
    g = {k: np.asarray(x) for k, x in inp.items()}
    a = constants()
    a["x"] = np.ascontiguousarray(g["x"][0].T.reshape(8, 128, 512))
    a["pos1"] = np.ascontiguousarray(g["positions"][0])
    a["w_in"] = np.stack([lay(g["w_in"][i], 8, 256) for i in range(2)])
    a["w_out"] = np.stack([lay(g["w_out"][i], 8, 256) for i in range(2)])
    a["w_up"] = np.stack([lay(g["w_up"][i], 8, 256) for i in range(2)])
    a["w_down"] = np.stack([lay(g["w_down"][i], 8, 256) for i in range(2)])
    q = {k[:-2]: x[0] for k, x in g.items() if k.endswith("_2")}
    a["pos2"] = np.ascontiguousarray(g["positions_2"][0])
    w = q["w_in"]
    a["w_in2"] = lay(np.concatenate([w[:, :2432]] + [w[:, 2432:2464]] * 4 + [w[:, 2464:]], 1), 8, 256)
    a["wa_up"] = np.concatenate([q["rw_w_up"], q["rw_a_up"]], 0)
    a["g_up"] = np.ascontiguousarray(q["rw_g_up"])
    wq = q["mla_w_q_up"].reshape(384, 8, 96)
    a["qn_up"] = lay(wq[:, :, :64].reshape(384, 512), 3, 512)[0, 0]
    a["qr_up"] = lay(wq[:, :, 64:].reshape(384, 256), 3, 256)[0, 0]
    wk = q["mla_w_kv_up"].reshape(256, 8, 128)
    a["kv_up"] = lay(np.concatenate([wk[:, :, :64].reshape(256, 512), wk[:, :, 64:].reshape(256, 512)], 1), 2, 1024)[0, 0]
    a["wb"] = np.stack([lay(q["w_branch_rw"], 4, 512)[:, 0], lay(q["w_branch_mla"], 4, 512)[:, 0]])
    a["w_out2"] = lay(q["w_out"], 8, 256)
    a["wr"] = lay(np.concatenate([q["moe_w_group"], q["moe_w_router"]], 1), 8, 36)[0, 0]
    a["br"] = np.concatenate([q["moe_b_group"], q["moe_b_router"]])
    w = q["moe_w_gu"].reshape(32, 2, 4, 128, 512).transpose(0, 1, 3, 2, 4)
    a["w_gu"] = np.ascontiguousarray(w).reshape(32, 2, 128, 2048)
    a["w_dn"] = np.ascontiguousarray(q["moe_w_down"].reshape(32, 2, 128, 1024).transpose(0, 2, 1, 3)).reshape(32, 128, 2048)
    vec = {"an0": g["attn_norm_w"][0], "an1": g["attn_norm_w"][1], "mn0": g["mlp_norm_w"][0],
           "mn1": g["mlp_norm_w"][1], "fn1": g["final_norm_w"], "lb": g["hgrn_lower_bounds"],
           "mixg": g["mix_norm_g_2"], "mu": g["rw_mu_2"], "w0": g["rw_w0_2"], "a0": g["rw_a0_2"],
           "kk": g["rw_k_k_2"], "ka": g["rw_k_a_2"], "rk": g["rw_r_k_2"], "gnw": g["rw_gn_w_2"],
           "gnb": g["rw_gn_b_2"], "gqa": g["mla_g_qa_2"], "gkva": g["mla_g_kva_2"],
           "ffg": g["ffn_norm_g_2"], "fing": g["final_norm_g_2"]}
    Vv = np.zeros((128, NV), np.float32)
    for k, x in vec.items():
        o, w = VO[k]
        Vv[:, o:o + w] = cols(x)
    a["vecs"] = Vv
    return a


def kernel(**inputs):
    import concourse.bacc as _bacc
    from concourse.bass_utils import run_bass_kernel_spmd as _run

    nc = _bacc.Bacc("TRN2", target_bir_lowering=False, num_devices=1)
    arrays = layout(inputs)
    I = {k: nc.dram_tensor("in_" + k, a.shape, mybir.dt.from_np(a.dtype), kind="ExternalInput").ap()
         for k, a in arrays.items()}
    out = nc.dram_tensor("out_0", (D, S), F32, kind="ExternalOutput").ap()
    build(nc, I, out)
    r = _run(nc, [{"in_" + k: a for k, a in arrays.items()}], core_ids=[0])
    return np.ascontiguousarray(r.results[0]["out_0"].T)[None]
```
